# Optimizing a Trainium2 kernel written in Bass

```python
import math
import jax, jax.numpy as jnp
from jax import lax
import numpy as np

D_MODEL = 1024
BATCH = 1
SEQ = 1024
DEPTH = 2

N_META = 16
N_A_LAYERS = DEPTH // 2
N_B_LAYERS = DEPTH - N_A_LAYERS
POOL_WINDOWS = (2, 4, 8, 16)
N_POOL_GROUPS = len(POOL_WINDOWS)
POOL_GROUP_DIM = D_MODEL // N_POOL_GROUPS
HEAD_DIM = 64
N_Q_HEADS = D_MODEL // HEAD_DIM
N_KV_HEADS = max(1, N_Q_HEADS // 8)
GROUP = N_Q_HEADS // N_KV_HEADS
ATTN_DIM = N_Q_HEADS * HEAD_DIM
KV_DIM = N_KV_HEADS * HEAD_DIM
WINDOW = 128
BLOCK = 128
N_BUCKETS = 32
MAX_DISTANCE = 128
D_FF = (((8 * D_MODEL + 2) // 3 + 255) // 256) * 256
EPS = 1e-6
PAD_FRONT = (-N_META) % BLOCK


def rms_norm(x, g):
    xf = x.astype(jnp.float32)
    y = xf * lax.rsqrt(jnp.mean(xf * xf, axis=-1, keepdims=True) + EPS)
    return (y * g.astype(jnp.float32)).astype(x.dtype)

def swiglu(h, w_gate_up, w_down):
    gu = h @ w_gate_up
    gate, up = jnp.split(gu, 2, axis=-1)
    return (jax.nn.silu(gate) * up) @ w_down

def pool_mixer(h, w_groups, scale):
    B, L, _ = h.shape
    hg = h.astype(jnp.float32).reshape(B, L, N_POOL_GROUPS, POOL_GROUP_DIM)
    cs = jnp.cumsum(hg, axis=1)
    pos = jnp.arange(1, L + 1, dtype=jnp.float32)
    outs = []
    for gi, w in enumerate(POOL_WINDOWS):
        c = cs[:, :, gi]
        lag = jnp.pad(c, ((0, 0), (w, 0), (0, 0)))[:, :L]
        cnt = jnp.minimum(pos, float(w))[None, :, None]
        outs.append((c - lag) / cnt - hg[:, :, gi])
    p = jnp.stack(outs, axis=2).astype(h.dtype)
    y = jnp.einsum('blgc,gcd->blgd', p, w_groups).reshape(B, L, D_MODEL)
    return y * scale

def t5_bucket(d):
    max_exact = N_BUCKETS // 2
    df = jnp.maximum(d, 1).astype(jnp.float32)
    large = max_exact + (jnp.log(df / max_exact) / math.log(MAX_DISTANCE / max_exact)
                         * (N_BUCKETS - max_exact)).astype(jnp.int32)
    large = jnp.minimum(large, N_BUCKETS - 1)
    return jnp.where(d < max_exact, d, large)

def band_bias_and_mask(rel_bias, n_blocks):
    q = jnp.arange(BLOCK)[:, None]
    s = jnp.arange(2 * BLOCK)[None, :]
    d = q + BLOCK - s
    in_window = (d >= 0) & (d < WINDOW)
    bias = rel_bias[t5_bucket(jnp.maximum(d, 0))]
    bias = jnp.transpose(bias, (2, 0, 1)).astype(jnp.float32)
    key_pos = jnp.arange(n_blocks)[:, None] * BLOCK + s - BLOCK
    valid = in_window[None] & (key_pos >= PAD_FRONT)[:, None, :]
    return bias, valid

def to_blocks_with_prev(t):
    B, L = t.shape[:2]
    nb = (L + PAD_FRONT) // BLOCK
    t = jnp.pad(t, ((0, 0), (PAD_FRONT + BLOCK, 0), (0, 0), (0, 0)))
    t = t.reshape(B, nb + 1, BLOCK, t.shape[2], t.shape[3])
    return jnp.concatenate([t[:, :-1], t[:, 1:]], axis=2)

def sliding_window_attention(h, k_blk, v_blk, w_q, b_q, w_o, b_o, sinks, bias, valid):
    B, L, _ = h.shape
    q = (h @ w_q + b_q).reshape(B, L, N_KV_HEADS, GROUP, HEAD_DIM)
    q = jnp.pad(q, ((0, 0), (PAD_FRONT, 0), (0, 0), (0, 0), (0, 0)))
    nb = q.shape[1] // BLOCK
    q = q.reshape(B, nb, BLOCK, N_KV_HEADS, GROUP, HEAD_DIM)
    logits = jnp.einsum('bnqhgd,bnshd->bhgnqs', q, k_blk,
                        preferred_element_type=jnp.float32) * (HEAD_DIM ** -0.5)
    logits = logits + bias.reshape(N_KV_HEADS, GROUP, 1, BLOCK, 2 * BLOCK)
    logits = jnp.where(valid, logits, -jnp.inf)
    sink = sinks.astype(jnp.float32).reshape(N_KV_HEADS, GROUP, 1, 1, 1)
    m = jnp.maximum(logits.max(axis=-1, keepdims=True), sink)
    p = jnp.exp(logits - m)
    denom = p.sum(axis=-1, keepdims=True) + jnp.exp(sink - m)
    probs = (p / denom).astype(v_blk.dtype)
    o = jnp.einsum('bhgnqs,bnshd->bnqhgd', probs, v_blk)
    o = o.reshape(B, nb * BLOCK, ATTN_DIM)[:, PAD_FRONT:]
    return o @ w_o + b_o

def first_inputs(seed: int = 0) -> dict:
    key = jax.random.key(seed)
    ks = jax.random.split(key, 24)
    f32 = jnp.float32

    def nrm(k, shape, scale):
        return jax.random.normal(k, shape, f32) * scale

    def gain(k, shape):
        return jnp.ones(shape, f32) + 0.05 * jax.random.normal(k, shape, f32)

    return {
        "x": nrm(ks[0], (BATCH, SEQ, D_MODEL), 1.0),
        "meta_tokens": nrm(ks[1], (N_META, D_MODEL), 1.0),
        "norm_mix_pre": gain(ks[2], (DEPTH, D_MODEL)),
        "norm_mix_post": gain(ks[3], (DEPTH, D_MODEL)),
        "norm_ffn_pre": gain(ks[4], (DEPTH, D_MODEL)),
        "norm_ffn_post": gain(ks[5], (DEPTH, D_MODEL)),
        "pool_w": nrm(ks[6], (N_A_LAYERS, N_POOL_GROUPS, POOL_GROUP_DIM, POOL_GROUP_DIM), POOL_GROUP_DIM ** -0.5),
        "pool_scale": gain(ks[7], (N_A_LAYERS, D_MODEL)) + 0.05 * jax.random.normal(ks[8], (N_A_LAYERS, D_MODEL), f32),
        "kv_norm": gain(ks[9], (D_MODEL,)),
        "w_k": nrm(ks[10], (D_MODEL, KV_DIM), D_MODEL ** -0.5),
        "b_k": nrm(ks[11], (KV_DIM,), 0.02),
        "w_v": nrm(ks[12], (D_MODEL, KV_DIM), D_MODEL ** -0.5),
        "b_v": nrm(ks[13], (KV_DIM,), 0.02),
        "w_q": nrm(ks[14], (N_B_LAYERS, D_MODEL, ATTN_DIM), D_MODEL ** -0.5),
        "b_q": nrm(ks[15], (N_B_LAYERS, ATTN_DIM), 0.02),
        "w_o": nrm(ks[16], (N_B_LAYERS, ATTN_DIM, D_MODEL), ATTN_DIM ** -0.5),
        "b_o": nrm(ks[17], (N_B_LAYERS, D_MODEL), 0.02),
        "sinks": nrm(ks[18], (N_B_LAYERS, N_Q_HEADS), 0.5),
        "rel_bias": nrm(ks[19], (N_BUCKETS, N_Q_HEADS), 0.3),
        "w_gate_up": nrm(ks[20], (DEPTH, D_MODEL, 2 * D_FF), D_MODEL ** -0.5),
        "w_down": nrm(ks[21], (DEPTH, D_FF, D_MODEL), D_FF ** -0.5),
    }

def first_block(x, meta_tokens, norm_mix_pre, norm_mix_post, norm_ffn_pre, norm_ffn_post,
              pool_w, pool_scale, kv_norm, w_k, b_k, w_v, b_v, w_q, b_q, w_o, b_o,
              sinks, rel_bias, w_gate_up, w_down):
    B = x.shape[0]
    meta = jnp.broadcast_to(meta_tokens[None].astype(x.dtype), (B, N_META, D_MODEL))
    hs = jnp.concatenate([meta, x], axis=1)
    L = hs.shape[1]
    n_blocks = (L + PAD_FRONT) // BLOCK
    bias, valid = band_bias_and_mask(rel_bias, n_blocks)
    k_blk = None
    v_blk = None
    for layer in range(DEPTH):
        h = rms_norm(hs, norm_mix_pre[layer])
        if layer < N_A_LAYERS:
            mix = pool_mixer(h, pool_w[layer], pool_scale[layer])
        else:
            j = layer - N_A_LAYERS
            mix = sliding_window_attention(h, k_blk, v_blk, w_q[j], b_q[j], w_o[j], b_o[j],
                                           sinks[j], bias, valid)
        hs = hs + rms_norm(mix, norm_mix_post[layer])
        h = rms_norm(hs, norm_ffn_pre[layer])
        hs = hs + rms_norm(swiglu(h, w_gate_up[layer], w_down[layer]), norm_ffn_post[layer])
        if layer == N_A_LAYERS - 1:
            kv_in = rms_norm(hs, kv_norm)
            k = (kv_in @ w_k + b_k).reshape(B, L, N_KV_HEADS, HEAD_DIM)
            v = (kv_in @ w_v + b_v).reshape(B, L, N_KV_HEADS, HEAD_DIM)
            k_blk = to_blocks_with_prev(k)
            v_blk = to_blocks_with_prev(v)
    return hs[:, N_META:]


DEPTH_2 = 1

D_MIX = D_MODEL
D_A = D_MIX // 2
D_B = D_MIX - D_A
HEAD_A = 64
G_A = D_A // HEAD_A
HEAD_B = 64
H_B = D_B // HEAD_B
CHUNK = 128
DECAY_RANK = 64
ICLR_RANK = 64
LN_EPS = 1e-5
GN_EPS = 64e-5
ALPHA = (2 * DEPTH_2) ** 0.25
BETA = (8 * DEPTH_2) ** -0.25

N_COLS_A = 3 * D_A
N_COLS_B = 4 * D_B + DECAY_RANK + ICLR_RANK
N_COLS = N_COLS_A + N_COLS_B


def _layer_norm(x, g, b, eps):
    xf = x.astype(jnp.float32)
    mu = jnp.mean(xf, axis=-1, keepdims=True)
    var = jnp.mean(jnp.square(xf - mu), axis=-1, keepdims=True)
    y = (xf - mu) * lax.rsqrt(var + eps)
    return (y * g.astype(jnp.float32) + b.astype(jnp.float32)).astype(x.dtype)

def _token_shift(p, mu):
    prev = jnp.pad(p, ((0, 0), (1, 0), (0, 0)))[:, :-1]
    return p + mu * (prev - p)

def _rwkv7_scan(r, w, k, v, a, b):
    Bsz, T, H, N = r.shape
    seq_first = lambda z: jnp.swapaxes(z, 0, 1)
    xs = tuple(seq_first(z) for z in (r, w, k, v, a, b))

    def step(S, inp):
        r_t, w_t, k_t, v_t, a_t, b_t = inp
        sa = jnp.einsum('bhij,bhj->bhi', S, a_t)
        S = S * w_t[:, :, None, :] + sa[..., None] * b_t[:, :, None, :] + v_t[..., None] * k_t[:, :, None, :]
        y = jnp.einsum('bhij,bhj->bhi', S, r_t)
        return S, y

    S0 = jnp.zeros((Bsz, H, N, N), jnp.float32)
    _, ys = lax.scan(step, S0, xs)
    return jnp.swapaxes(ys, 0, 1)

def _gmlp_branch(p_a, ln_v_g, ln_v_b, w_spatial, b_spatial):
    Bsz, T, _ = p_a.shape
    u = jax.nn.gelu(p_a[..., :D_A])
    v = jax.nn.gelu(p_a[..., D_A:2 * D_A])
    gate = p_a[..., 2 * D_A:]
    v = v.reshape(Bsz, T, G_A, HEAD_A)
    v = _layer_norm(v, ln_v_g, ln_v_b, LN_EPS)
    v = v.reshape(Bsz, T // CHUNK, CHUNK, G_A, HEAD_A)
    causal = jnp.tril(jnp.ones((CHUNK, CHUNK), dtype=bool))
    w_m = jnp.where(causal[None], w_spatial, jnp.zeros((), w_spatial.dtype))
    v = jnp.einsum('gts,bcsgd->bctgd', w_m, v) + jnp.swapaxes(b_spatial, 0, 1)[None, None, :, :, None]
    v = v.reshape(Bsz, T, D_A)
    return u * v * jax.nn.silu(gate)

def _rwkv7_branch(p_b, mu_b, w0, w_up, a0, a_up, k_k, k_a, r_k, gn_g, gn_b):
    Bsz, T, _ = p_b.shape
    p_b = _token_shift(p_b, mu_b)
    o = 0
    r = p_b[..., o:o + D_B]; o += D_B
    k = p_b[..., o:o + D_B]; o += D_B
    v = p_b[..., o:o + D_B]; o += D_B
    gate = p_b[..., o:o + D_B]; o += D_B
    wd = p_b[..., o:o + DECAY_RANK]; o += DECAY_RANK
    ad = p_b[..., o:o + ICLR_RANK]

    w_raw = -jax.nn.softplus(-(w0 + jnp.tanh(wd) @ w_up)) - 0.5
    a = jax.nn.sigmoid(a0 + ad @ a_up)

    heads = lambda z: z.reshape(Bsz, T, H_B, HEAD_B).astype(jnp.float32)
    kk = heads(k * k_k)
    kk = kk * lax.rsqrt(jnp.sum(kk * kk, axis=-1, keepdims=True) + 1e-12)
    k = k * (1 + (a - 1) * k_a)
    rh, kh, vh, ah = heads(r), heads(k), heads(v), heads(a)
    decay = jnp.exp(-jnp.exp(heads(w_raw)))

    y = _rwkv7_scan(rh, decay, kh, vh, -kk, kk * ah)
    y = _layer_norm(y, gn_g, gn_b, GN_EPS)
    bonus = jnp.sum(rh * kh * r_k.astype(jnp.float32), axis=-1, keepdims=True) * vh
    y = (y + bonus).reshape(Bsz, T, D_B).astype(p_b.dtype)
    return y * jax.nn.silu(gate)

def second_inputs(seed: int = 0) -> dict:
    key = jax.random.key(seed)
    ks = jax.random.split(key, 24)
    f32 = jnp.float32
    nrm = lambda k, s, sc: jax.random.normal(k, s, f32) * sc
    return {
        "x": nrm(ks[0], (BATCH, SEQ, D_MODEL), 1.0),
        "c": nrm(ks[1], (BATCH, D_MODEL), 1.0),
        "w_ada": nrm(ks[2], (D_MODEL, 3 * D_MODEL), D_MODEL ** -0.5),
        "b_ada": nrm(ks[3], (3 * D_MODEL,), 0.02),
        "w_in": nrm(ks[4], (D_MODEL, N_COLS), D_MODEL ** -0.5),
        "mu_b": jax.random.uniform(ks[5], (N_COLS_B,), f32),
        "ln_v_g": 1.0 + nrm(ks[6], (G_A, HEAD_A), 0.05),
        "ln_v_b": nrm(ks[7], (G_A, HEAD_A), 0.02),
        "w_spatial": nrm(ks[8], (G_A, CHUNK, CHUNK), CHUNK ** -0.5),
        "b_spatial": 1.0 + nrm(ks[9], (G_A, CHUNK), 0.1),
        "w0": jax.random.uniform(ks[10], (D_B,), f32, -4.0, 1.0),
        "w_up": nrm(ks[11], (DECAY_RANK, D_B), 0.5 * DECAY_RANK ** -0.5),
        "a0": nrm(ks[12], (D_B,), 0.5),
        "a_up": nrm(ks[13], (ICLR_RANK, D_B), 0.5 * ICLR_RANK ** -0.5),
        "k_k": 0.85 + nrm(ks[14], (D_B,), 0.05),
        "k_a": 1.0 + nrm(ks[15], (D_B,), 0.05),
        "r_k": nrm(ks[16], (H_B, HEAD_B), 0.1),
        "gn_g": 1.0 + nrm(ks[17], (H_B, HEAD_B), 0.05),
        "gn_b": nrm(ks[18], (H_B, HEAD_B), 0.02),
        "w_out": nrm(ks[19], (D_MIX, D_MODEL), BETA * D_MIX ** -0.5),
        "ln_g": 1.0 + nrm(ks[20], (D_MODEL,), 0.05),
        "ln_b": nrm(ks[21], (D_MODEL,), 0.02),
    }

def second_block(x, c, w_ada, b_ada, w_in, mu_b, ln_v_g, ln_v_b, w_spatial, b_spatial,
              w0, w_up, a0, a_up, k_k, k_a, r_k, gn_g, gn_b, w_out, ln_g, ln_b):
    mod = jax.nn.silu(c) @ w_ada + b_ada
    shift, scale, gate = [m[:, None, :] for m in jnp.split(mod, 3, axis=-1)]
    for _ in range(DEPTH_2):
        h = x * (1 + scale) + shift
        p = h @ w_in
        out_a = _gmlp_branch(p[..., :N_COLS_A], ln_v_g, ln_v_b, w_spatial, b_spatial)
        out_b = _rwkv7_branch(p[..., N_COLS_A:], mu_b, w0, w_up, a0, a_up, k_k, k_a, r_k, gn_g, gn_b)
        o = jnp.concatenate([out_a, out_b], axis=-1) @ w_out
        x = _layer_norm(ALPHA * x + gate * o, ln_g, ln_b, LN_EPS)
    return x


def setup_inputs(seed=0):
    out = dict(first_inputs(seed))
    for name, value in second_inputs(seed + 1).items():
        if name != "x":
            out[name + "_2"] = value
    return out


def reference(
    x, meta_tokens, norm_mix_pre, norm_mix_post, norm_ffn_pre, norm_ffn_post, pool_w,
    pool_scale, kv_norm, w_k, b_k, w_v, b_v, w_q, b_q, w_o, b_o, sinks, rel_bias, w_gate_up,
    w_down, c_2, w_ada_2, b_ada_2, w_in_2, mu_b_2, ln_v_g_2, ln_v_b_2, w_spatial_2, b_spatial_2,
    w0_2, w_up_2, a0_2, a_up_2, k_k_2, k_a_2, r_k_2, gn_g_2, gn_b_2, w_out_2, ln_g_2, ln_b_2,
):
    x = first_block(
        x, meta_tokens, norm_mix_pre, norm_mix_post, norm_ffn_pre, norm_ffn_post, pool_w,
        pool_scale, kv_norm, w_k, b_k, w_v, b_v, w_q, b_q, w_o, b_o, sinks, rel_bias, w_gate_up,
        w_down,
    )
    return second_block(
        x, c_2, w_ada_2, b_ada_2, w_in_2, mu_b_2, ln_v_g_2, ln_v_b_2, w_spatial_2, b_spatial_2,
        w0_2, w_up_2, a0_2, a_up_2, k_k_2, k_a_2, r_k_2, gn_g_2, gn_b_2, w_out_2, ln_g_2,
        ln_b_2,
    )


_drawn_inputs = setup_inputs


def setup_inputs(seed=0):
    import zlib

    import numpy as np

    out = dict(_drawn_inputs(seed))
    spreads = {}
    factors = {'b_k': 24.984,
     'b_q': 3.522,
     'sinks': 8.0,
     'ln_v_g_2': 6.254,
     'ln_v_b_2': 28.554,
     'w_up_2': 4.854,
     'k_k_2': 25.876,
     'gn_g_2': 8.0,
     'gn_b_2': 42.921,
     'ln_b_2': 2.858,
     'b_spatial_2': 3.606}
    for name, (base, spread) in spreads.items():
        noise = np.random.default_rng([zlib.crc32(name.encode()), seed]).standard_normal(out[name].shape)
        drawn = base * np.exp(spread * noise) if base else spread * noise
        out[name] = __import__('jax').numpy.asarray(drawn.astype(out[name].dtype))
    for name, factor in factors.items():
        out[name] = (out[name] * factor).astype(out[name].dtype)
    return out
```

```python
import concourse.bass as bass
from concourse import mybir
from contextlib import ExitStack, contextmanager

f32 = mybir.dt.float32
f32r = mybir.dt.float32r
ALU = mybir.AluOpType
ACT = mybir.ActivationFunctionType

P = 128
D = 1024
KC = D // P
SEQ = 1024
META = 16
NT = SEQ // P
TOK = META + SEQ
FF = 2816
NQ = FF // P
EPS = 1e-6
POOLS = (2, 4, 8, 16)
HEADS = 16
KVH = 2
HD = 64
PAD = P - META
NEG = -1e30

TILES_META = [(0, META)] + [(META + P * i, P) for i in range(NT)]
TILES_SEQ = [(P * i, P) for i in range(NT)]
SLICES_META = [(0, 348), (348, 346), (694, 346)]
SLICES_SEQ = [(0, 512), (512, 512)]

C_ID = 0
C_BAND = C_ID + P
C_PREV = C_BAND + 4 * P
C_MBAND = C_PREV + 4 * META
C_MPREV = C_MBAND + 4 * META
C_HOT = C_MPREV + 4 * META
C_DIST = 3 * P - 1
C_TRIU = C_HOT + C_DIST + 1
C_TRIX = C_TRIU + P
C_BLK = C_TRIX + P
C_CAUS = C_BLK + P
C_LVL = C_CAUS + P
C_IND = C_LVL + 6 * P
C_END = C_IND + 2
CHUNK = 64
DA = 512
GA = DA // HD
COLS_A = 3 * DA
NB = 17


def constants():
    import math
    import numpy as np
    c = np.zeros((P, C_END), np.float32)
    i = np.arange(P)
    s, t = i[:, None], i[None, :]
    c[:, C_ID:C_ID + P] = np.eye(P)
    for g, w in enumerate(POOLS):
        c[:, C_BAND + g * P:C_BAND + (g + 1) * P] = ((t - s >= 0) & (t - s < w)) / w - (s == t)
        prev = ((t + P - s) < w) / w
        c[:, C_PREV + g * META:C_PREV + (g + 1) * META] = prev[:, :META]
        c[:META, C_MPREV + g * META:C_MPREV + (g + 1) * META] = prev[P - META:, :META]
        m = ((t - s >= 0) & (t - s < w)) / np.minimum(t + 1, w).astype(np.float32) - (s == t)
        c[:META, C_MBAND + g * META:C_MBAND + (g + 1) * META] = m[:META, :META]
    for u in range(C_DIST):
        d = 2 * P - 1 - u
        if 0 <= d < P:
            if d < 16:
                b = d
            else:
                b = min(31, 16 + int(np.float32(np.float32(math.log(np.float32(d) / np.float32(16.0))) / np.float32(math.log(8.0))) * np.float32(16)))
            c[b, C_HOT + u] = 1
        else:
            c[32, C_HOT + u] = 1
    same = (s // CHUNK) == (t // CHUNK)
    c[:, C_TRIU:C_TRIU + P] = (s <= t) & same
    c[:, C_TRIX:C_TRIX + P] = (s < t) & same
    c[:, C_BLK:C_BLK + P] = same
    c[:, C_CAUS:C_CAUS + P] = s <= t
    for l in range(6):
        m = 1 << l
        c[:, C_LVL + l * P:C_LVL + (l + 1) * P] = (s // (2 * m) == t // (2 * m)) & (s % (2 * m) < m) & (t % (2 * m) >= m)
    c[:, C_IND:C_IND + 2] = (i[:, None] // HD) == np.arange(2)[None, :]
    return c


def rows_of(vector, n=P):
    return vector.rearrange("(a n) -> a n", a=1).broadcast_to([n, vector.shape[0]])


def lay_out(inputs):
    import numpy as np
    a = {n: np.ascontiguousarray(v) for n, v in inputs.items()}
    for n in ("b_q", "b_k"):
        a[n] = np.ascontiguousarray(a[n].reshape(-1, P).T)
    for n in ("w_gate_up", "w_q"):
        w = a[n]
        w = w.reshape(w.shape[0], KC, P, w.shape[2] // P, P)
        a[n] = np.ascontiguousarray(w.transpose(0, 3, 2, 1, 4))
    for n in ("c_2", "mu_b_2", "a0_2", "k_k_2", "k_a_2", "r_k_2", "gn_g_2", "gn_b_2"):
        a[n] = np.ascontiguousarray(a[n].reshape(-1, P).T)
    a["w_spatial_2"] = np.ascontiguousarray(a["w_spatial_2"].transpose(2, 0, 1))
    a["b_spatial_2"] = np.ascontiguousarray(a["b_spatial_2"].T)
    w = a["w_in_2"]
    a["w_in_2"] = np.ascontiguousarray(w[:, :COLS_A])
    a["w_in_b_2"] = np.ascontiguousarray(w[:, COLS_A:].reshape(KC, P, NB, P).transpose(2, 1, 0, 3))
    a["cst"] = constants()
    return a


class Builder:

    def __init__(self, nc, ctx, ins, out):
        self.nc, self.ctx, self.ins, self.out = nc, ctx, ins, out
        self.eps = self.sb(ctx, "eps", [P, 1])
        self.ident = self.sb(ctx, "identity", [P, P])
        self.scopes = []
        self.Y = self.sb(ctx, "Y", [P, NT + 1, D])
        self.res = [nc.dram_tensor(f"residual{i}", [TOK, D], f32, kind="Internal").ap() for i in range(4)]

    def sb(self, ctx, name, shape, dt=f32, side="left"):
        return ctx.enter_context(self.nc.sbuf_tensor(name, shape, dt, side=side))

    def ps(self, ctx, name, shape, dt=f32):
        return ctx.enter_context(self.nc.psum_tensor(name, shape, dt))

    def sem(self, ctx, name):
        handle = ctx.enter_context(self.nc.semaphore(name))
        self.scopes[-1].append(handle)
        return handle

    @contextmanager
    def stage(self):
        with ExitStack() as ctx:
            self.scopes.append([])
            yield ctx
            used = self.scopes.pop()
            if used:
                with self.nc.Block() as block:
                    @block.gpsimd
                    def _(pool):
                        for handle in used:
                            pool.sem_clear(handle)

    def alloc_x(self, ctx, name, tokens, side="left"):
        self.XH = self.sb(ctx, name + "XH", [P, KC, tokens], f32r, side)
        self.XL = self.sb(ctx, name + "XL", [P, KC, tokens], f32r, side)


def linker(eng, sem):
    n = [0]

    def link(ins):
        n[0] += 1
        ins.then_inc(sem, 1)
        eng.wait_ge(sem, n[0])
    return link


def pool_stage(b):
    nc, ins = b.nc, b.ins
    G = len(POOLS)
    with b.stage() as ctx:
        cst = b.sb(ctx, "pool_constants", [P, C_HOT])
        xin = b.sb(ctx, "xin", [P, 3, D])
        junk = b.sb(ctx, "sq_junk", [P, D])
        xn = b.sb(ctx, "xn", [P, 3, D])
        gpre = b.sb(ctx, "gpre", [P, D])
        scale = b.sb(ctx, "pool_scale_rows", [P, D])
        wraw = b.sb(ctx, "wraw", [P, 2 * G, 256])
        wH = b.sb(ctx, "wH", [P, 2 * G, 256], f32r)
        wL = b.sb(ctx, "wL", [P, 2 * G, 256], f32r)
        pH = b.sb(ctx, "pH", [P, 2, KC, P], f32r)
        pL = b.sb(ctx, "pL", [P, 2, KC, P], f32r)
        ss = b.sb(ctx, "ss", [P, 9]); sd = b.sb(ctx, "sd", [P, 9]); rs = b.sb(ctx, "rs", [P, 9])
        pt = b.ps(ctx, "pt", [P, 2, KC, P])
        mx = b.ps(ctx, "mx", [P, 2, D])
        loaded = [b.sem(ctx, f"pool_x{i}") for i in range(3)]
        s_cst, s_w, s_sc = b.sem(ctx, "pool_cst"), b.sem(ctx, "pool_w_in"), b.sem(ctx, "pool_sc")
        s_wh, s_wl, s_eps = b.sem(ctx, "pool_wh"), b.sem(ctx, "pool_wl"), b.sem(ctx, "pool_eps")
        s_ss, s_sd, s_r, s_xn = (b.sem(ctx, f"pool_{n}") for n in ("ss", "sd", "r", "xn"))
        s_pt, s_ph, s_pl, s_mx, s_y = (b.sem(ctx, f"pool_{n}") for n in ("pt", "ph", "pl", "mx", "y"))
        N = len(TILES_META)

        with nc.Block() as block:
            @block.sync
            def _(sp):
                for t, (_, r) in enumerate(TILES_META):
                    if t >= 3:
                        sp.wait_ge(s_xn, t - 2)
                    src = ins["meta_tokens"] if t == 0 else ins["x"][0, P * (t - 1):P * t, :]
                    sp.dma_start(xin[0:r, t % 3], src).then_inc(loaded[t % 3], 16)
                    if t == 0:
                        sp.dma_start(cst[:, :], ins["cst"][:, 0:C_HOT]).then_inc(s_cst, 16)
                        sp.dma_start(b.ident[:, :], ins["cst"][:, C_ID:C_ID + P]).then_inc(s_cst, 16)
                        sp.dma_start(gpre[:, :], rows_of(ins["norm_mix_pre"][0])).then_inc(s_cst, 16)
                        sp.dma_start(wraw[:, :, :], ins["pool_w"][0].rearrange("g (k p) d -> p (g k) d", p=P)).then_inc(s_w, 16)
                        sp.dma_start(scale[:, :], rows_of(ins["pool_scale"][0])).then_inc(s_sc, 16)

            @block.gpsimd
            def _(pool):
                pool.memset(b.eps[:, :], EPS).then_inc(s_eps, 1)

            @block.scalar
            def _(act):
                act.wait_ge(s_eps, 1)
                for t in range(N + 1):
                    if t < N:
                        r = TILES_META[t][1]
                        act.wait_ge(loaded[t % 3], 16 * (t // 3 + 1))
                        act.activation(junk[0:r], xin[0:r, t % 3], ACT.Square, accum_out=ss[0:r, t:t + 1]).then_inc(s_ss, 1)
                        act.wait_ge(s_ss, t + 1)
                        act.activation(sd[0:r, t:t + 1], ss[0:r, t:t + 1], ACT.Sqrt, bias=b.eps[0:r], scale=1.0 / D).then_inc(s_sd, 1)
                    if t == 0:
                        act.wait_ge(s_w, 16)
                        act.activation(wH[:, :, :], wraw[:, :, :], ACT.Copy).then_inc(s_wh, 1)
                    if t >= 1:
                        k, r = t - 1, TILES_META[t - 1][1]
                        act.wait_ge(s_pt, k + 1)
                        if k >= 2:
                            act.wait_ge(s_mx, k - 1)
                        act.activation(pH[:, k % 2, :, 0:r], pt[:, k % 2, :, 0:r], ACT.Copy).then_inc(s_ph, 1)

            @block.vector
            def _(dve):
                dve.wait_ge(s_cst, 48)
                for t in range(N + 3):
                    if t < N:
                        r = TILES_META[t][1]
                        dve.wait_ge(s_sd, t + 1)
                        dve.reciprocal(rs[0:r, t:t + 1], sd[0:r, t:t + 1]).then_inc(s_r, 1)
                        dve.wait_ge(s_r, t + 1)
                        if t >= 3:
                            dve.wait_ge(s_pt, t - 1)
                        dve.scalar_tensor_tensor(xn[0:r, t % 3], xin[0:r, t % 3], rs[0:r, t:t + 1], gpre[0:r], ALU.mult, ALU.mult).then_inc(s_xn, 1)
                    if t == 0:
                        dve.wait_ge(s_wh, 1)
                        dve.tensor_tensor(wL[:, :, :], wraw[:, :, :], wH[:, :, :].bitcast(f32), ALU.subtract).then_inc(s_wl, 1)
                        dve.wait_ge(s_sc, 16)
                    if 1 <= t <= N:
                        k, r = t - 1, TILES_META[t - 1][1]
                        dve.wait_ge(s_ph, k + 1)
                        dve.tensor_tensor(pL[:, k % 2, :, 0:r], pt[:, k % 2, :, 0:r], pH[:, k % 2, :, 0:r].bitcast(f32), ALU.subtract).then_inc(s_pl, 1)
                    if 2 <= t < N + 2:
                        k, r = t - 2, TILES_META[t - 2][1]
                        dve.wait_ge(s_mx, k + 1)
                        dve.tensor_tensor(b.Y[0:r, k], mx[0:r, k % 2], scale[0:r], ALU.mult).then_inc(s_y, 1)

            @block.tensor
            def _(pe):
                pe.wait_ge(s_cst, 48)
                for t in range(N + 1):
                    if t < N:
                        r = TILES_META[t][1]
                        pe.wait_ge(s_xn, t + 1)
                        if t >= 2:
                            pe.wait_ge(s_pl, t - 1)
                        for f in range(KC):
                            g = f // 2
                            band = cst[0:r, C_BAND + g * P:C_BAND + g * P + r] if t else cst[0:r, C_MBAND + g * META:C_MBAND + (g + 1) * META]
                            last = pe.matmul(pt[:, t % 2, f, 0:r], xn[0:r, t % 3, f * P:(f + 1) * P], band, start=True, stop=True, skip_group_check=True)
                            if t:
                                rp = TILES_META[t - 1][1]
                                c0 = C_PREV if t > 1 else C_MPREV
                                last = pe.matmul(pt[:, t % 2, f, 0:META], xn[0:rp, (t - 1) % 3, f * P:(f + 1) * P],
                                                 cst[0:rp, c0 + g * META:c0 + (g + 1) * META], start=False, stop=True, skip_group_check=True)
                        last.then_inc(s_pt, 1)
                    if t >= 1:
                        k, r = t - 1, TILES_META[t - 1][1]
                        pe.wait_ge(s_pl, k + 1)
                        pe.wait_ge(s_wl, 1)
                        if k >= 2:
                            pe.wait_ge(s_y, k - 1)
                        for g in range(G):
                            for i in range(2):
                                c = 2 * g + i
                                o = mx[0:r, k % 2, 256 * g:256 * (g + 1)]
                                pe.matmul(o, pH[:, k % 2, c, 0:r], wH[:, c], start=(i == 0), stop=False)
                                pe.matmul(o, pL[:, k % 2, c, 0:r], wH[:, c], start=False, stop=False)
                                last = pe.matmul(o, pH[:, k % 2, c, 0:r], wL[:, c], start=False, stop=(i == 1))
                        last.then_inc(s_mx, 1)


def post_stage(b, name, tiles, residual, store, post_gain, pre_gain, kv=None, modulate=None):
    nc, ins = b.nc, b.ins
    N = len(tiles)
    with b.stage() as ctx:
        rx = b.sb(ctx, name + "rx", [P, 3, D])
        junk = b.sb(ctx, name + "junk", [P, D])
        junk2 = junk if modulate else b.sb(ctx, name + "junk2", [P, D])
        xn = b.sb(ctx, name + "xn", [P, 2, D])
        gpost = b.sb(ctx, name + "gpost", [P, D])
        gpre = None if modulate else b.sb(ctx, name + "gpre", [P, D])
        st = b.sb(ctx, name + "st", [P, 6, 9])
        tp = b.ps(ctx, name + "tp", [P, 2, KC, P])
        s = {n: b.sem(ctx, name + n) for n in ("rx0", "rx1", "rx2", "gains", "ss1", "sd1", "r1", "xg", "x", "ss2", "sd2", "r2", "xn", "tp", "xh", "xl", "stored")}
        if kv:
            gkv = b.sb(ctx, name + "gkv", [P, D])
            xk = b.sb(ctx, name + "xk", [P, 2, D])
            kx = b.sb(ctx, name + "kx", [P, 2, KC, P])
            wk = b.sb(ctx, name + "wk", [P, KC, P])
            wv = b.sb(ctx, name + "wv", [P, KC, P])
            bk = b.sb(ctx, name + "bk", [P, 1])
            bv = b.sb(ctx, name + "bv", [P, P])
            tk = b.ps(ctx, name + "tk", [P, KC, P])
            kvp = b.ps(ctx, name + "kvp", [P, 2, 512])
            s.update({n: b.sem(ctx, name + n) for n in ("wkv", "xk", "tk", "kx", "kvp", "k", "v", "kdup", "kdup2", "zero")})

        with nc.Block() as block:
            @block.sync
            def _(sp):
                sp.dma_start(gpost[:, :], rows_of(post_gain)).then_inc(s["gains"], 16)
                if not modulate:
                    sp.dma_start(gpre[:, :], rows_of(pre_gain)).then_inc(s["gains"], 16)
                for t in range(N + 1):
                    if t < N:
                        c, r = tiles[t]
                        if t >= 3:
                            sp.wait_ge(s["x"], t - 2)
                        sp.dma_start(rx[0:r, t % 3], residual(t)).then_inc(s[f"rx{t % 3}"], 16)
                        if kv and t == 0:
                            sp.dma_start(gkv[:, :], rows_of(ins["kv_norm"])).then_inc(s["wkv"], 16)
                            sp.dma_start(wk[:, :, :], ins["w_k"].rearrange("(k p) f -> p k f", p=P)).then_inc(s["wkv"], 16)
                            sp.dma_start(wv[:, :, :], ins["w_v"].rearrange("(k p) f -> p k f", p=P)).then_inc(s["wkv"], 16)
                            sp.dma_start(bk[:, :], ins["b_k"]).then_inc(s["wkv"], 16)
                            sp.dma_start(bv[:, :], rows_of(ins["b_v"])).then_inc(s["wkv"], 16)
                    if t >= 1:
                        c, r = tiles[t - 1]
                        sp.wait_ge(s["x"], t)
                        sp.dma_start(store[c:c + r, :], b.Y[0:r, t - 1]).then_inc(s["stored"], 16)
                if kv:
                    sp.wait_ge(s["kdup2"], 2 * N)
                    sp.dma_start(kv["KT"][HD:P, 0, :], kv["KT"][0:HD, 0, :]).then_inc(s["kdup"], 16)
                    sp.dma_start(kv["KT"][0:HD, 1, :], kv["KT"][HD:P, 1, :]).then_inc(s["kdup"], 16)
                    sp.wait_ge(s["kdup"], 32)
                sp.wait_ge(s["stored"], 16 * N)

            if kv:
                @block.gpsimd
                def _(pool):
                    pool.memset(kx[:, 0, :, 0:PAD], 0.0).then_inc(s["zero"], 1)

            @block.scalar
            def _(act):
                for k in range(N + 6):
                    if k < N:
                        r = tiles[k][1]
                        act.activation(junk[0:r], b.Y[0:r, k], ACT.Square, accum_out=st[0:r, 0, k:k + 1]).then_inc(s["ss1"], 1)
                        act.wait_ge(s["ss1"], k + 1)
                        act.activation(st[0:r, 1, k:k + 1], st[0:r, 0, k:k + 1], ACT.Sqrt, bias=b.eps[0:r], scale=1.0 / D).then_inc(s["sd1"], 1)
                    if 2 <= k < N + 2 and not modulate:
                        t = k - 2
                        r = tiles[t][1]
                        act.wait_ge(s["x"], t + 1)
                        act.activation(junk2[0:r], b.Y[0:r, t], ACT.Square, accum_out=st[0:r, 3, t:t + 1]).then_inc(s["ss2"], 1)
                        act.wait_ge(s["ss2"], t + 1)
                        act.activation(st[0:r, 4, t:t + 1], st[0:r, 3, t:t + 1], ACT.Sqrt, bias=b.eps[0:r], scale=1.0 / D).then_inc(s["sd2"], 1)
                    if 5 <= k < N + 5:
                        t = k - 5
                        c, r = tiles[t]
                        if not (kv and t == 0):
                            tt = t
                            act.wait_ge(s["tp"], t + 1)
                            o = kv["cols"](t) if kv else slice(c, c + r)
                            act.activation(b.XH[:, :, o], tp[:, t % 2, :, 0:r], ACT.Copy).then_inc(s["xh"], 1)
                        if kv:
                            act.wait_ge(s["tk"], t + 1)
                            if t == 0:
                                act.wait_ge(s["zero"], 1)
                            if t >= 2:
                                act.wait_ge(s["kvp"], t - 1)
                            o = P - r
                            act.activation(kx[:, t % 2, :, o:P], tk[:, :, 0:r], ACT.Copy).then_inc(s["kx"], 1)

            @block.vector
            def _(dve):
                dve.wait_ge(s["gains"], 16 if modulate else 32)
                if kv:
                    dve.wait_ge(s["wkv"], 80)
                for k in range(N + 8):
                    if 1 <= k < N + 1:
                        t = k - 1
                        r = tiles[t][1]
                        dve.wait_ge(s["sd1"], t + 1)
                        dve.reciprocal(st[0:r, 2, t:t + 1], st[0:r, 1, t:t + 1]).then_inc(s["r1"], 1)
                        dve.wait_ge(s["r1"], t + 1)
                        dve.scalar_tensor_tensor(b.Y[0:r, t], b.Y[0:r, t], st[0:r, 2, t:t + 1], gpost[0:r], ALU.mult, ALU.mult).then_inc(s["xg"], 1)
                        dve.wait_ge(s[f"rx{t % 3}"], 16 * (t // 3 + 1))
                        dve.wait_ge(s["xg"], t + 1)
                        dve.tensor_tensor(b.Y[0:r, t], b.Y[0:r, t], rx[0:r, t % 3], ALU.add).then_inc(s["x"], 1)
                    if 3 <= k < N + 3:
                        t = k - 3
                        r = tiles[t][1]
                        if modulate:
                            scale1, shift = modulate
                            if t >= 2:
                                dve.wait_ge(s["tp"], t - 1)
                            dve.tensor_tensor(xn[:, t % 2], b.Y[:, t], scale1, ALU.mult).then_inc(s["r2"], 1)
                            dve.wait_ge(s["r2"], t + 1)
                            dve.tensor_tensor(xn[:, t % 2], xn[:, t % 2], shift, ALU.add).then_inc(s["xn"], 1)
                    if 3 <= k < N + 3 and not modulate:
                        dve.wait_ge(s["sd2"], t + 1)
                        dve.reciprocal(st[0:r, 5, t:t + 1], st[0:r, 4, t:t + 1]).then_inc(s["r2"], 1)
                        dve.wait_ge(s["r2"], t + 1)
                        if t >= 2:
                            dve.wait_ge(s["tp"], t - 1)
                        dve.scalar_tensor_tensor(xn[0:r, t % 2], b.Y[0:r, t], st[0:r, 5, t:t + 1], gpre[0:r], ALU.mult, ALU.mult).then_inc(s["xn"], 1)
                        if kv:
                            if t >= 2:
                                dve.wait_ge(s["tk"], t - 1)
                            dve.scalar_tensor_tensor(xk[0:r, t % 2], b.Y[0:r, t], st[0:r, 5, t:t + 1], gkv[0:r], ALU.mult, ALU.mult).then_inc(s["xk"], 1)
                    if 6 <= k < N + 6:
                        t = k - 6
                        c, r = tiles[t]
                        n_h = t if kv else t + 1
                        if not (kv and t == 0):
                            dve.wait_ge(s["xh"], n_h)
                            o = kv["cols"](t) if kv else slice(c, c + r)
                            dve.tensor_tensor(b.XL[:, :, o], tp[:, t % 2, :, 0:r], b.XH[:, :, o].bitcast(f32), ALU.subtract).then_inc(s["xl"], 1)
                    if kv and 7 <= k < N + 7:
                        t = k - 7
                        dve.wait_ge(s["kvp"], t + 1)
                        dve.tensor_scalar(kv["KT"][0:HD, 0, t * P:(t + 1) * P], kvp[0:HD, 0, 0:P], bk[0:HD], None, ALU.add).then_inc(s["kdup2"], 1)
                        dve.tensor_scalar(kv["KT"][HD:P, 1, t * P:(t + 1) * P], kvp[HD:P, 0, 0:P], bk[HD:P], None, ALU.add).then_inc(s["kdup2"], 1)
                        dve.tensor_tensor(kv["V"][:, t, :], kvp[:, 1, 0:P], bv[:, :], ALU.add).then_inc(s["k"], 1)

            @block.tensor
            def _(pe):
                for k in range(N + 3):
                    if k < N:
                        c, r = tiles[k]
                        n_l = k - 2 if kv else k - 1
                        pe.wait_ge(s["xn"], k + 1)
                        if n_l > 0:
                            pe.wait_ge(s["xl"], n_l)
                        for f in range(KC):
                            last = pe.transpose(tp[:, k % 2, f, 0:r], xn[0:r, k % 2, f * P:(f + 1) * P], b.ident[0:r, 0:r])
                        last.then_inc(s["tp"], 1)
                        if kv:
                            pe.wait_ge(s["xk"], k + 1)
                            if k >= 1:
                                pe.wait_ge(s["kx"], k)
                            for f in range(KC):
                                last = pe.transpose(tk[:, f, 0:r], xk[0:r, k % 2, f * P:(f + 1) * P], b.ident[0:r, 0:r])
                            last.then_inc(s["tk"], 1)
                    if kv and 1 <= k < N + 1:
                        t = k - 1
                        pe.wait_ge(s["wkv"], 80)
                        pe.wait_ge(s["kx"], t + 1)
                        if t >= 1:
                            pe.wait_ge(s["k"], t)
                        for f in range(KC):
                            pe.matmul(kvp[:, 0, 0:P], wk[:, f], kx[:, t % 2, f], start=(f == 0), stop=(f == KC - 1))
                        for f in range(KC):
                            last = pe.matmul(kvp[:, 1, 0:P], kx[:, t % 2, f], wv[:, f], start=(f == 0), stop=(f == KC - 1))
                        last.then_inc(s["kvp"], 1)


def ffn_stage(b, name, layer, tiles, slices):
    nc, ins = b.nc, b.ins
    NS, NTL = len(slices), len(tiles)
    ND = 2 * NTL
    NG = NQ // 2
    WMAX = max(w for _, w in slices)
    wgu = ins["w_gate_up"][layer].rearrange("c p k f -> p c k f")
    wdn = ins["w_down"][layer]
    with b.stage() as ctx:
        raw = b.sb(ctx, name + "raw", [P, 3, KC, P])
        wH = b.sb(ctx, name + "wH", [P, 2, 2, KC, P], f32r)
        wL = b.sb(ctx, name + "wL", [P, 2, 2, KC, P], f32r)
        dH = b.sb(ctx, name + "dH", [P, 2, D], f32r)
        dL = b.sb(ctx, name + "dL", [P, 2, D], f32r)
        hH = b.sb(ctx, name + "hH", [P, 2, 2, TOK], f32r)
        hL = b.sb(ctx, name + "hL", [P, 2, 2, TOK], f32r)
        sg = b.sb(ctx, name + "sg", [P, 2, WMAX])
        hf = b.sb(ctx, name + "hf", [P, 2, WMAX])
        gu = b.ps(ctx, name + "gu", [P, 2, 2, 512])
        dn = b.ps(ctx, name + "dn", [P, 4, 512])
        s = {n: b.sem(ctx, name + n) for n in ("rg", "ru", "rd", "ghi", "uhi", "dhi", "glo", "ulo", "dlo", "unit", "silu", "mul", "hh", "hl", "down", "acc", "zero")}

        def gate_src(q):
            return wgu[:, bass.ds(q, 1)].rearrange("p c k f -> p (c k) f")

        def up_src(q):
            return wgu[:, bass.ds(NQ + q, 1)].rearrange("p c k f -> p (c k) f")

        def down_src(q):
            return wdn[bass.ds(q * P, P), :]

        with nc.Block() as block:
            @block.sync
            def _(sp):
                def gate_up(q, first=False):
                    if not first:
                        sp.wait_ge(s["glo"], q)
                    sp.dma_start(raw[:, 0], gate_src(q)).then_inc(s["rg"], 16)
                    if not first:
                        sp.wait_ge(s["ulo"], q)
                    sp.dma_start(raw[:, 1], up_src(q)).then_inc(s["ru"], 16)

                def down(q):
                    sp.wait_ge(s["dlo"], q)
                    sp.dma_start(raw[:, 2].rearrange("p k f -> p (k f)"), down_src(q)).then_inc(s["rd"], 16)

                gate_up(0, first=True)
                gate_up(1)
                with sp.Fori(0, NQ - 2) as q:
                    gate_up(q + 2)
                    down(q)
                down(NQ - 2)
                down(NQ - 1)

            @block.gpsimd
            def _(pool):
                pool.memset(b.Y[:, 0:NTL, :], 0.0).then_inc(s["zero"], 1)

            @block.scalar
            def _(act):
                def split_gate_up(q, slot, wait_slot=True):
                    if wait_slot:
                        act.wait_ge(s["unit"], (q - 1) * NS)
                    act.wait_ge(s["rg"], 16 * q + 16)
                    act.activation(wH[:, slot, 0], raw[:, 0], ACT.Copy).then_inc(s["ghi"], 1)
                    act.wait_ge(s["ru"], 16 * q + 16)
                    act.activation(wH[:, slot, 1], raw[:, 1], ACT.Copy).then_inc(s["uhi"], 1)

                def split_down(q, c):
                    act.wait_ge(s["down"], (q - c) * NTL)
                    act.wait_ge(s["rd"], 16 * q + 16)
                    act.activation(dH[:, c], raw[:, 2].rearrange("p k f -> p (k f)"), ACT.Copy).then_inc(s["dhi"], 1)

                def unit(q, n, slot, c, first=False):
                    c0, w = slices[n]
                    u = q * NS + n
                    i = (c * NS + n) % 2
                    act.wait_ge(s["unit"], u + 1)
                    if not first:
                        act.wait_ge(s["mul"], u - 1)
                    act.activation(sg[:, i, 0:w], gu[:, i, 0, 0:w], ACT.Silu).then_inc(s["silu"], 1)
                    act.wait_ge(s["mul"], u + 1)
                    act.activation(hH[:, slot, c, c0:c0 + w], hf[:, i, 0:w], ACT.Copy).then_inc(s["hh"], 1)

                def step(g, slot, first=False, final=False):
                    for c in range(2):
                        q = 2 * g + c
                        if not (final and c == 1):
                            split_gate_up(q + 1, (c + 1) % 2, wait_slot=not (first and c == 0))
                        if not first:
                            split_down(q - 2, c)
                        for n in range(NS):
                            unit(q, n, slot, c, first=first and c == 0 and n < 2)

                split_gate_up(0, 0, wait_slot=False)
                step(0, 0, first=True)
                with act.Fori(0, (NG - 3) // 2) as j:
                    step(2 * j + 1, 1)
                    step(2 * j + 2, 0)
                step(NG - 2, 1)
                step(NG - 1, 0, final=True)
                split_down(NQ - 2, 0)
                split_down(NQ - 1, 1)

            @block.vector
            def _(dve):
                def split_gate_up(q, slot):
                    dve.wait_ge(s["ghi"], q + 1)
                    dve.tensor_tensor(wL[:, slot, 0], raw[:, 0], wH[:, slot, 0].bitcast(f32), ALU.subtract).then_inc(s["glo"], 1)
                    dve.wait_ge(s["uhi"], q + 1)
                    dve.tensor_tensor(wL[:, slot, 1], raw[:, 1], wH[:, slot, 1].bitcast(f32), ALU.subtract).then_inc(s["ulo"], 1)

                def split_down(q, c):
                    dve.wait_ge(s["dhi"], q + 1)
                    dve.tensor_tensor(dL[:, c], raw[:, 2].rearrange("p k f -> p (k f)"), dH[:, c].bitcast(f32), ALU.subtract).then_inc(s["dlo"], 1)

                def unit(q, n, slot, c):
                    c0, w = slices[n]
                    u = q * NS + n
                    i = (c * NS + n) % 2
                    dve.wait_ge(s["silu"], u + 1)
                    dve.tensor_tensor(hf[:, i, 0:w], sg[:, i, 0:w], gu[:, i, 1, 0:w], ALU.mult).then_inc(s["mul"], 1)
                    dve.wait_ge(s["hh"], u + 1)
                    dve.tensor_tensor(hL[:, slot, c, c0:c0 + w], hf[:, i, 0:w], hH[:, slot, c, c0:c0 + w].bitcast(f32), ALU.subtract).then_inc(s["hl"], 1)

                def adds(g, par):
                    for i in range(ND):
                        t, half = i // 2, i % 2
                        r = tiles[t][1]
                        y = b.Y[0:r, t, 512 * half:512 * (half + 1)]
                        dve.wait_ge(s["down"], g * ND + i + 1)
                        dve.wait_ge(s["acc"], g * ND + i + 1)
                        dve.tensor_tensor(y, dn[0:r, (par * ND + i) % 4], y, ALU.add).then_inc(s["acc"], 1)

                def step(g, slot, first=False, final=False):
                    for c in range(2):
                        q = 2 * g + c
                        if not (final and c == 1):
                            split_gate_up(q + 1, (c + 1) % 2)
                        if not first:
                            split_down(q - 2, c)
                        for n in range(NS):
                            unit(q, n, slot, c)
                    if not first:
                        adds(g - 1, 1 - slot)

                split_gate_up(0, 0)
                dve.wait_ge(s["zero"], 1)
                dve.sem_inc(s["acc"], ND)
                step(0, 0, first=True)
                with dve.Fori(0, (NG - 3) // 2) as j:
                    step(2 * j + 1, 1)
                    step(2 * j + 2, 0)
                step(NG - 2, 1)
                step(NG - 1, 0, final=True)
                split_down(NQ - 2, 0)
                split_down(NQ - 1, 1)
                adds(NG - 1, 0)

            @block.tensor
            def _(pe):
                def gate_up(g, slot, first=False):
                    for c in range(2):
                        q = 2 * g + c
                        pe.wait_ge(s["ulo"], q + 1)
                        for n, (c0, w) in enumerate(slices):
                            i = (c * NS + n) % 2
                            u = q * NS + n
                            if not (first and c == 0 and n < 2):
                                pe.wait_ge(s["mul"], u - 1)
                            for j in range(2):
                                o = gu[:, i, j, 0:w]
                                for k in range(KC):
                                    xh, xl = b.XH[:, k, c0:c0 + w], b.XL[:, k, c0:c0 + w]
                                    pe.matmul(o, wH[:, c, j, k], xh, start=(k == 0), stop=False)
                                    pe.matmul(o, wH[:, c, j, k], xl, start=False, stop=False)
                                    last = pe.matmul(o, wL[:, c, j, k], xh, start=False, stop=(k == KC - 1))
                            last.then_inc(s["unit"], 1)

                def down(g, slot):
                    pe.wait_ge(s["dlo"], 2 * g + 2)
                    pe.wait_ge(s["hl"], (2 * g + 2) * NS)
                    for i in range(ND):
                        t, half = i // 2, i % 2
                        t0, r = tiles[t]
                        o = dn[0:r, (slot * ND + i) % 4]
                        pe.wait_ge(s["acc"], (g + 1) * ND + i - 3)
                        for c in range(2):
                            hh, hl = hH[:, slot, c, t0:t0 + r], hL[:, slot, c, t0:t0 + r]
                            wh, wl = (w[:, c, 512 * half:512 * (half + 1)] for w in (dH, dL))
                            pe.matmul(o, hh, wh, start=(c == 0), stop=False)
                            pe.matmul(o, hh, wl, start=False, stop=False)
                            last = pe.matmul(o, hl, wh, start=False, stop=(c == 1))
                        last.then_inc(s["down"], 1)

                gate_up(0, 0, first=True)
                with pe.Fori(0, (NG - 3) // 2) as j:
                    gate_up(2 * j + 1, 1)
                    down(2 * j, 0)
                    gate_up(2 * j + 2, 0)
                    down(2 * j + 1, 1)
                gate_up(NG - 2, 1)
                down(NG - 3, 0)
                gate_up(NG - 1, 0)
                down(NG - 2, 1)
                down(NG - 1, 0)


def project_features(b, name, M, chunk_src, slices, small, evac_act, evac_dve=None, raws=3):
    NS = len(slices)
    with b.stage() as ctx:
        raw = b.sb(ctx, name + "raw", [P, raws, KC, P])
        wH = b.sb(ctx, name + "wH", [P, 2, KC, P], f32r)
        wL = b.sb(ctx, name + "wL", [P, 2, KC, P], f32r)
        pr = b.ps(ctx, name + "pr", [P, 4, 512])
        s = {n: b.sem(ctx, name + n) for n in ("r0", "r1", "r2", "small", "hi", "lo", "unit", "act", "dve")}
        with b.nc.Block() as block:
            @block.sync
            def _(sp):
                for dst, src in small:
                    sp.dma_start(dst, src).then_inc(s["small"], 16)
                for m in range(M):
                    if m >= raws:
                        sp.wait_ge(s["lo"], m - raws + 1)
                    sp.dma_start(raw[:, m % raws], chunk_src(m)).then_inc(s[f"r{m % raws}"], 16)

            @block.scalar
            def _(act):
                act.wait_ge(s["small"], 16 * len(small))

                def split(m):
                    act.wait_ge(s[f"r{m % raws}"], 16 * (m // raws + 1))
                    if m >= 2:
                        act.wait_ge(s["unit"], (m - 1) * NS)
                    act.activation(wH[:, m % 2], raw[:, m % raws], ACT.Copy).then_inc(s["hi"], 1)
                split(0)
                for m in range(M):
                    if m + 1 < M:
                        split(m + 1)
                    for n, (c0, w) in enumerate(slices):
                        u = m * NS + n
                        act.wait_ge(s["unit"], u + 1)
                        evac_act(act, m, n, c0, w, pr[:, u % 4, 0:w], s["dve"], u).then_inc(s["act"], 1)

            @block.vector
            def _(dve):
                dve.wait_ge(s["small"], 16 * len(small))

                def split(m):
                    dve.wait_ge(s["hi"], m + 1)
                    dve.tensor_tensor(wL[:, m % 2], raw[:, m % raws], wH[:, m % 2].bitcast(f32), ALU.subtract).then_inc(s["lo"], 1)
                split(0)
                for m in range(M):
                    if m + 1 < M:
                        split(m + 1)
                    if evac_dve:
                        for n, (c0, w) in enumerate(slices):
                            u = m * NS + n
                            dve.wait_ge(s["act"], u + 1)
                            evac_dve(dve, m, n, c0, w, pr[:, u % 4, 0:w], s["dve"], u).then_inc(s["dve"], 1)

            @block.tensor
            def _(pe):
                done = s["dve"] if evac_dve else s["act"]
                for m in range(M):
                    pe.wait_ge(s["lo"], m + 1)
                    for n, (c0, w) in enumerate(slices):
                        u = m * NS + n
                        if u >= 4:
                            pe.wait_ge(done, u - 3)
                        o = pr[:, u % 4, 0:w]
                        for k in range(KC):
                            xh, xl = b.XH[:, k, c0:c0 + w], b.XL[:, k, c0:c0 + w]
                            pe.matmul(o, wH[:, m % 2, k], xh, start=(k == 0), stop=False)
                            pe.matmul(o, wH[:, m % 2, k], xl, start=False, stop=False)
                            last = pe.matmul(o, wL[:, m % 2, k], xh, start=False, stop=(k == KC - 1))
                        last.then_inc(s["unit"], 1)


def project_tokens(b, name, weights, parts, small, evac, on_act=False, slots=2):
    with b.stage() as ctx:
        raw = b.sb(ctx, name + "raw", [P, 3, 2, 512])
        wH = b.sb(ctx, name + "wH", [P, slots, KC, 512], f32r)
        wL = b.sb(ctx, name + "wL", [P, slots, KC, 512], f32r)
        pr = b.ps(ctx, name + "pr", [P, 4, 512])
        s = {n: b.sem(ctx, name + n) for n in ("r0", "r1", "r2", "small", "hi", "lo", "unit", "out")}
        src = weights.rearrange("(k p) f -> p k f", p=P)
        NP = KC // 2
        with b.nc.Block() as block:
            @block.sync
            def _(sp):
                for i in range(parts * NP):
                    c, k = i // NP, 2 * (i % NP)
                    if i >= 3:
                        sp.wait_ge(s["lo"], i - 2)
                    sp.dma_start(raw[:, i % 3], src[:, k:k + 2, 512 * c:512 * (c + 1)]).then_inc(s[f"r{i % 3}"], 16)
                    if i == 0:
                        for dst, a in small:
                            sp.dma_start(dst, a).then_inc(s["small"], 16)

            @block.scalar
            def _(act):
                def split(c):
                    for i in range(c * NP, (c + 1) * NP):
                        k = 2 * (i % NP)
                        act.wait_ge(s[f"r{i % 3}"], 16 * (i // 3 + 1))
                        if c >= slots:
                            act.wait_ge(s["unit"], NT * (c - slots + 1))
                        act.activation(wH[:, c % slots, k:k + 2], raw[:, i % 3], ACT.Copy).then_inc(s["hi"], 1)
                for c in range(slots):
                    split(c)
                act.wait_ge(s["small"], 16 * len(small))
                for c in range(parts):
                    if on_act:
                        for t in range(NT):
                            act.wait_ge(s["unit"], c * NT + t + 1)
                            evac(act, c, t, pr[:, (c * NT + t) % 4]).then_inc(s["out"], 1)
                    if c + slots < parts:
                        split(c + slots)

            @block.vector
            def _(dve):
                def split(c):
                    for i in range(c * NP, (c + 1) * NP):
                        k = 2 * (i % NP)
                        dve.wait_ge(s["hi"], i + 1)
                        dve.tensor_tensor(wL[:, c % slots, k:k + 2], raw[:, i % 3], wH[:, c % slots, k:k + 2].bitcast(f32), ALU.subtract).then_inc(s["lo"], 1)
                for c in range(slots):
                    split(c)
                dve.wait_ge(s["small"], 16 * len(small))
                for c in range(parts):
                    if not on_act:
                        for t in range(NT):
                            u = c * NT + t
                            dve.wait_ge(s["unit"], u + 1)
                            evac(dve, c, t, pr[:, u % 4]).then_inc(s["out"], 1)
                    if c + slots < parts:
                        split(c + slots)

            @block.tensor
            def _(pe):
                for c in range(parts):
                    for t in range(NT):
                        u = c * NT + t
                        if u >= 4:
                            pe.wait_ge(s["out"], u - 3)
                        o = pr[:, u % 4]
                        for k in range(KC):
                            if t == 0 and k % 2 == 0:
                                pe.wait_ge(s["lo"], c * NP + k // 2 + 1)
                            xh, xl = (x[:, k, P * t:P * (t + 1)] for x in (b.XH, b.XL))
                            pe.matmul(o, xh, wH[:, c % slots, k], start=(k == 0), stop=False)
                            pe.matmul(o, xh, wL[:, c % slots, k], start=False, stop=False)
                            last = pe.matmul(o, xl, wH[:, c % slots, k], start=False, stop=(k == KC - 1))
                        last.then_inc(s["unit"], 1)


def bias_stage(b, bias_rows, sinks):
    nc, ins = b.nc, b.ins
    W = 3 * P
    table = nc.dram_tensor("bias_table", [HEADS, P, W], f32, kind="Internal").ap()
    with b.stage() as ctx:
        rel = b.sb(ctx, "rel", [33, HEADS])
        hot = b.sb(ctx, "hot", [33, W])
        g = b.sb(ctx, "bias_by_offset", [HEADS, W])
        pb = b.ps(ctx, "pb", [HEADS, 512])
        s_in, s_neg, s_g, s_ge, s_out = (b.sem(ctx, n) for n in ("bias_in", "bias_neg", "bias_g", "bias_ge", "bias_out"))
        with nc.Block() as block:
            @block.sync
            def _(sp):
                sp.dma_start(rel[0:32, :], ins["rel_bias"]).then_inc(s_in, 16)
                sp.dma_start(hot[:, :], ins["cst"][0:33, C_HOT:C_HOT + W]).then_inc(s_in, 16)
                sp.dma_start(sinks[:, :], rows_of(ins["sinks"][0])).then_inc(s_in, 16)
                sp.wait_ge(s_ge, 1)
                sp.dma_start(table, g[:, :].rearrange("h (o w) -> h o w", o=1).broadcast_to([HEADS, P, W])).then_inc(s_out, 16)
                sp.wait_ge(s_out, 16)
                skew = bass.AP(tensor=table.tensor, offset=P - 1, ap=[[W - 1, P], [P * W, HEADS], [1, 2 * P]])
                sp.dma_start(bias_rows[:, :, :], skew).then_inc(s_out, 16)
                sp.wait_ge(s_out, 32)

            @block.gpsimd
            def _(pool):
                pool.memset(rel[32:33, :], NEG).then_inc(s_neg, 1)

            @block.tensor
            def _(pe):
                pe.wait_ge(s_in, 48)
                pe.wait_ge(s_neg, 1)
                pe.matmul(pb[:, 0:W], rel[:, :], hot[:, :], start=True, stop=True).then_inc(s_g, 1)

            @block.vector
            def _(dve):
                dve.wait_ge(s_g, 1)
                dve.tensor_copy(g[:, :], pb[:, 0:W]).then_inc(s_ge, 1)


def attention_stage(b, KT, V, QT, bias_rows, sinks):
    nc = b.nc
    NP = HEADS // 2
    order = list(range(1, NT)) + [0]
    with b.stage() as ctx:
        lg = b.sb(ctx, "logits", [P, 3, 2, 2 * P])
        pr = b.sb(ctx, "probs", [P, 4, 2, 2 * P])
        pT = b.sb(ctx, "probsT", [P, 2, 4, P])
        m, nm, dm, rsum, es, den, rden = (b.sb(ctx, "attn_" + n, [P, 4, 2]) for n in ("m", "nm", "dm", "rsum", "es", "den", "rden"))
        qk = b.ps(ctx, "qk", [P, 2, 2, 512])
        tp = b.ps(ctx, "attn_tp", [P, 2, 4, P])
        op = b.ps(ctx, "op", [P, 2, 512])
        s = {n: b.sem(ctx, "attn_" + n) for n in ("qk", "max", "nm", "dm", "exp", "es", "den", "rd", "pn", "tp", "pT", "pv", "xh", "xl", "mask")}
        U = NT * NP
        LAST = U + 4

        def unit(u):
            return order[u // NP], u % NP, (u % NP) // (NP // KVH)

        with nc.Block() as block:
            @block.tensor
            def _(pe):
                for k in range(LAST):
                    if k < U:
                        n, p, kvh = unit(k)
                        if k >= 2:
                            pe.wait_ge(s["max"], 2 * (k - 1))
                        for e in range(2):
                            last = pe.matmul(qk[:, k % 2, e, 0:2 * P], QT[HD * e:HD * (e + 1), p, P * n:P * (n + 1)],
                                             KT[HD * e:HD * (e + 1), kvh, P * n:P * (n + 2)], start=True, stop=True)
                        last.then_inc(s["qk"], 1)
                    if 2 <= k < U + 2:
                        u = k - 2
                        pe.wait_ge(s["pn"], 2 * (u + 1))
                        if u >= 2:
                            pe.wait_ge(s["pT"], u - 1)
                        for e in range(2):
                            for j in range(2):
                                last = pe.transpose(tp[:, u % 2, 2 * e + j], pr[:, u % 4, e, P * j:P * (j + 1)], b.ident[:, :])
                        last.then_inc(s["tp"], 1)
                    if 3 <= k < U + 3:
                        u = k - 3
                        n, p, kvh = unit(u)
                        pe.wait_ge(s["pT"], u + 1)
                        if u >= 2:
                            pe.wait_ge(s["xl"], u - 1)
                        for e in range(2):
                            for j in range(2):
                                last = pe.matmul(op[HD * e:HD * (e + 1), u % 2, 0:P], V[:, n + j, HD * kvh:HD * (kvh + 1)], pT[:, u % 2, 2 * e + j],
                                                 start=(j == 0), stop=(j == 1))
                        last.then_inc(s["pv"], 1)

            @block.vector
            def _(dve):
                for k in range(LAST):
                    if k < U:
                        n, p, _ = unit(k)
                        i = k % 4
                        if k == U - NP:
                            dve.wait_ge(s["max"], 2 * k)
                            dve.memset(bias_rows[:, :, 0:PAD], NEG).then_inc(s["mask"], 1)
                            dve.wait_ge(s["mask"], 1)
                        dve.wait_ge(s["qk"], k + 1)
                        if k >= 3:
                            dve.wait_ge(s["exp"], 2 * (k - 2))
                        for e in range(2):
                            h = 2 * p + e
                            dve.tensor_tensor_reduce(out=lg[:, k % 3, e], in0=qk[:, k % 2, e, 0:2 * P], in1=bias_rows[:, h], scale=1.0, scalar=sinks[:, h:h + 1],
                                                     op0=ALU.add, op1=ALU.max, accum_out=m[:, i, e:e + 1]).then_inc(s["max"], 1)
                        dve.wait_ge(s["max"], 2 * (k + 1))
                        dve.tensor_scalar(nm[:, i], m[:, i], -1.0, None, ALU.mult).then_inc(s["nm"], 1)
                        dve.tensor_tensor(dm[:, i], sinks[:, 2 * p:2 * p + 2], m[:, i], ALU.subtract).then_inc(s["dm"], 1)
                    if 1 <= k < U + 1:
                        u = k - 1
                        i = u % 4
                        dve.wait_ge(s["es"], u + 1)
                        dve.tensor_tensor(den[:, i], es[:, i], rsum[:, i], ALU.add).then_inc(s["den"], 1)
                        dve.wait_ge(s["den"], u + 1)
                        dve.reciprocal(rden[:, i], den[:, i]).then_inc(s["rd"], 1)
                        dve.wait_ge(s["rd"], u + 1)
                        for e in range(2):
                            dve.tensor_scalar(pr[:, i, e], pr[:, i, e], rden[:, i, e:e + 1], None, ALU.mult).then_inc(s["pn"], 1)
                    if k >= 4:
                        u = k - 4
                        n, p, _ = unit(u)
                        dve.wait_ge(s["xh"], u + 1)
                        o = (slice(None), p, slice(P * n, P * (n + 1)))
                        dve.tensor_tensor(b.XL[o], op[:, u % 2, 0:P], b.XH[o].bitcast(f32), ALU.subtract).then_inc(s["xl"], 1)

            @block.scalar
            def _(act):
                for k in range(1, LAST):
                    if k < U + 1:
                        u = k - 1
                        i = u % 4
                        act.wait_ge(s["nm"], u + 1)
                        if u >= 4:
                            act.wait_ge(s["tp"], u - 3)
                        for e in range(2):
                            act.activation(pr[:, i, e], lg[:, u % 3, e], ACT.Exp, bias=nm[:, i, e:e + 1], accum_out=rsum[:, i, e:e + 1]).then_inc(s["exp"], 1)
                        act.wait_ge(s["dm"], u + 1)
                        act.wait_ge(s["exp"], 2 * (u + 1))
                        act.activation(es[:, i], dm[:, i], ACT.Exp).then_inc(s["es"], 1)
                    if 2 <= k < U + 2:
                        u = k - 2
                        act.wait_ge(s["tp"], u + 1)
                        if u >= 2:
                            act.wait_ge(s["pv"], u - 1)
                        act.activation(pT[:, u % 2], tp[:, u % 2], ACT.Copy).then_inc(s["pT"], 1)
                    if 3 <= k < U + 3:
                        u = k - 3
                        n, p, _ = unit(u)
                        act.wait_ge(s["pv"], u + 1)
                        act.activation(b.XH[:, p, P * n:P * (n + 1)], op[:, u % 2, 0:P], ACT.Copy).then_inc(s["xh"], 1)


def layer1_mixer(b, residual_in, residual_out, x1):
    ins = b.ins
    with b.stage() as ctx:
        KT = b.sb(ctx, "KT", [P, KVH, P * (NT + 1)])
        V = b.sb(ctx, "V", [P, NT + 1, P])
        kv = {"KT": KT, "V": V, "cols": lambda t: slice(P * (t - 1), P * t)}

        def rows(src):
            return lambda t: src[TILES_META[t][0]:TILES_META[t][0] + TILES_META[t][1], :]
        post_stage(b, "p1", TILES_META, rows(residual_in), residual_out, ins["norm_ffn_post"][0], ins["norm_mix_pre"][1], kv)
        QT = b.sb(ctx, "QT", [P, KC, SEQ])
        bias_rows = b.sb(ctx, "bias_rows", [P, HEADS, 2 * P])
        sinks = b.sb(ctx, "sinks_rows", [P, HEADS])
        bias_stage(b, bias_rows, sinks)
        with b.stage() as c2:
            bq = b.sb(c2, "bq", [P, KC])
            bq8 = b.sb(c2, "bq8", [P, KC])
            s_bq = b.sem(c2, "q_bias")
            wq = ins["w_q"][0]
            done = []

            def evac(act, m, n, c0, w, bank, _, u):
                if not done:
                    act.activation(bq8[:, :], bq[:, :], ACT.Copy, scale=HD ** -0.5).then_inc(s_bq, 1)
                    act.wait_ge(s_bq, 1)
                    done.append(1)
                return act.activation(QT[:, m, c0:c0 + w], bank, ACT.Identity, bias=bq8[:, m:m + 1], scale=HD ** -0.5)
            project_features(b, "w_q_", KC, lambda m: wq[m], SLICES_SEQ, [(bq[:, :], ins["b_q"])], evac, None)
        attention_stage(b, KT, V, QT, bias_rows, sinks)
    with b.stage() as ctx:
        bo = b.sb(ctx, "bo", [P, D])
        project_tokens(b, "w_o_", ins["w_o"][0], 2, [(bo[:, :], rows_of(ins["b_o"][0]))],
                       lambda dve, c, t, bank: dve.tensor_tensor(b.Y[:, t, 512 * c:512 * (c + 1)], bank, bo[:, 512 * c:512 * (c + 1)], ALU.add))
    post_stage(b, "p2", TILES_SEQ, lambda t: residual_out[META + P * t:META + P * (t + 1), :], x1, ins["norm_mix_post"][1], ins["norm_ffn_pre"][1])


def ada_stage(b, scale1, shift, gate):
    nc, ins = b.nc, b.ins
    w = ins["w_ada_2"].rearrange("(k p) f -> p k f", p=P)
    with b.stage() as ctx:
        cc = b.sb(ctx, "cc", [P, KC])
        cs = b.sb(ctx, "cs", [P, KC])
        cb = b.sb(ctx, "cb", [P, KC, P])
        bias = b.sb(ctx, "ada_bias", [P, 3 * D])
        raw = b.sb(ctx, "ada_w", [P, 3, 2, 512])
        pm = b.ps(ctx, "ada_ps", [P, 2, 512])
        s_c, s_cs, s_cb, s_mm, s_out, s_one = (b.sem(ctx, n) for n in ("ada_c", "ada_cs", "ada_cb", "ada_mm", "ada_out", "ada_one"))
        s_w = [b.sem(ctx, f"ada_w{i}") for i in range(3)]
        s_used = b.sem(ctx, "ada_used")
        NPC = KC // 2
        with nc.Block() as block:
            @block.sync
            def _(sp):
                sp.dma_start(cc[:, :], ins["c_2"]).then_inc(s_c, 16)
                sp.dma_start(bias[:, :], rows_of(ins["b_ada_2"])).then_inc(s_c, 16)
                for i in range(6 * NPC):
                    c, k = i // NPC, 2 * (i % NPC)
                    if i >= 3:
                        sp.wait_ge(s_used, i - 2)
                    sp.dma_start(raw[:, i % 3], w[:, k:k + 2, 512 * c:512 * (c + 1)]).then_inc(s_w[i % 3], 16)

            @block.scalar
            def _(act):
                act.wait_ge(s_c, 32)
                act.activation(cs[:, :], cc[:, :], ACT.Silu).then_inc(s_cs, 1)

            @block.vector
            def _(dve):
                dve.wait_ge(s_cs, 1)
                dve.tensor_copy(cb[:, :, :], cs[:, :].rearrange("p (k o) -> p k o", o=1).broadcast_to([P, KC, P])).then_inc(s_cb, 1)
                dsts = [shift, scale1, gate]
                for c in range(6):
                    cols = slice(512 * (c % 2), 512 * (c % 2 + 1))
                    dve.wait_ge(s_mm, c + 1)
                    dve.tensor_tensor(dsts[c // 2][:, cols], pm[:, c % 2], bias[:, 512 * c:512 * (c + 1)], ALU.add).then_inc(s_out, 1)
                    if c // 2 == 1:
                        dve.wait_ge(s_out, c + 1)
                        dve.tensor_scalar(scale1[:, cols], scale1[:, cols], 1.0, None, ALU.add).then_inc(s_one, 1)

            @block.tensor
            def _(pe):
                pe.wait_ge(s_cb, 1)
                for c in range(6):
                    if c >= 2:
                        pe.wait_ge(s_out, c - 1)
                    for k in range(KC):
                        i = c * NPC + k // 2
                        if k % 2 == 0:
                            pe.wait_ge(s_w[i % 3], 16 * (i // 3 + 1))
                        last = pe.matmul(pm[:, c % 2], cb[:, k], raw[:, i % 3, k % 2], start=(k == 0), stop=(k == KC - 1))
                        if k % 2:
                            last.then_inc(s_used, 1)
                    pe.wait_ge(s_used, (c + 1) * NPC)
                    pe.sem_inc(s_mm, 1)


def gmlp_stage(b):
    nc, ins = b.nc, b.ins
    U = b.Y[:, 0:4].rearrange("p a (t f) -> p (a t) f", f=DA)
    V = b.Y[:, 4:8].rearrange("p a (t f) -> p (a t) f", f=DA)
    with ExitStack() as outer:
        G = b.sb(outer, "G", [P, NT, DA])

        def evac(act, c, t, bank):
            dst, f = ((U, ACT.Gelu_apprx_tanh), (V, ACT.Gelu_apprx_tanh), (G, ACT.Silu))[c]
            return act.activation(dst[:, t], bank, f)
        project_tokens(b, "w_in_a_", ins["w_in_2"], 3, [], evac, on_act=True, slots=1)
        with b.stage() as ctx:
            sq = b.sb(ctx, "sq", [P, NT, DA])
            gv = b.sb(ctx, "gv", [P, DA])
            bv = b.sb(ctx, "bv_ln", [P, DA])
            ws = b.sb(ctx, "ws", [P, GA, P])
            bs = b.sb(ctx, "bs", [P, GA])
            eps = b.sb(ctx, "ln_eps", [P, 1])
            st = b.sb(ctx, "ln_st", [P, 5, NT * GA])
            vm = b.ps(ctx, "vm", [P, 4, 512])
            s_in, s_mask, s_eps, s_sq, s_sd, s_vn, s_mm, s_o, s_ch = (b.sem(ctx, "gmlp_" + n) for n in ("in", "mask", "eps", "sq", "sd", "vn", "mm", "o", "chain"))
            grp = lambda x: x.rearrange("p t (g d) -> p (t g) d", d=HD)
            row = lambda x, i: x[:, i].rearrange("p (g o) -> p g o", o=1).broadcast_to([P, NT * GA, HD])
            with nc.Block() as block:
                @block.sync
                def _(sp):
                    sp.dma_start(gv[:, :], rows_of(ins["ln_v_g_2"].rearrange("g d -> (g d)"))).then_inc(s_in, 16)
                    sp.dma_start(bv[:, :], rows_of(ins["ln_v_b_2"].rearrange("g d -> (g d)"))).then_inc(s_in, 16)
                    sp.dma_start(ws[:, :, :], ins["w_spatial_2"]).then_inc(s_in, 16)
                    sp.dma_start(bs[:, :], ins["b_spatial_2"]).then_inc(s_in, 16)

                @block.gpsimd
                def _(pool):
                    pool.memset(eps[:, :], 1e-5).then_inc(s_eps, 1)
                    pool.wait_ge(s_in, 64)
                    pool.affine_select(out=ws[:, :, :], in_=ws[:, :, :], compare_op=ALU.is_ge, fill=0.0, base=0,
                                       pattern=[[0, GA], [1, P]], channel_multiplier=-1).then_inc(s_mask, 1)

                @block.scalar
                def _(act):
                    act.wait_ge(s_eps, 1)
                    act.wait_ge(s_ch, 3)
                    act.activation(sq[:, :, :], V, ACT.Square).then_inc(s_sq, 1)
                    act.wait_ge(s_ch, 4)
                    act.activation(st[:, 3], st[:, 2], ACT.Sqrt, bias=eps[:, :], scale=1.0 / HD).then_inc(s_sd, 1)

                @block.vector
                def _(dve):
                    link = linker(dve, s_ch)
                    link(dve.reduce_sum(st[:, 0], grp(V), axis=mybir.AxisListType.X))
                    link(dve.tensor_scalar(st[:, 1], st[:, 0], 1.0 / HD, None, ALU.mult))
                    link(dve.tensor_tensor(grp(V), grp(V), row(st, 1), ALU.subtract))
                    dve.wait_ge(s_sq, 1)
                    link(dve.reduce_sum(st[:, 2], grp(sq[:, :, :]), axis=mybir.AxisListType.X))
                    dve.wait_ge(s_sd, 1)
                    link(dve.reciprocal(st[:, 4], st[:, 3]))
                    link(dve.tensor_tensor(grp(V), grp(V), row(st, 4), ALU.mult))
                    dve.wait_ge(s_in, 64)
                    tiles = lambda x: x[:, :].rearrange("p (o f) -> p o f", o=1).broadcast_to([P, NT, DA])
                    link(dve.tensor_tensor(V, V, tiles(gv), ALU.mult))
                    dve.tensor_tensor(V, V, tiles(bv), ALU.add).then_inc(s_vn, 1)
                    for g in range(GA):
                        u = U[:, :, HD * g:HD * (g + 1)]
                        dve.wait_ge(s_mm, g + 1)
                        dve.scalar_tensor_tensor(u, vm[:, g % 4].rearrange("p (t d) -> p t d", d=HD), bs[:, g:g + 1], u, ALU.add, ALU.mult).then_inc(s_o, 1)
                    dve.wait_ge(s_o, GA)
                    link(dve.tensor_tensor(U, U, G[:, :, :], ALU.mult))

                @block.tensor
                def _(pe):
                    pe.wait_ge(s_mask, 1)
                    pe.wait_ge(s_vn, 1)
                    for g in range(GA):
                        if g >= 4:
                            pe.wait_ge(s_o, g - 3)
                        pe.matmul(vm[:, g % 4], ws[:, g], V[:, :, HD * g:HD * (g + 1)], start=True, stop=True).then_inc(s_mm, 1)


def recurrent_inputs(b, PB):
    ins = b.ins
    with b.stage() as ctx:
        W = SEQ + 1
        shifted = b.sb(ctx, "shifted", [P, 2, W])
        diff = b.sb(ctx, "diff", [P, 2, 512])
        mu = b.sb(ctx, "mu", [P, NB])
        s_zero, s_diff = b.sem(ctx, "shift_zero"), b.sem(ctx, "shift_diff")
        started = []

        def evac_act(act, m, n, c0, w, bank, s_dve, u):
            if not started:
                started.append(1)
                act.activation(shifted[:, :, 0:1], mu[:, 0:2].rearrange("p (a o) -> p a o", o=1), ACT.Copy, scale=0.0).then_inc(s_zero, 1)
            if m >= 2:
                act.wait_ge(s_dve, 2 * (m - 1))
            return act.activation(shifted[:, m % 2, 1 + c0:1 + c0 + w], bank, ACT.Copy)

        def evac_dve(dve, m, n, c0, w, bank, s_dve, u):
            if m == 0 and n == 0:
                dve.wait_ge(s_zero, 1)
            now, before = shifted[:, m % 2, 1 + c0:1 + c0 + w], shifted[:, m % 2, c0:c0 + w]
            if u >= 2:
                dve.wait_ge(s_dve, u - 1)
            dve.tensor_tensor(diff[:, u % 2, 0:w], before, now, ALU.subtract).then_inc(s_diff, 1)
            dve.wait_ge(s_diff, 2 * m + n + 1)
            return dve.scalar_tensor_tensor(PB[:, m, c0:c0 + w], diff[:, u % 2, 0:w], mu[:, m:m + 1], now, ALU.mult, ALU.add)
        project_features(b, "w_in_b_", NB, lambda m: ins["w_in_b_2"][m], SLICES_SEQ, [(mu[:, :], ins["mu_b_2"])], evac_act, evac_dve, raws=2)


def recurrent_gates(b, PB, kk, ab, bv, lw):
    nc, ins = b.nc, b.ins
    r, k, v, gate = (PB[:, 4 * i:4 * i + 4] for i in range(4))
    with b.stage() as ctx:
        th = b.sb(ctx, "th", [HD + 1, SEQ])
        wup = b.sb(ctx, "wup", [HD + 1, DA])
        aup = b.sb(ctx, "aup", [P, DA])
        cols = b.sb(ctx, "gate_cols", [P, 5, 4])
        blk = b.sb(ctx, "blk", [P, P])
        eps = b.sb(ctx, "kk_eps", [P, 1])
        sq = b.sb(ctx, "kk_sq", [P, 4, SEQ])
        pp = b.ps(ctx, "gates_ps", [P, 4, 512])
        n_ = {n: b.sem(ctx, "gates_" + n) for n in ("in", "const", "th", "z", "kk", "sq", "sd", "rk", "mm", "act", "dve", "chain", "gate")}
        SL = 2

        def sl(u):
            return u // SL, slice(512 * (u % SL), 512 * (u % SL + 1))
        with nc.Block() as block:
            @block.sync
            def _(sp):
                for i, n in enumerate(("a0_2", "k_k_2", "k_a_2", "r_k_2")):
                    sp.dma_start(cols[:, i], ins[n]).then_inc(n_["in"], 16)
                sp.dma_start(wup[0:HD, :], ins["w_up_2"]).then_inc(n_["in"], 16)
                sp.dma_start(wup[HD:HD + 1, :], ins["w0_2"].rearrange("(a n) -> a n", a=1)).then_inc(n_["in"], 16)
                sp.dma_start(aup[HD:P, :], ins["a_up_2"]).then_inc(n_["in"], 16)
                sp.dma_start(blk[:, :], ins["cst"][:, C_BLK:C_BLK + P]).then_inc(n_["in"], 16)

            @block.gpsimd
            def _(pool):
                pool.memset(th[HD:HD + 1, :], 1.0).then_inc(n_["const"], 1)
                pool.wait_ge(n_["const"], 1)
                pool.memset(eps[:, :], 1e-12).then_inc(n_["const"], 1)

            @block.scalar
            def _(act):
                act.wait_ge(n_["in"], 128)
                act.wait_ge(n_["const"], 2)
                act.activation(th[0:HD, :], PB[0:HD, 16], ACT.Tanh).then_inc(n_["th"], 1)
                for t in range(NT):
                    act.wait_ge(n_["mm"], t + 1)
                    act.activation(lw[:, t], pp[:, t % 4], ACT.Sigmoid).then_inc(n_["act"], 1)
                for u in range(8):
                    c, s = sl(u)
                    act.wait_ge(n_["mm"], 8 + u + 1)
                    act.activation(ab[:, c, s], pp[:, u % 4], ACT.Sigmoid, bias=cols[:, 0, c:c + 1]).then_inc(n_["act"], 1)
                for c in range(4):
                    act.wait_ge(n_["kk"], c + 1)
                    act.activation(sq[:, c], kk[:, c], ACT.Square).then_inc(n_["sq"], 1)
                act.activation(gate, gate, ACT.Silu).then_inc(n_["gate"], 1)
                for u in range(8):
                    c, s = sl(u)
                    act.wait_ge(n_["mm"], 16 + u + 1)
                    act.activation(bv[:, c, s], pp[:, u % 4], ACT.Sqrt, bias=eps[:, :]).then_inc(n_["act"], 1)

            @block.vector
            def _(dve):
                link = linker(dve, n_["chain"])
                dve.wait_ge(n_["in"], 128)
                for c in range(4):
                    dve.tensor_scalar(kk[:, c], k[:, c], cols[:, 1, c:c + 1], None, ALU.mult).then_inc(n_["kk"], 1)
                link(dve.tensor_scalar(cols[:, 4], cols[:, 2], -1.0, 1.0, ALU.mult, ALU.add))
                for u in range(8):
                    c, s = sl(u)
                    dve.wait_ge(n_["act"], 16 + u + 1)
                    link(dve.reciprocal(bv[:, c, s], bv[:, c, s]))
                    if u == 0:
                        dve.wait_ge(n_["kk"], 4)
                    link(dve.tensor_tensor(kk[:, c, s], kk[:, c, s], bv[:, c, s], ALU.mult))
                for c in range(4):
                    link(dve.tensor_scalar(sq[:, c], ab[:, c], cols[:, 2, c:c + 1], cols[:, 4, c:c + 1], ALU.mult, ALU.add))
                    link(dve.tensor_tensor(k[:, c], k[:, c], sq[:, c], ALU.mult))
                    link(dve.scalar_tensor_tensor(ab[:, c], ab[:, c], -1.0, kk[:, c], ALU.mult, ALU.mult))
                    dve.scalar_tensor_tensor(sq[:, c], r[:, c], cols[:, 3, c:c + 1], k[:, c], ALU.mult, ALU.mult).then_inc(n_["rk"], 1)
                for u in range(8):
                    c, s = sl(u)
                    dve.wait_ge(n_["mm"], 24 + u + 1)
                    dve.tensor_tensor(bv[:, c, s], pp[:, u % 4], v[:, c, s], ALU.mult).then_inc(n_["dve"], 1)

            @block.tensor
            def _(pe):
                pe.wait_ge(n_["in"], 128)
                pe.wait_ge(n_["th"], 1)
                for u in range(32):
                    if 4 <= u < 28:
                        pe.wait_ge(n_["act"], u - 3)
                    elif u >= 28:
                        pe.wait_ge(n_["dve"], u - 27)
                    o = pp[:, u % 4]
                    if u < 8:
                        mm = pe.matmul(o, th[:, P * u:P * (u + 1)], wup[:, :], start=True, stop=True)
                    elif u < 16:
                        c, s = sl(u - 8)
                        mm = pe.matmul(o, aup[HD:P, P * c:P * (c + 1)], PB[HD:P, 16, s], start=True, stop=True)
                    elif u < 24:
                        c, s = sl(u - 16)
                        pe.wait_ge(n_["sq"], c + 1)
                        mm = pe.matmul(o, blk[:, :], sq[:, c, s], start=True, stop=True)
                    else:
                        c, s = sl(u - 24)
                        pe.wait_ge(n_["rk"], c + 1)
                        mm = pe.matmul(o, blk[:, :], sq[:, c, s], start=True, stop=True)
                    mm.then_inc(n_["mm"], 1)


class Marks:

    def __init__(self, sem, names):
        self.sem, self.names, self.n = sem, names, 0

    def mark(self, ins, name):
        assert self.names[self.n % len(self.names)] == name, (self.names[self.n % len(self.names)], name)
        self.n += 1
        ins.then_inc(self.sem, 1)

    def wait(self, eng, t, name):
        if t >= 0:
            eng.wait_ge(self.sem, t * len(self.names) + self.names.index(name) + 1)


def recurrence_stage(b, PB, kk, ab, lw):
    nc, ins = b.nc, b.ins
    LV = 6
    r, k, v = (PB[:, 4 * i:4 * i + 4] for i in range(3))
    with b.stage() as ctx:
        tri = b.sb(ctx, "tri", [P, 2 * P])
        tris = b.sb(ctx, "tris", [P, 2 * P])
        lvl = b.sb(ctx, "lvl", [P, LV, P])
        ein = b.sb(ctx, "ein", [P, 2, 4, P])
        mid = b.sb(ctx, "mid", [P, 2, 4, P])
        ta = b.sb(ctx, "ta", [P, DA])
        tb = b.sb(ctx, "tb", [P, 2, DA]); tk = b.sb(ctx, "tk_tok", [P, 2, DA]); tv = b.sb(ctx, "tv", [P, 2, DA])
        LT = b.sb(ctx, "LT", [P, 2, 4, P]); AK = b.sb(ctx, "AK", [P, 2, 4, P])
        RB = b.sb(ctx, "RB", [P, 2, 4, P]); RK = b.sb(ctx, "RK", [P, 2, 4, P])
        Xi = b.sb(ctx, "Xi", [P, 2, 4, P]); XT = b.sb(ctx, "XT", [P, 2, 4, P])
        Uo = b.sb(ctx, "Uo", [P, 2, 4, P])
        MV = b.sb(ctx, "MV", [P, DA])
        WT = b.sb(ctx, "WT", [P, 2, 4, P]); UU = b.sb(ctx, "UU", [P, 2, DA])
        SA = b.sb(ctx, "SA", [P, DA])
        S = b.sb(ctx, "S", [P, 4, P])
        Sx = b.sb(ctx, "Sx", [P, 4, HD])
        inv = b.ps(ctx, "inv_ps", [P, 4, 512])
        wk = b.ps(ctx, "work_ps", [P, 2, 512])
        ch = b.ps(ctx, "chain_ps", [P, 512])
        yp = b.ps(ctx, "y_ps", [P, 512])
        s_in, s_c = b.sem(ctx, "rec_in"), b.sem(ctx, "rec_const")
        levels = range(1, LV)
        last = LV - 1

        def of_level(l):
            return ["xt"] if l == last else ["x", "xt"]

        def marks(name, names):
            return Marks(b.sem(ctx, "rec_" + name), names)

        pf = marks("pe", ["cum", "ta", "tb", "tk", "tv", "ab0", "ab1", "ak0", "ak1", "tx0", "tx1"]
                   + [n for l in levels for n in [f"p{l}0", f"p{l}1"] + [f"{x}{l}{e}" for e in range(2) for x in of_level(l)]]
                   + ["mv", "wt", "uu"])
        af = marks("act", ["ein", "eex", "eneg", "ta", "tb", "tk", "tv", "tx0", "tx1"]
                   + [f"p{l}{e}" for l in levels for e in range(2)] + ["mv", "wt"])
        df = marks("dve", ["at", "bt", "kt", "rt", "ab0", "ab1", "ak0", "ak1"]
                   + [f"{x}{l}{e}" for l in levels for e in range(2) for x in of_level(l)] + ["uu"])
        of = marks("pool", ["m0", "i0", "m1", "i1"] + [f"u{l}{e}" for l in levels for e in range(2)])
        pc = marks("pe_chain", ["sa0", "rb0", "rb1", "st0", "rk0", "rk1", "sa1", "st1", "y"])
        ac = marks("act_chain", ["y"])
        dc = marks("dve_chain", ["sa0", "rb0", "rb1", "sx00", "sx01", "s00", "s01", "rk0", "rk1", "sa1", "sx10", "sx11", "s10", "s11"])

        def tok(t):
            return slice(P * t, P * (t + 1))

        def head(c, e):
            return slice(P * c + HD * e, P * c + HD * (e + 1))

        def rows(i):
            return slice(HD * i, HD * (i + 1))

        def four(m):
            return m.rearrange("p (o t) -> p o t", o=1).broadcast_to([P, 4, P])

        def by_four(bank):
            return bank.rearrange("p (c t) -> p c t", c=4)

        with nc.Block() as block:
            @block.sync
            def _(sp):
                sp.dma_start(tri[:, :], ins["cst"][:, C_TRIU:C_TRIU + 2 * P]).then_inc(s_in, 16)
                sp.dma_start(lvl[:, :, :], ins["cst"][:, C_LVL:C_LVL + LV * P].rearrange("p (l t) -> p l t", l=LV)).then_inc(s_in, 16)

            @block.gpsimd
            def _(pool):
                pool.memset(S[:, :, :], 0.0).then_inc(s_c, 1)
                pool.wait_ge(s_in, 32)
                pool.tensor_scalar(tris[:, :], tri[:, :], -0.6065306597126334, None, ALU.mult).then_inc(s_c, 1)
                for t in range(NT):
                    for e in range(2):
                        df.wait(pool, t, f"ab{e}")
                        pf.wait(pool, t - 1, "uu")
                        of.mark(pool.tensor_tensor(XT[:, e], LT[:, e], four(lvl[:, 0]), ALU.mult), f"m{e}")
                        of.wait(pool, t, f"m{e}")
                        of.mark(pool.tensor_tensor(XT[:, e], XT[:, e], four(b.ident[:, :]), ALU.add), f"i{e}")
                    for l in levels:
                        for e in range(2):
                            if l > 1:
                                pf.wait(pool, t, f"p{l - 1}{e}")
                            else:
                                pf.wait(pool, t - 1, f"p{last}{e}")
                            of.mark(pool.tensor_tensor(Uo[:, e], LT[:, e], four(lvl[:, l]), ALU.mult), f"u{l}{e}")

            @block.scalar
            def _(act):
                def chain(t, seg):
                    if seg == 5:
                        pc.wait(act, t, "y")
                        ac.mark(act.activation(r[:, :, tok(t)], by_four(yp[:, :]), ACT.Copy), "y")

                for t in range(NT):
                    cum = wk[:, :, :].rearrange("p a (c x) -> p (a c) x", c=2)
                    pf.wait(act, t, "cum")
                    dc.wait(act, t - 2, "s11")
                    af.mark(act.activation(ein[:, t % 2], cum[:, :, 0:P], ACT.Exp), "ein")
                    pf.wait(act, t - 1, f"xt{last}1")
                    af.mark(act.activation(mid[:, 0], cum[:, :, P:2 * P], ACT.Exp), "eex")
                    af.mark(act.activation(mid[:, 1], cum[:, :, 0:P], ACT.Exp, scale=-1.0), "eneg")
                    for n, dst, bank in (("ta", ta[:, :], 0), ("tb", tb[:, t % 2], 1), ("tk", tk[:, t % 2], 0), ("tv", tv[:, t % 2], 1)):
                        pf.wait(act, t, n)
                        if n == "ta":
                            pf.wait(act, t - 1, "wt")
                        else:
                            pc.wait(act, t - 2, "y")
                        af.mark(act.activation(dst, wk[:, bank], ACT.Copy), n)
                    for e in range(2):
                        pf.wait(act, t, f"tx{e}")
                        af.mark(act.activation(Xi[:, e], by_four(inv[:, e]), ACT.Copy), f"tx{e}")
                    for l in levels:
                        for e in range(2):
                            pf.wait(act, t, f"p{l}{e}")
                            if l == 1:
                                df.wait(act, t, "kt")
                            else:
                                pf.wait(act, t, f"xt{l - 1}{e}")
                            af.mark(act.activation(mid[:, e], by_four(inv[:, e]), ACT.Copy), f"p{l}{e}")
                        if t:
                            chain(t - 1, l)
                    pf.wait(act, t, "mv")
                    af.mark(act.activation(MV[:, :], wk[:, 0], ACT.Copy), "mv")
                    pf.wait(act, t, "wt")
                    pc.wait(act, t - 2, "sa1")
                    af.mark(act.activation(WT[:, t % 2], by_four(wk[:, 1]), ACT.Copy), "wt")
                for l in levels:
                    chain(NT - 1, l)

            @block.vector
            def _(dve):
                def chain(t, seg):
                    if seg in (1, 3):
                        q = seg // 2
                        pc.wait(dve, t, f"sa{q}")
                        df.wait(dve, t, "uu")
                        pc.wait(dve, t - 1, "y")
                        dc.mark(dve.tensor_tensor(SA[rows(q)], ch[rows(q)], UU[rows(q), t % 2], ALU.add), f"sa{q}")
                    if seg == 1:
                        for e in range(2):
                            pc.wait(dve, t, f"rb{e}")
                            dc.mark(dve.tensor_tensor(RB[:, e], by_four(wk[:, e]), four(tri[:, 0:P]), ALU.mult), f"rb{e}")
                    if seg in (2, 4):
                        q = seg // 2 - 1
                        pc.wait(dve, t, f"st{q}")
                        for e in range(2):
                            dc.mark(dve.tensor_tensor(Sx[rows(e)], S[rows(e), :, rows(e)], by_four(ch[:, :])[rows(e), :, rows(e)], ALU.add), f"sx{q}{e}")
                        for e in range(2):
                            dc.wait(dve, t, f"sx{q}{e}")
                            d = ein[rows(e), t % 2, :, HD * q + HD - 1:HD * q + HD].broadcast_to([HD, 4, HD])
                            dc.mark(dve.tensor_tensor(S[rows(e), :, rows(e)], Sx[rows(e)], d, ALU.mult), f"s{q}{e}")
                    if seg == 2:
                        for e in range(2):
                            pc.wait(dve, t, f"rk{e}")
                            dc.mark(dve.tensor_tensor(RK[:, e], by_four(wk[:, e]), four(tri[:, 0:P]), ALU.mult), f"rk{e}")

                dve.wait_ge(s_c, 2)
                for t in range(NT):
                    af.wait(dve, t, "eneg")
                    df.mark(dve.tensor_tensor(kk[:, :, tok(t)], kk[:, :, tok(t)], mid[:, 0], ALU.mult), "at")
                    df.mark(dve.tensor_tensor(ab[:, :, tok(t)], ab[:, :, tok(t)], mid[:, 1], ALU.mult), "bt")
                    df.mark(dve.tensor_tensor(k[:, :, tok(t)], k[:, :, tok(t)], mid[:, 1], ALU.mult), "kt")
                    df.mark(dve.tensor_tensor(r[:, :, tok(t)], r[:, :, tok(t)], ein[:, t % 2], ALU.mult), "rt")
                    for x, dst, bank in (("ab", LT, 0), ("ak", AK, 2)):
                        for e in range(2):
                            pf.wait(dve, t, f"{x}{e}")
                            if x == "ab":
                                of.wait(dve, t - 1, f"u{last}{e}")
                            df.mark(dve.tensor_tensor(dst[:, e], by_four(inv[:, bank + e]), four(tri[:, P:2 * P]), ALU.mult), f"{x}{e}")
                    for l in levels:
                        for e in range(2):
                            for x in of_level(l):
                                pf.wait(dve, t, f"{x}{l}{e}")
                                bank = (3, 2)[e] if l == last else (2 if x == "x" else 3)
                                m = Xi if x == "x" else XT
                                df.mark(dve.tensor_tensor(m[:, e], m[:, e], by_four(inv[:, bank]), ALU.add), f"{x}{l}{e}")
                        if t:
                            chain(t - 1, l)
                    pf.wait(dve, t, "uu")
                    df.mark(dve.tensor_copy(UU[:, t % 2], wk[:, 0]), "uu")
                for l in levels:
                    chain(NT - 1, l)

            @block.tensor
            def _(pe):
                def gram(bank, left, right, t, e):
                    for c in range(4):
                        mm = pe.matmul(bank[:, P * c:P * (c + 1)], left[rows(e), c, tok(t)], right[rows(e), c, tok(t)], start=True, stop=True)
                    return mm

                def chain(t, seg):
                    if seg in (1, 3):
                        q = seg // 2
                        af.wait(pe, t, "wt")
                        if q:
                            dc.wait(pe, t, "s01")
                        else:
                            dc.wait(pe, t - 1, "s11")
                            pe.wait_ge(s_c, 2)
                        for c in range(4):
                            mm = pe.matmul(ch[rows(q), P * c:P * (c + 1)], WT[:, t % 2, c, rows(q)], S[:, c], start=True, stop=True)
                        pc.mark(mm, f"sa{q}")
                    if seg in (2, 4):
                        q = seg // 2 - 1
                        if q == 0:
                            ac.wait(pe, t - 1, "y")
                        for c in range(4):
                            pe.matmul(yp[:, P * c + HD * q:P * c + HD * (q + 1)], S[:, c], r[:, c, P * t + HD * q:P * t + HD * (q + 1)],
                                      start=(q == 0 and c == 0), stop=False, skip_group_check=True)
                        dc.wait(pe, t, f"sa{q}")
                        for c in range(4):
                            o = ch[:, P * c:P * (c + 1)]
                            pe.matmul(o, tk[rows(q), t % 2, P * c:P * (c + 1)], tv[rows(q), t % 2, P * c:P * (c + 1)], start=True, stop=False)
                            mm = pe.matmul(o, tb[rows(q), t % 2, P * c:P * (c + 1)], SA[rows(q), P * c:P * (c + 1)], start=False, stop=True)
                        pc.mark(mm, f"st{q}")
                    if seg == 1:
                        for e in range(2):
                            if t + 1 < NT:
                                af.wait(pe, t + 1, ("tk", "tv")[e])
                            else:
                                af.wait(pe, t, "wt")
                                df.wait(pe, t, "uu")
                            pc.mark(gram(wk[:, e], ab, r, t, e), f"rb{e}")
                    if seg == 2:
                        for e in range(2):
                            dc.wait(pe, t, f"rb{e}")
                            pc.mark(gram(wk[:, e], k, r, t, e), f"rk{e}")
                    if seg == 5:
                        dc.wait(pe, t, "sa1")
                        dc.wait(pe, t, "rk1")
                        for c in range(4):
                            for e in range(2):
                                o = yp[rows(e), P * c:P * (c + 1)]
                                pe.matmul(o, SA[:, head(c, e)], RB[:, e, c], start=False, stop=False, skip_group_check=True)
                                mm = pe.matmul(o, tv[:, t % 2, head(c, e)], RK[:, e, c], start=False, stop=True, skip_group_check=True)
                        pc.mark(mm, "y")

                def four_of(name, e, bank, left, right):
                    for c in range(4):
                        mm = pe.matmul(inv[:, bank, P * c:P * (c + 1)], left[:, e, c], right[:, e, c], start=True, stop=True)
                    pf.mark(mm, name)

                pe.wait_ge(s_c, 2)
                for t in range(NT):
                    af.wait(pe, t - 1, "wt")
                    df.wait(pe, t - 1, "uu")
                    for c in range(4):
                        mm = pe.matmul(wk[:, c // 2, 2 * P * (c % 2):2 * P * (c % 2 + 1)], lw[:, t, P * c:P * (c + 1)], tris[:, :], start=True, stop=True)
                    pf.mark(mm, "cum")
                    af.wait(pe, t, "eneg")
                    for n, src, bank, ready, free in (("ta", kk, 0, "at", None), ("tb", ab, 1, "bt", None), ("tk", k, 0, "kt", "ta"), ("tv", v, 1, None, "tb")):
                        if ready:
                            df.wait(pe, t, ready)
                        if free:
                            af.wait(pe, t, free)
                        for c in range(4):
                            mm = pe.transpose(wk[:, bank, P * c:P * (c + 1)], src[:, c, tok(t)], b.ident[:, :])
                        pf.mark(mm, n)
                    for x, left, bank in (("ab", ab, 0), ("ak", k, 2)):
                        for e in range(2):
                            if x == "ab":
                                af.wait(pe, t - 1, f"p{last}{e}")
                            else:
                                df.wait(pe, t - 1, f"xt{last}{1 - e}")
                            pf.mark(gram(inv[:, bank + e], left, kk, t, e), f"{x}{e}")
                    for e in range(2):
                        of.wait(pe, t, f"i{e}")
                        for c in range(4):
                            mm = pe.transpose(inv[:, e, P * c:P * (c + 1)], XT[:, e, c], b.ident[:, :])
                        pf.mark(mm, f"tx{e}")
                    for l in levels:
                        for e in range(2):
                            of.wait(pe, t, f"u{l}{e}")
                            if l == 1:
                                af.wait(pe, t, f"tx{e}")
                            else:
                                df.wait(pe, t, f"x{l - 1}{e}")
                                af.wait(pe, t, f"p{l - 1}{e}")
                            four_of(f"p{l}{e}", e, e, Uo, Xi)
                        for e in range(2):
                            af.wait(pe, t, f"p{l}{e}")
                            for x in of_level(l):
                                bank = (3, 2)[e] if l == last else (2 if x == "x" else 3)
                                if l == last:
                                    df.wait(pe, t, f"xt{l - 1}1" if e == 0 else f"x{l - 1}1")
                                elif e == 1:
                                    df.wait(pe, t, f"{x}{l}0")
                                elif l > 1:
                                    df.wait(pe, t, f"{x}{l - 1}1")
                                else:
                                    df.wait(pe, t, "ak0" if x == "x" else "ak1")
                                if l > 1:
                                    df.wait(pe, t, f"xt{l - 1}{e}")
                                if x == "x":
                                    four_of(f"x{l}{e}", e, bank, XT, mid)
                                else:
                                    four_of(f"xt{l}{e}", e, bank, mid, XT)
                        if t:
                            chain(t - 1, l)
                    df.wait(pe, t, "ak1")
                    dc.wait(pe, t - 1, "rk0")
                    for h in range(8):
                        mm = pe.matmul(wk[:, 0, HD * h:HD * (h + 1)], AK[:, h % 2, h // 2], tv[:, t % 2, HD * h:HD * (h + 1)], start=True, stop=True)
                    pf.mark(mm, "mv")
                    dc.wait(pe, t - 1, "rk1")
                    df.wait(pe, t, f"xt{last}1")
                    for c in range(4):
                        for e in range(2):
                            mm = pe.matmul(wk[rows(e), 1, P * c:P * (c + 1)], ta[:, head(c, e)], XT[:, e, c], start=True, stop=True)
                    pf.mark(mm, "wt")
                    af.wait(pe, t, "mv")
                    for h in range(8):
                        mm = pe.matmul(wk[:, 0, HD * h:HD * (h + 1)], XT[:, h % 2, h // 2], MV[:, HD * h:HD * (h + 1)], start=True, stop=True)
                    pf.mark(mm, "uu")
                for l in levels:
                    chain(NT - 1, l)


def recurrent_output(b, PB, bv):
    nc, ins = b.nc, b.ins
    y, gate = PB[:, 0:4], PB[:, 12:16]
    with b.stage() as ctx:
        blk = b.sb(ctx, "blk2", [P, P])
        eps = b.sb(ctx, "gn_eps", [P, 1])
        cols = b.sb(ctx, "gn_cols", [P, 2, 4])
        sq = b.sb(ctx, "gn_sq", [P, 2, 512])
        sd = b.sb(ctx, "gn_sd", [P, 2, 512])
        pp = b.ps(ctx, "gn_ps", [P, 2, 2, 512])
        s = {n: b.sem(ctx, "gn_" + n) for n in ("in", "eps", "mean", "yc", "sq", "var", "sd", "rs", "yn", "aff", "sum", "out")}
        U = 8

        def sl(u):
            return u // 2, slice(512 * (u % 2), 512 * (u % 2 + 1))
        with nc.Block() as block:
            @block.sync
            def _(sp):
                sp.dma_start(blk[:, :], ins["cst"][:, C_BLK:C_BLK + P]).then_inc(s["in"], 16)
                sp.dma_start(cols[:, 0], ins["gn_g_2"]).then_inc(s["in"], 16)
                sp.dma_start(cols[:, 1], ins["gn_b_2"]).then_inc(s["in"], 16)

            @block.gpsimd
            def _(pool):
                pool.memset(eps[:, :], 64e-5).then_inc(s["eps"], 1)

            @block.tensor
            def _(pe):
                pe.wait_ge(s["in"], 48)
                for i in range(U + 1):
                    if i < U:
                        c, t = sl(i)
                        if i >= 2:
                            pe.wait_ge(s["yc"], i - 1)
                        pe.matmul(pp[:, i % 2, 0], blk[:, :], y[:, c, t], start=True, stop=True).then_inc(s["mean"], 1)
                    if i >= 1:
                        u = i - 1
                        pe.wait_ge(s["sq"], u + 1)
                        if u >= 2:
                            pe.wait_ge(s["sd"], u - 1)
                        pe.matmul(pp[:, u % 2, 1], blk[:, :], sq[:, u % 2], start=True, stop=True).then_inc(s["var"], 1)

            @block.scalar
            def _(act):
                act.wait_ge(s["eps"], 1)
                act.wait_ge(s["in"], 48)
                for i in range(U + 2):
                    if i < U:
                        c, t = sl(i)
                        act.wait_ge(s["yc"], i + 1)
                        if i >= 2:
                            act.wait_ge(s["var"], i - 1)
                        act.activation(sq[:, i % 2], y[:, c, t], ACT.Square).then_inc(s["sq"], 1)
                    if 1 <= i <= U:
                        u = i - 1
                        act.wait_ge(s["var"], u + 1)
                        if u >= 2:
                            act.wait_ge(s["yn"], u - 1)
                        act.activation(sd[:, u % 2], pp[:, u % 2, 1], ACT.Sqrt, bias=eps[:, :], scale=1.0 / HD).then_inc(s["sd"], 1)
                    if i >= 2:
                        u = i - 2
                        c, t = sl(u)
                        act.wait_ge(s["yn"], u + 1)
                        act.activation(y[:, c, t], y[:, c, t], ACT.Identity, bias=cols[:, 1, c:c + 1], scale=cols[:, 0, c:c + 1]).then_inc(s["aff"], 1)

            @block.vector
            def _(dve):
                for i in range(U + 3):
                    if i < U:
                        c, t = sl(i)
                        dve.wait_ge(s["mean"], i + 1)
                        dve.scalar_tensor_tensor(y[:, c, t], pp[:, i % 2, 0], -1.0 / HD, y[:, c, t], ALU.mult, ALU.add).then_inc(s["yc"], 1)
                    if 1 <= i <= U:
                        u = i - 1
                        c, t = sl(u)
                        dve.wait_ge(s["sd"], u + 1)
                        dve.reciprocal(sd[:, u % 2], sd[:, u % 2]).then_inc(s["rs"], 1)
                        dve.wait_ge(s["rs"], u + 1)
                        dve.tensor_tensor(y[:, c, t], y[:, c, t], sd[:, u % 2], ALU.mult).then_inc(s["yn"], 1)
                    if i >= 3:
                        u = i - 3
                        c, t = sl(u)
                        dve.wait_ge(s["aff"], u + 1)
                        dve.tensor_tensor(y[:, c, t], y[:, c, t], bv[:, c, t], ALU.add).then_inc(s["sum"], 1)
                        dve.wait_ge(s["sum"], u + 1)
                        dve.tensor_tensor(gate[:, c, t], gate[:, c, t], y[:, c, t], ALU.mult).then_inc(s["out"], 1)


def join_stage(b, PB, out_a):
    nc = b.nc
    gate = PB[:, 12:16]
    with b.stage() as ctx:
        a = b.sb(ctx, "out_a_in", [P, 2, DA])
        tp = b.ps(ctx, "join_tp", [P, 2, 4, P])
        s_a = [b.sem(ctx, f"join_a{i}") for i in range(2)]
        s_tp, s_h, s_l, s_gh, s_gl = (b.sem(ctx, "join_" + n) for n in ("tp", "h", "l", "gh", "gl"))
        with nc.Block() as block:
            @block.sync
            def _(sp):
                for t in range(NT):
                    if t >= 2:
                        sp.wait_ge(s_tp, t - 1)
                    sp.dma_start(a[:, t % 2], out_a[:, t]).then_inc(s_a[t % 2], 16)

            @block.tensor
            def _(pe):
                for t in range(NT):
                    pe.wait_ge(s_a[t % 2], 16 * (t // 2 + 1))
                    if t >= 2:
                        pe.wait_ge(s_l, t - 1)
                    for c in range(4):
                        mm = pe.transpose(tp[:, t % 2, c], a[:, t % 2, P * c:P * (c + 1)], b.ident[:, :])
                    mm.then_inc(s_tp, 1)

            @block.scalar
            def _(act):
                for t in range(NT):
                    if t % 2 == 0:
                        c = t // 2
                        act.activation(b.XH[:, 4 + c], gate[:, c], ACT.Copy).then_inc(s_gh, 1)
                    act.wait_ge(s_tp, t + 1)
                    act.activation(b.XH[:, 0:4, P * t:P * (t + 1)], tp[:, t % 2], ACT.Copy).then_inc(s_h, 1)

            @block.vector
            def _(dve):
                for t in range(NT):
                    if t % 2 == 0:
                        c = t // 2
                        dve.wait_ge(s_gh, c + 1)
                        dve.tensor_tensor(b.XL[:, 4 + c], gate[:, c], b.XH[:, 4 + c].bitcast(f32), ALU.subtract).then_inc(s_gl, 1)
                    dve.wait_ge(s_h, t + 1)
                    o = (slice(None), slice(0, 4), slice(P * t, P * (t + 1)))
                    dve.tensor_tensor(b.XL[o], tp[:, t % 2], b.XH[o].bitcast(f32), ALU.subtract).then_inc(s_l, 1)


def final_stage(b, x, out):
    nc, ins = b.nc, b.ins
    ALPHA = 2 ** 0.25
    with b.stage() as ctx:
        rx = b.sb(ctx, "fin_x", [P, 3, D])
        z = b.sb(ctx, "fin_z", [P, 2, D])
        g = b.sb(ctx, "fin_g", [P, D]); be = b.sb(ctx, "fin_b", [P, D])
        eps = b.sb(ctx, "fin_eps", [P, 1])
        st = b.sb(ctx, "fin_st", [P, NT, 2, 6]); mv = b.sb(ctx, "fin_mv", [P, NT, 2])
        sd = b.sb(ctx, "fin_sd", [P, NT]); rs = b.sb(ctx, "fin_rs", [P, NT])
        s = {n: b.sem(ctx, "fin_" + n) for n in ("x0", "x1", "x2", "gb", "eps", "z", "st", "mv", "sd", "rs", "c", "n", "o", "out")}
        with nc.Block() as block:
            @block.sync
            def _(sp):
                for t in range(NT):
                    if t >= 3:
                        sp.wait_ge(s["z"], t - 2)
                    sp.dma_start(rx[:, t % 3], x[P * t:P * (t + 1), :]).then_inc(s[f"x{t % 3}"], 16)
                    if t == 0:
                        sp.dma_start(g[:, :], rows_of(ins["ln_g_2"])).then_inc(s["gb"], 16)
                        sp.dma_start(be[:, :], rows_of(ins["ln_b_2"])).then_inc(s["gb"], 16)
                for t in range(NT):
                    sp.wait_ge(s["o"], t + 1)
                    sp.dma_start(out[0, P * t:P * (t + 1), :], b.Y[:, t]).then_inc(s["out"], 16)
                sp.wait_ge(s["out"], 16 * NT)

            @block.gpsimd
            def _(pool):
                pool.memset(eps[:, :], 1e-5).then_inc(s["eps"], 1)
                pool.wait_ge(s["gb"], 32)
                for t in range(NT):
                    pool.wait_ge(s["n"], t + 1)
                    pool.tensor_tensor(b.Y[:, t], b.Y[:, t], be[:, :], ALU.add).then_inc(s["o"], 1)

            @block.scalar
            def _(act):
                act.wait_ge(s["eps"], 1)
                for t in range(NT):
                    act.wait_ge(s["mv"], t + 1)
                    act.activation(sd[:, t:t + 1], mv[:, t, 1:2], ACT.Sqrt, bias=eps[:, :]).then_inc(s["sd"], 1)

            @block.vector
            def _(dve):
                for t in range(NT + 1):
                    if t < NT:
                        dve.wait_ge(s[f"x{t % 3}"], 16 * (t // 3 + 1))
                        if t >= 2:
                            dve.wait_ge(s["n"], t - 1)
                        dve.scalar_tensor_tensor(z[:, t % 2], rx[:, t % 3], ALPHA, b.Y[:, t], ALU.mult, ALU.add).then_inc(s["z"], 1)
                        dve.wait_ge(s["z"], t + 1)
                        for h in range(2):
                            dve.bn_stats(st[:, t, h], z[:, t % 2, 512 * h:512 * (h + 1)]).then_inc(s["st"], 1)
                        dve.wait_ge(s["st"], 2 * t + 2)
                        dve.bn_aggr(mv[:, t], st[:, t].rearrange("p a b -> p (a b)")).then_inc(s["mv"], 1)
                    if t >= 1:
                        u = t - 1
                        dve.wait_ge(s["gb"], 32)
                        dve.wait_ge(s["sd"], u + 1)
                        dve.reciprocal(rs[:, u:u + 1], sd[:, u:u + 1]).then_inc(s["rs"], 1)
                        dve.wait_ge(s["rs"], u + 1)
                        dve.tensor_scalar(z[:, u % 2], z[:, u % 2], mv[:, u, 0:1], rs[:, u:u + 1], ALU.subtract, ALU.mult).then_inc(s["c"], 1)
                        dve.wait_ge(s["c"], u + 1)
                        dve.tensor_tensor(b.Y[:, u], z[:, u % 2], g[:, :], ALU.mult).then_inc(s["n"], 1)


def second_block(b, x3, x4):
    nc, ins = b.nc, b.ins
    gate_rows = b.Y[:, NT]
    out_a = nc.dram_tensor("out_a", [P, NT, DA], f32, kind="Internal").ap()
    with ExitStack() as right:
        b.alloc_x(right, "b2", SEQ, "right")
        with ExitStack() as ctx:
            scale1 = b.sb(ctx, "scale1", [P, D])
            shift = b.sb(ctx, "shift", [P, D])
            ada_stage(b, scale1, shift, gate_rows)
            post_stage(b, "p3", TILES_SEQ, lambda t: x3[P * t:P * (t + 1), :], x4, ins["norm_ffn_post"][1], None, modulate=(scale1[:, :], shift[:, :]))
        gmlp_stage(b)
        with b.stage() as ctx:
            s_a = b.sem(ctx, "out_a_kept")
            with nc.Block() as block:
                @block.sync
                def _(sp):
                    sp.dma_start(out_a, b.Y[:, 0:4].rearrange("p a (t f) -> p (a t) f", f=DA)).then_inc(s_a, 16)
                    sp.wait_ge(s_a, 16)
        left = ExitStack()
        PB = b.sb(left, "PB", [P, NB, SEQ])
        recurrent_inputs(b, PB)
    with ExitStack() as ctx:
        kk = b.sb(ctx, "kk", [P, 4, SEQ])
        ab = b.sb(ctx, "ab", [P, 4, SEQ])
        bv = b.Y[:, 0:4]
        lw = b.Y[:, 4:8].rearrange("p a (t f) -> p (a t) f", f=DA)
        recurrent_gates(b, PB, kk, ab, bv, lw)
        recurrence_stage(b, PB, kk, ab, lw)
        recurrent_output(b, PB, bv)
    with ExitStack() as right:
        b.alloc_x(right, "b3", SEQ, "right")
        join_stage(b, PB, out_a)
        left.close()
        project_tokens(b, "w_out_", ins["w_out_2"], 2, [],
                       lambda dve, c, t, bank: dve.tensor_tensor(b.Y[:, t, 512 * c:512 * (c + 1)], bank, gate_rows[:, 512 * c:512 * (c + 1)], ALU.mult))
    final_stage(b, x4, b.out)


def program(nc, ins, out):
    with ExitStack() as ctx:
        b = Builder(nc, ctx, ins, out)
        meta, x = ins["meta_tokens"], ins["x"]
        with ExitStack() as first:
            b.alloc_x(first, "b1", TOK, "right")
            pool_stage(b)
            post_stage(b, "p0", TILES_META, lambda t: meta if t == 0 else x[0, P * (t - 1):P * t, :], b.res[0], ins["norm_mix_post"][0], ins["norm_ffn_pre"][0])
            ffn_stage(b, "f0", 0, TILES_META, SLICES_META)
            layer1_mixer(b, b.res[0], b.res[1], b.res[2])
            ffn_stage(b, "f1", 1, TILES_SEQ, SLICES_SEQ)
        second_block(b, b.res[2], b.res[3])


def kernel(**inputs):
    import concourse.bacc as bacc
    from concourse.bass_utils import run_bass_kernel_spmd

    nc = bacc.Bacc("TRN2", target_bir_lowering=False, num_devices=1)
    arrays = {f"in_{n}": a for n, a in lay_out(inputs).items()}
    ins = {n[3:]: nc.dram_tensor(n, a.shape, mybir.dt.from_np(a.dtype), kind="ExternalInput").ap() for n, a in arrays.items()}
    out = nc.dram_tensor("out", (1, SEQ, D), f32, kind="ExternalOutput").ap()
    program(nc, ins, out)
    r = run_bass_kernel_spmd(nc, [arrays], core_ids=[0])
    return r.results[0]["out"]
```

```python
import concourse.bass as bass
from concourse import mybir
from contextlib import ExitStack, contextmanager

f32 = mybir.dt.float32
f32r = mybir.dt.float32r
ALU = mybir.AluOpType
ACT = mybir.ActivationFunctionType

P = 128
D = 1024
KC = D // P
SEQ = 1024
META = 16
NT = SEQ // P
TOK = META + SEQ
FF = 2816
NQ = FF // P
EPS = 1e-6
POOLS = (2, 4, 8, 16)
HEADS = 16
KVH = 2
HD = 64
PAD = P - META
NEG = -1e30

TILES_META = [(0, META)] + [(META + P * i, P) for i in range(NT)]
TILES_SEQ = [(P * i, P) for i in range(NT)]
SLICES_META = [(0, 348), (348, 346), (694, 346)]
SLICES_SEQ = [(0, 512), (512, 512)]

C_ID = 0
C_BAND = C_ID + P
C_PREV = C_BAND + 4 * P
C_MBAND = C_PREV + 4 * META
C_MPREV = C_MBAND + 4 * META
C_HOT = C_MPREV + 4 * META
C_DIST = 3 * P - 1
C_TRIU = C_HOT + C_DIST + 1
C_TRIX = C_TRIU + P
C_BLK = C_TRIX + P
C_CAUS = C_BLK + P
C_LVL = C_CAUS + P
C_IND = C_LVL + 6 * P
C_END = C_IND + 2
CHUNK = 64
DA = 512
GA = DA // HD
COLS_A = 3 * DA
NB = 17


def constants():
    import math
    import numpy as np
    c = np.zeros((P, C_END), np.float32)
    i = np.arange(P)
    s, t = i[:, None], i[None, :]
    c[:, C_ID:C_ID + P] = np.eye(P)
    for g, w in enumerate(POOLS):
        c[:, C_BAND + g * P:C_BAND + (g + 1) * P] = ((t - s >= 0) & (t - s < w)) / w - (s == t)
        prev = ((t + P - s) < w) / w
        c[:, C_PREV + g * META:C_PREV + (g + 1) * META] = prev[:, :META]
        c[:META, C_MPREV + g * META:C_MPREV + (g + 1) * META] = prev[P - META:, :META]
        m = ((t - s >= 0) & (t - s < w)) / np.minimum(t + 1, w).astype(np.float32) - (s == t)
        c[:META, C_MBAND + g * META:C_MBAND + (g + 1) * META] = m[:META, :META]
    for u in range(C_DIST):
        d = 2 * P - 1 - u
        if 0 <= d < P:
            if d < 16:
                b = d
            else:
                b = min(31, 16 + int(np.float32(np.float32(math.log(np.float32(d) / np.float32(16.0))) / np.float32(math.log(8.0))) * np.float32(16)))
            c[b, C_HOT + u] = 1
        else:
            c[32, C_HOT + u] = 1
    same = (s // CHUNK) == (t // CHUNK)
    c[:, C_TRIU:C_TRIU + P] = (s <= t) & same
    c[:, C_TRIX:C_TRIX + P] = (s < t) & same
    c[:, C_BLK:C_BLK + P] = same
    c[:, C_CAUS:C_CAUS + P] = s <= t
    for l in range(6):
        m = 1 << l
        c[:, C_LVL + l * P:C_LVL + (l + 1) * P] = (s // (2 * m) == t // (2 * m)) & (s % (2 * m) < m) & (t % (2 * m) >= m)
    c[:, C_IND:C_IND + 2] = (i[:, None] // HD) == np.arange(2)[None, :]
    return c


def rows_of(vector, n=P):
    return vector.rearrange("(a n) -> a n", a=1).broadcast_to([n, vector.shape[0]])


def lay_out(inputs):
    import numpy as np
    a = {n: np.ascontiguousarray(v) for n, v in inputs.items()}
    for n in ("b_q", "b_k", "b_v"):
        a[n] = np.ascontiguousarray(a[n].reshape(-1, P).T)
    a["gains_q"] = np.ascontiguousarray(a["norm_mix_pre"][1].reshape(-1, P).T)
    a["gains_kv"] = np.ascontiguousarray(a["kv_norm"].reshape(-1, P).T)
    for n in ("w_gate_up", "w_q"):
        w = a[n]
        w = w.reshape(w.shape[0], KC, P, w.shape[2] // P, P)
        a[n] = np.ascontiguousarray(w.transpose(0, 3, 2, 1, 4))
    for n in ("c_2", "mu_b_2", "a0_2", "k_k_2", "k_a_2", "r_k_2", "gn_g_2", "gn_b_2"):
        a[n] = np.ascontiguousarray(a[n].reshape(-1, P).T)
    a["w_spatial_2"] = np.ascontiguousarray(a["w_spatial_2"].transpose(2, 0, 1))
    a["b_spatial_2"] = np.ascontiguousarray(a["b_spatial_2"].T)
    w = a["w_in_2"]
    a["w_in_2"] = np.ascontiguousarray(w[:, :COLS_A])
    a["w_in_b_2"] = np.ascontiguousarray(w[:, COLS_A:].reshape(KC, P, NB, P).transpose(2, 1, 0, 3))
    a["cst"] = constants()
    return a


class Builder:

    def __init__(self, nc, ctx, ins, out):
        self.nc, self.ctx, self.ins, self.out = nc, ctx, ins, out
        self.eps = self.sb(ctx, "eps", [P, 1])
        self.ident = self.sb(ctx, "identity", [P, P])
        self.scopes = []
        self.Y = self.sb(ctx, "Y", [P, NT + 1, D])
        self.res = [nc.dram_tensor(f"residual{i}", [TOK, D], f32, kind="Internal").ap() for i in range(4)]

    def sb(self, ctx, name, shape, dt=f32, side="left"):
        return ctx.enter_context(self.nc.sbuf_tensor(name, shape, dt, side=side))

    def ps(self, ctx, name, shape, dt=f32):
        return ctx.enter_context(self.nc.psum_tensor(name, shape, dt))

    def sem(self, ctx, name):
        handle = ctx.enter_context(self.nc.semaphore(name))
        self.scopes[-1].append(handle)
        return handle

    @contextmanager
    def stage(self):
        with ExitStack() as ctx:
            self.scopes.append([])
            yield ctx
            used = self.scopes.pop()
            if used:
                with self.nc.Block() as block:
                    @block.gpsimd
                    def _(pool):
                        for handle in used:
                            pool.sem_clear(handle)

    def alloc_x(self, ctx, name, tokens, side="left"):
        self.XH = self.sb(ctx, name + "XH", [P, KC, tokens], f32r, side)
        self.XL = self.sb(ctx, name + "XL", [P, KC, tokens], f32r, side)


def linker(eng, sem):
    n = [0]

    def link(ins):
        n[0] += 1
        ins.then_inc(sem, 1)
        eng.wait_ge(sem, n[0])
    return link


def pool_stage(b):
    nc, ins = b.nc, b.ins
    G = len(POOLS)
    with b.stage() as ctx:
        cst = b.sb(ctx, "pool_constants", [P, C_HOT])
        xin = b.sb(ctx, "xin", [P, 3, D])
        junk = b.sb(ctx, "sq_junk", [P, D])
        xn = b.sb(ctx, "xn", [P, 3, D])
        gpre = b.sb(ctx, "gpre", [P, D])
        scale = b.sb(ctx, "pool_scale_rows", [P, D])
        wraw = b.sb(ctx, "wraw", [P, 2 * G, 256])
        wH = b.sb(ctx, "wH", [P, 2 * G, 256], f32r)
        wL = b.sb(ctx, "wL", [P, 2 * G, 256], f32r)
        pH = b.sb(ctx, "pH", [P, 2, KC, P], f32r)
        pL = b.sb(ctx, "pL", [P, 2, KC, P], f32r)
        ss = b.sb(ctx, "ss", [P, 9]); sd = b.sb(ctx, "sd", [P, 9]); rs = b.sb(ctx, "rs", [P, 9])
        pt = b.ps(ctx, "pt", [P, 2, KC, P])
        mx = b.ps(ctx, "mx", [P, 2, D])
        loaded = [b.sem(ctx, f"pool_x{i}") for i in range(3)]
        s_cst, s_w, s_sc = b.sem(ctx, "pool_cst"), b.sem(ctx, "pool_w_in"), b.sem(ctx, "pool_sc")
        s_wh, s_wl, s_eps = b.sem(ctx, "pool_wh"), b.sem(ctx, "pool_wl"), b.sem(ctx, "pool_eps")
        s_ss, s_sd, s_r, s_xn = (b.sem(ctx, f"pool_{n}") for n in ("ss", "sd", "r", "xn"))
        s_pt, s_ph, s_pl, s_mx, s_y = (b.sem(ctx, f"pool_{n}") for n in ("pt", "ph", "pl", "mx", "y"))
        N = len(TILES_META)

        with nc.Block() as block:
            @block.sync
            def _(sp):
                for t, (_, r) in enumerate(TILES_META):
                    if t >= 3:
                        sp.wait_ge(s_xn, t - 2)
                    src = ins["meta_tokens"] if t == 0 else ins["x"][0, P * (t - 1):P * t, :]
                    sp.dma_start(xin[0:r, t % 3], src).then_inc(loaded[t % 3], 16)
                    if t == 0:
                        sp.dma_start(cst[:, :], ins["cst"][:, 0:C_HOT]).then_inc(s_cst, 16)
                        sp.dma_start(b.ident[:, :], ins["cst"][:, C_ID:C_ID + P]).then_inc(s_cst, 16)
                        sp.dma_start(gpre[:, :], rows_of(ins["norm_mix_pre"][0])).then_inc(s_cst, 16)
                        sp.dma_start(wraw[:, :, :], ins["pool_w"][0].rearrange("g (k p) d -> p (g k) d", p=P)).then_inc(s_w, 16)
                        sp.dma_start(scale[:, :], rows_of(ins["pool_scale"][0])).then_inc(s_sc, 16)

            @block.gpsimd
            def _(pool):
                pool.memset(b.eps[:, :], EPS).then_inc(s_eps, 1)

            @block.scalar
            def _(act):
                act.wait_ge(s_eps, 1)
                for t in range(N + 1):
                    if t < N:
                        r = TILES_META[t][1]
                        act.wait_ge(loaded[t % 3], 16 * (t // 3 + 1))
                        act.activation(junk[0:r], xin[0:r, t % 3], ACT.Square, accum_out=ss[0:r, t:t + 1]).then_inc(s_ss, 1)
                        act.wait_ge(s_ss, t + 1)
                        act.activation(sd[0:r, t:t + 1], ss[0:r, t:t + 1], ACT.Sqrt, bias=b.eps[0:r], scale=1.0 / D).then_inc(s_sd, 1)
                    if t == 0:
                        act.wait_ge(s_w, 16)
                        act.activation(wH[:, :, :], wraw[:, :, :], ACT.Copy).then_inc(s_wh, 1)
                    if t >= 1:
                        k, r = t - 1, TILES_META[t - 1][1]
                        act.wait_ge(s_pt, k + 1)
                        if k >= 2:
                            act.wait_ge(s_mx, k - 1)
                        act.activation(pH[:, k % 2, :, 0:r], pt[:, k % 2, :, 0:r], ACT.Copy).then_inc(s_ph, 1)

            @block.vector
            def _(dve):
                dve.wait_ge(s_cst, 48)
                for t in range(N + 3):
                    if t < N:
                        r = TILES_META[t][1]
                        dve.wait_ge(s_sd, t + 1)
                        dve.reciprocal(rs[0:r, t:t + 1], sd[0:r, t:t + 1]).then_inc(s_r, 1)
                        dve.wait_ge(s_r, t + 1)
                        if t >= 3:
                            dve.wait_ge(s_pt, t - 1)
                        dve.scalar_tensor_tensor(xn[0:r, t % 3], xin[0:r, t % 3], rs[0:r, t:t + 1], gpre[0:r], ALU.mult, ALU.mult).then_inc(s_xn, 1)
                    if t == 0:
                        dve.wait_ge(s_wh, 1)
                        dve.tensor_tensor(wL[:, :, :], wraw[:, :, :], wH[:, :, :].bitcast(f32), ALU.subtract).then_inc(s_wl, 1)
                        dve.wait_ge(s_sc, 16)
                    if 1 <= t <= N:
                        k, r = t - 1, TILES_META[t - 1][1]
                        dve.wait_ge(s_ph, k + 1)
                        dve.tensor_tensor(pL[:, k % 2, :, 0:r], pt[:, k % 2, :, 0:r], pH[:, k % 2, :, 0:r].bitcast(f32), ALU.subtract).then_inc(s_pl, 1)
                    if 2 <= t < N + 2:
                        k, r = t - 2, TILES_META[t - 2][1]
                        dve.wait_ge(s_mx, k + 1)
                        dve.tensor_tensor(b.Y[0:r, k], mx[0:r, k % 2], scale[0:r], ALU.mult).then_inc(s_y, 1)

            @block.tensor
            def _(pe):
                pe.wait_ge(s_cst, 48)
                for t in range(N + 1):
                    if t < N:
                        r = TILES_META[t][1]
                        pe.wait_ge(s_xn, t + 1)
                        if t >= 2:
                            pe.wait_ge(s_pl, t - 1)
                        for f in range(KC):
                            g = f // 2
                            band = cst[0:r, C_BAND + g * P:C_BAND + g * P + r] if t else cst[0:r, C_MBAND + g * META:C_MBAND + (g + 1) * META]
                            last = pe.matmul(pt[:, t % 2, f, 0:r], xn[0:r, t % 3, f * P:(f + 1) * P], band, start=True, stop=True, skip_group_check=True)
                            if t:
                                rp = TILES_META[t - 1][1]
                                c0 = C_PREV if t > 1 else C_MPREV
                                last = pe.matmul(pt[:, t % 2, f, 0:META], xn[0:rp, (t - 1) % 3, f * P:(f + 1) * P],
                                                 cst[0:rp, c0 + g * META:c0 + (g + 1) * META], start=False, stop=True, skip_group_check=True)
                        last.then_inc(s_pt, 1)
                    if t >= 1:
                        k, r = t - 1, TILES_META[t - 1][1]
                        pe.wait_ge(s_pl, k + 1)
                        pe.wait_ge(s_wl, 1)
                        if k >= 2:
                            pe.wait_ge(s_y, k - 1)
                        for g in range(G):
                            for i in range(2):
                                c = 2 * g + i
                                o = mx[0:r, k % 2, 256 * g:256 * (g + 1)]
                                pe.matmul(o, pH[:, k % 2, c, 0:r], wH[:, c], start=(i == 0), stop=False)
                                pe.matmul(o, pL[:, k % 2, c, 0:r], wH[:, c], start=False, stop=False)
                                last = pe.matmul(o, pH[:, k % 2, c, 0:r], wL[:, c], start=False, stop=(i == 1))
                        last.then_inc(s_mx, 1)


class Tail:

    STEPS = 5

    def __init__(self, b, ctx, name, tiles, residual, store, post_gain, pre_gain=None, modulate=None, cols=None,
                 ready=None, junk=None, loads=2, slots=2):
        self.b, self.tiles, self.residual, self.store = b, tiles, residual, store
        self.post_gain, self.pre_gain, self.modulate = post_gain, pre_gain, modulate
        self.loads, self.slots, self.N = loads, slots, len(tiles)
        self.cols = cols or (lambda t: slice(tiles[t][0], tiles[t][0] + tiles[t][1]))
        self.ready = ready or (lambda eng, t: None)
        self.rx = b.sb(ctx, name + "rx", [P, loads, D])
        self.junk = junk if junk is not None else b.sb(ctx, name + "junk", [P, D])
        self.xn = b.sb(ctx, name + "xn", [P, 2, D])
        self.gpost = b.sb(ctx, name + "gpost", [P, D])
        self.gpre = b.sb(ctx, name + "gpre", [P, D]) if pre_gain is not None else None
        self.scale = b.sb(ctx, name + "scale", [P, D]) if modulate else None
        self.shift = b.sb(ctx, name + "shift", [P, D]) if modulate else None
        self.st = b.sb(ctx, name + "st", [P, 6, 9])
        self.tp = b.ps(ctx, name + "tp", [P, slots, KC, P])
        names = [f"rx{i}" for i in range(loads)] + ["gains", "ss1", "sd1", "r1", "xg", "x", "ss2", "sd2", "r2", "xn", "tp", "xh", "xl", "stored"]
        self.s = {n: b.sem(ctx, name + n) for n in names}

    def load_gains(self, sp):
        s = self.s["gains"]
        sp.dma_start(self.gpost[:, :], rows_of(self.post_gain)).then_inc(s, 16)
        self.gains = 16
        if self.gpre is not None:
            sp.dma_start(self.gpre[:, :], rows_of(self.pre_gain)).then_inc(s, 16)
            self.gains += 16
        if self.modulate:
            sp.dma_start(self.scale[:, :], rows_of(self.modulate[0])).then_inc(s, 16)
            sp.dma_start(self.shift[:, :], rows_of(self.modulate[1])).then_inc(s, 16)
            self.gains += 32

    def load(self, sp, t):
        r = self.tiles[t][1]
        if t >= self.loads:
            sp.wait_ge(self.s["x"], t - self.loads + 1)
        sp.dma_start(self.rx[0:r, t % self.loads], self.residual(t)).then_inc(self.s[f"rx{t % self.loads}"], 16)

    def keep(self, sp, t):
        c, r = self.tiles[t]
        sp.wait_ge(self.s["x"], t + 1)
        sp.dma_start(self.store[c:c + r, :], self.b.Y[0:r, t]).then_inc(self.s["stored"], 16)

    def sync(self, sp):
        ahead = self.loads - 1
        for t in range(ahead):
            self.load(sp, t)
        for t in range(self.N):
            if t + ahead < self.N:
                self.load(sp, t + ahead)
            self.keep(sp, t)
        sp.wait_ge(self.s["stored"], 16 * self.N)

    def gpsimd(self, pool):
        s, Y = self.s, self.b.Y
        for t in range(self.N):
            r = self.tiles[t][1]
            pool.wait_ge(s[f"rx{t % self.loads}"], 16 * (t // self.loads + 1))
            pool.wait_ge(s["xg"], t + 1)
            pool.tensor_tensor(Y[0:r, t], Y[0:r, t], self.rx[0:r, t % self.loads], ALU.add).then_inc(s["x"], 1)

    def _square(self, act, t, row, total, root):
        r, st = self.tiles[t][1], self.st
        act.activation(self.junk[0:r], self.b.Y[0:r, t], ACT.Square, accum_out=st[0:r, row, t:t + 1]).then_inc(self.s[total], 1)
        act.wait_ge(self.s[total], t + 1)
        act.activation(st[0:r, row + 1, t:t + 1], st[0:r, row, t:t + 1], ACT.Sqrt, bias=self.b.eps[0:r], scale=1.0 / D).then_inc(self.s[root], 1)

    def scalar(self, act, k):
        s = self.s
        if k < self.N:
            self.ready(act, k)
            self._square(act, k, 0, "ss1", "sd1")
        if 0 <= k - 2 < self.N and not self.modulate:
            act.wait_ge(s["x"], k - 1)
            self._square(act, k - 2, 3, "ss2", "sd2")
        if 0 <= k - 3 < self.N:
            t = k - 3
            act.wait_ge(s["tp"], t + 1)
            act.activation(self.b.XH[:, :, self.cols(t)], self.tp[:, t % self.slots, :, 0:self.tiles[t][1]], ACT.Copy).then_inc(s["xh"], 1)

    def vector(self, dve, k):
        s, st, Y, xn = self.s, self.st, self.b.Y, self.xn
        if k == 0:
            dve.wait_ge(s["gains"], self.gains)
        if k < self.N:
            t, r = k, self.tiles[k][1]
            self.ready(dve, t)
            dve.wait_ge(s["sd1"], t + 1)
            dve.reciprocal(st[0:r, 2, t:t + 1], st[0:r, 1, t:t + 1]).then_inc(s["r1"], 1)
            dve.wait_ge(s["r1"], t + 1)
            dve.scalar_tensor_tensor(Y[0:r, t], Y[0:r, t], st[0:r, 2, t:t + 1], self.gpost[0:r], ALU.mult, ALU.mult).then_inc(s["xg"], 1)
        if 0 <= k - 4 < self.N:
            t = k - 4
            r, o = self.tiles[t][1], self.cols(t)
            dve.wait_ge(s["xh"], t + 1)
            dve.tensor_tensor(self.b.XL[:, :, o], self.tp[:, t % self.slots, :, 0:r], self.b.XH[:, :, o].bitcast(f32), ALU.subtract).then_inc(s["xl"], 1)
        if 0 <= k - 2 < self.N:
            t = k - 2
            r = self.tiles[t][1]
            if self.modulate:
                dve.wait_ge(s["x"], t + 1)
                if t >= 2:
                    dve.wait_ge(s["tp"], t - 1)
                dve.tensor_tensor(xn[0:r, t % 2], Y[0:r, t], self.scale[0:r], ALU.mult).then_inc(s["r2"], 1)
                dve.wait_ge(s["r2"], t + 1)
                dve.tensor_tensor(xn[0:r, t % 2], xn[0:r, t % 2], self.shift[0:r], ALU.add).then_inc(s["xn"], 1)
            else:
                dve.wait_ge(s["sd2"], t + 1)
                dve.reciprocal(st[0:r, 5, t:t + 1], st[0:r, 4, t:t + 1]).then_inc(s["r2"], 1)
                dve.wait_ge(s["r2"], t + 1)
                if t >= 2:
                    dve.wait_ge(s["tp"], t - 1)
                if self.gpre is not None:
                    dve.scalar_tensor_tensor(xn[0:r, t % 2], Y[0:r, t], st[0:r, 5, t:t + 1], self.gpre[0:r], ALU.mult, ALU.mult).then_inc(s["xn"], 1)
                else:
                    dve.tensor_scalar(xn[0:r, t % 2], Y[0:r, t], st[0:r, 5, t:t + 1], None, ALU.mult).then_inc(s["xn"], 1)

    def tensor(self, pe, t):
        r = self.tiles[t][1]
        pe.wait_ge(self.s["xn"], t + 1)
        if t >= self.slots:
            pe.wait_ge(self.s["xl"], t - self.slots + 1)
        for f in range(KC):
            last = pe.transpose(self.tp[:, t % self.slots, f, 0:r], self.xn[0:r, t % 2, f * P:(f + 1) * P], self.b.ident[0:r, 0:r])
        last.then_inc(self.s["tp"], 1)


def post_stage(b, name, tiles, residual, store, post_gain, pre_gain=None, **more):
    with b.stage() as ctx:
        tail = Tail(b, ctx, name, tiles, residual, store, post_gain, pre_gain, loads=3, **more)
        with b.nc.Block() as block:
            @block.sync
            def _(sp):
                tail.load_gains(sp)
                tail.sync(sp)

            @block.gpsimd
            def _(pool):
                tail.gpsimd(pool)

            @block.scalar
            def _(act):
                for k in range(tail.N + tail.STEPS):
                    tail.scalar(act, k)

            @block.vector
            def _(dve):
                for k in range(tail.N + tail.STEPS):
                    tail.vector(dve, k)

            @block.tensor
            def _(pe):
                for t in range(tail.N):
                    tail.tensor(pe, t)


def ffn_stage(b, name, layer, tiles, slices):
    nc, ins = b.nc, b.ins
    NS, NTL = len(slices), len(tiles)
    ND = 2 * NTL
    NG = NQ // 2
    WMAX = max(w for _, w in slices)
    wgu = ins["w_gate_up"][layer].rearrange("c p k f -> p c k f")
    wdn = ins["w_down"][layer]
    with b.stage() as ctx:
        raw = b.sb(ctx, name + "raw", [P, 3, KC, P])
        wH = b.sb(ctx, name + "wH", [P, 2, 2, KC, P], f32r)
        wL = b.sb(ctx, name + "wL", [P, 2, 2, KC, P], f32r)
        dH = b.sb(ctx, name + "dH", [P, 2, D], f32r)
        dL = b.sb(ctx, name + "dL", [P, 2, D], f32r)
        hH = b.sb(ctx, name + "hH", [P, 2, 2, TOK], f32r)
        hL = b.sb(ctx, name + "hL", [P, 2, 2, TOK], f32r)
        sg = b.sb(ctx, name + "sg", [P, 2, WMAX])
        hf = b.sb(ctx, name + "hf", [P, 2, WMAX])
        gu = b.ps(ctx, name + "gu", [P, 2, 2, 512])
        dn = b.ps(ctx, name + "dn", [P, 4, 512])
        s = {n: b.sem(ctx, name + n) for n in ("rg", "ru", "rd", "ghi", "uhi", "dhi", "glo", "ulo", "dlo", "unit", "silu", "mul", "hh", "hl", "down", "acc", "zero")}

        def gate_src(q):
            return wgu[:, bass.ds(q, 1)].rearrange("p c k f -> p (c k) f")

        def up_src(q):
            return wgu[:, bass.ds(NQ + q, 1)].rearrange("p c k f -> p (c k) f")

        def down_src(q):
            return wdn[bass.ds(q * P, P), :]

        with nc.Block() as block:
            @block.sync
            def _(sp):
                def gate_up(q, first=False):
                    if not first:
                        sp.wait_ge(s["glo"], q)
                    sp.dma_start(raw[:, 0], gate_src(q)).then_inc(s["rg"], 16)
                    if not first:
                        sp.wait_ge(s["ulo"], q)
                    sp.dma_start(raw[:, 1], up_src(q)).then_inc(s["ru"], 16)

                def down(q):
                    sp.wait_ge(s["dlo"], q)
                    sp.dma_start(raw[:, 2].rearrange("p k f -> p (k f)"), down_src(q)).then_inc(s["rd"], 16)

                gate_up(0, first=True)
                gate_up(1)
                with sp.Fori(0, NQ - 2) as q:
                    gate_up(q + 2)
                    down(q)
                down(NQ - 2)
                down(NQ - 1)

            @block.gpsimd
            def _(pool):
                pool.memset(b.Y[:, 0:NTL, :], 0.0).then_inc(s["zero"], 1)

            @block.scalar
            def _(act):
                def split_gate_up(q, slot, wait_slot=True):
                    if wait_slot:
                        act.wait_ge(s["unit"], (q - 1) * NS)
                    act.wait_ge(s["rg"], 16 * q + 16)
                    act.activation(wH[:, slot, 0], raw[:, 0], ACT.Copy).then_inc(s["ghi"], 1)
                    act.wait_ge(s["ru"], 16 * q + 16)
                    act.activation(wH[:, slot, 1], raw[:, 1], ACT.Copy).then_inc(s["uhi"], 1)

                def split_down(q, c):
                    act.wait_ge(s["down"], (q - c) * NTL)
                    act.wait_ge(s["rd"], 16 * q + 16)
                    act.activation(dH[:, c], raw[:, 2].rearrange("p k f -> p (k f)"), ACT.Copy).then_inc(s["dhi"], 1)

                def unit(q, n, slot, c, first=False):
                    c0, w = slices[n]
                    u = q * NS + n
                    i = (c * NS + n) % 2
                    act.wait_ge(s["unit"], u + 1)
                    if not first:
                        act.wait_ge(s["mul"], u - 1)
                    act.activation(sg[:, i, 0:w], gu[:, i, 0, 0:w], ACT.Silu).then_inc(s["silu"], 1)
                    act.wait_ge(s["mul"], u + 1)
                    act.activation(hH[:, slot, c, c0:c0 + w], hf[:, i, 0:w], ACT.Copy).then_inc(s["hh"], 1)

                def step(g, slot, first=False, final=False):
                    for c in range(2):
                        q = 2 * g + c
                        if not (final and c == 1):
                            split_gate_up(q + 1, (c + 1) % 2, wait_slot=not (first and c == 0))
                        if not first:
                            split_down(q - 2, c)
                        for n in range(NS):
                            unit(q, n, slot, c, first=first and c == 0 and n < 2)

                split_gate_up(0, 0, wait_slot=False)
                step(0, 0, first=True)
                with act.Fori(0, (NG - 3) // 2) as j:
                    step(2 * j + 1, 1)
                    step(2 * j + 2, 0)
                step(NG - 2, 1)
                step(NG - 1, 0, final=True)
                split_down(NQ - 2, 0)
                split_down(NQ - 1, 1)

            @block.vector
            def _(dve):
                def split_gate_up(q, slot):
                    dve.wait_ge(s["ghi"], q + 1)
                    dve.tensor_tensor(wL[:, slot, 0], raw[:, 0], wH[:, slot, 0].bitcast(f32), ALU.subtract).then_inc(s["glo"], 1)
                    dve.wait_ge(s["uhi"], q + 1)
                    dve.tensor_tensor(wL[:, slot, 1], raw[:, 1], wH[:, slot, 1].bitcast(f32), ALU.subtract).then_inc(s["ulo"], 1)

                def split_down(q, c):
                    dve.wait_ge(s["dhi"], q + 1)
                    dve.tensor_tensor(dL[:, c], raw[:, 2].rearrange("p k f -> p (k f)"), dH[:, c].bitcast(f32), ALU.subtract).then_inc(s["dlo"], 1)

                def unit(q, n, slot, c):
                    c0, w = slices[n]
                    u = q * NS + n
                    i = (c * NS + n) % 2
                    dve.wait_ge(s["silu"], u + 1)
                    dve.tensor_tensor(hf[:, i, 0:w], sg[:, i, 0:w], gu[:, i, 1, 0:w], ALU.mult).then_inc(s["mul"], 1)
                    dve.wait_ge(s["hh"], u + 1)
                    dve.tensor_tensor(hL[:, slot, c, c0:c0 + w], hf[:, i, 0:w], hH[:, slot, c, c0:c0 + w].bitcast(f32), ALU.subtract).then_inc(s["hl"], 1)

                def adds(g, par):
                    for i in range(ND):
                        t, half = i // 2, i % 2
                        r = tiles[t][1]
                        y = b.Y[0:r, t, 512 * half:512 * (half + 1)]
                        dve.wait_ge(s["down"], g * ND + i + 1)
                        dve.wait_ge(s["acc"], g * ND + i + 1)
                        dve.tensor_tensor(y, dn[0:r, (par * ND + i) % 4], y, ALU.add).then_inc(s["acc"], 1)

                def step(g, slot, first=False, final=False):
                    for c in range(2):
                        q = 2 * g + c
                        if not (final and c == 1):
                            split_gate_up(q + 1, (c + 1) % 2)
                        if not first:
                            split_down(q - 2, c)
                        for n in range(NS):
                            unit(q, n, slot, c)
                    if not first:
                        adds(g - 1, 1 - slot)

                split_gate_up(0, 0)
                dve.wait_ge(s["zero"], 1)
                dve.sem_inc(s["acc"], ND)
                step(0, 0, first=True)
                with dve.Fori(0, (NG - 3) // 2) as j:
                    step(2 * j + 1, 1)
                    step(2 * j + 2, 0)
                step(NG - 2, 1)
                step(NG - 1, 0, final=True)
                split_down(NQ - 2, 0)
                split_down(NQ - 1, 1)
                adds(NG - 1, 0)

            @block.tensor
            def _(pe):
                def gate_up(g, slot, first=False):
                    for c in range(2):
                        q = 2 * g + c
                        pe.wait_ge(s["ulo"], q + 1)
                        for n, (c0, w) in enumerate(slices):
                            i = (c * NS + n) % 2
                            u = q * NS + n
                            if not (first and c == 0 and n < 2):
                                pe.wait_ge(s["mul"], u - 1)
                            for j in range(2):
                                o = gu[:, i, j, 0:w]
                                for k in range(KC):
                                    xh, xl = b.XH[:, k, c0:c0 + w], b.XL[:, k, c0:c0 + w]
                                    pe.matmul(o, wH[:, c, j, k], xh, start=(k == 0), stop=False)
                                    pe.matmul(o, wH[:, c, j, k], xl, start=False, stop=False)
                                    last = pe.matmul(o, wL[:, c, j, k], xh, start=False, stop=(k == KC - 1))
                            last.then_inc(s["unit"], 1)

                def down(g, slot):
                    pe.wait_ge(s["dlo"], 2 * g + 2)
                    pe.wait_ge(s["hl"], (2 * g + 2) * NS)
                    for i in range(ND):
                        t, half = i // 2, i % 2
                        t0, r = tiles[t]
                        o = dn[0:r, (slot * ND + i) % 4]
                        pe.wait_ge(s["acc"], (g + 1) * ND + i - 3)
                        for c in range(2):
                            hh, hl = hH[:, slot, c, t0:t0 + r], hL[:, slot, c, t0:t0 + r]
                            wh, wl = (w[:, c, 512 * half:512 * (half + 1)] for w in (dH, dL))
                            pe.matmul(o, hh, wh, start=(c == 0), stop=False)
                            pe.matmul(o, hh, wl, start=False, stop=False)
                            last = pe.matmul(o, hl, wh, start=False, stop=(c == 1))
                        last.then_inc(s["down"], 1)

                gate_up(0, 0, first=True)
                with pe.Fori(0, (NG - 3) // 2) as j:
                    gate_up(2 * j + 1, 1)
                    down(2 * j, 0)
                    gate_up(2 * j + 2, 0)
                    down(2 * j + 1, 1)
                gate_up(NG - 2, 1)
                down(NG - 3, 0)
                gate_up(NG - 1, 0)
                down(NG - 2, 1)
                down(NG - 1, 0)


class Guest:

    def sync(self, sp, m):
        pass

    def gpsimd(self, pool):
        pass

    def scalar(self, act):
        pass

    def vector(self, dve, m):
        pass

    def tensor(self, pe, m):
        pass


def project_features(b, name, chunks, small, evac_act, evac_dve=None, raws=3, guests=()):
    M = len(chunks)
    units = [(m, n, c0, w) for m in range(M) for n, (c0, w) in enumerate(chunks[m][1])]
    of = [[u for u in range(len(units)) if units[u][0] == m] for m in range(M)]
    gained = [0]
    for _, _, gain in chunks:
        gained.append(gained[-1] + (gain is not None))
    with b.stage() as ctx:
        raw = b.sb(ctx, name + "raw", [P, raws, KC, P])
        wH = b.sb(ctx, name + "wH", [P, 2, KC, P], f32r)
        wL = b.sb(ctx, name + "wL", [P, 2, KC, P], f32r)
        pr = b.ps(ctx, name + "pr", [P, 4, 512])
        s = {n: b.sem(ctx, name + n) for n in ("r0", "r1", "r2", "small", "gained", "hi", "lo", "unit", "act", "dve")}
        with b.nc.Block() as block:
            @block.sync
            def _(sp):
                for dst, src in small:
                    sp.dma_start(dst, src).then_inc(s["small"], 16)
                for m in range(M):
                    if m >= raws:
                        sp.wait_ge(s["lo"], m - raws + 1)
                    sp.dma_start(raw[:, m % raws], chunks[m][0]).then_inc(s[f"r{m % raws}"], 16)
                    for guest in guests:
                        guest.sync(sp, m)
                for guest in guests:
                    guest.sync(sp, M)

            @block.gpsimd
            def _(pool):
                for guest in guests:
                    guest.gpsimd(pool)

            @block.scalar
            def _(act):
                act.wait_ge(s["small"], 16 * len(small))
                for guest in guests:
                    guest.scalar(act)

                def split(m):
                    act.wait_ge(s[f"r{m % raws}"], 16 * (m // raws + 1))
                    if chunks[m][2] is not None:
                        act.wait_ge(s["gained"], gained[m + 1])
                    if m >= 2:
                        act.wait_ge(s["unit"], of[m - 2][-1] + 1)
                    act.activation(wH[:, m % 2], raw[:, m % raws], ACT.Copy).then_inc(s["hi"], 1)
                split(0)
                for m in range(M):
                    if m + 1 < M:
                        split(m + 1)
                    for u in of[m]:
                        _, n, c0, w = units[u]
                        act.wait_ge(s["unit"], u + 1)
                        made = evac_act(act, m, n, c0, w, pr[:, u % 4, 0:w], s["dve"], u)
                        if made:
                            made.then_inc(s["act"], 1)
                        else:
                            act.sem_inc(s["act"], 1)

            @block.vector
            def _(dve):
                dve.wait_ge(s["small"], 16 * len(small))

                def gain(m):
                    if chunks[m][2] is not None:
                        g = chunks[m][2].rearrange("p (k o) -> p k o", o=1).broadcast_to([P, KC, P])
                        dve.wait_ge(s[f"r{m % raws}"], 16 * (m // raws + 1))
                        dve.tensor_tensor(raw[:, m % raws], raw[:, m % raws], g, ALU.mult).then_inc(s["gained"], 1)

                def split(m):
                    dve.wait_ge(s["hi"], m + 1)
                    dve.tensor_tensor(wL[:, m % 2], raw[:, m % raws], wH[:, m % 2].bitcast(f32), ALU.subtract).then_inc(s["lo"], 1)
                gain(0)
                gain(1)
                split(0)
                for m in range(M):
                    if m + 1 < M:
                        split(m + 1)
                    if m + 2 < M:
                        gain(m + 2)
                    for guest in guests:
                        guest.vector(dve, m)
                    if evac_dve:
                        for u in of[m]:
                            _, n, c0, w = units[u]
                            dve.wait_ge(s["act"], u + 1)
                            evac_dve(dve, m, n, c0, w, pr[:, u % 4, 0:w], s["dve"], u).then_inc(s["dve"], 1)
                for guest in guests:
                    guest.vector(dve, M)

            @block.tensor
            def _(pe):
                done = s["dve"] if evac_dve else s["act"]
                for m in range(M):
                    for guest in guests:
                        guest.tensor(pe, m)
                    pe.wait_ge(s["lo"], m + 1)
                    for u in of[m]:
                        _, n, c0, w = units[u]
                        if u >= 4:
                            pe.wait_ge(done, u - 3)
                        o = pr[:, u % 4, 0:w]
                        for k in range(KC):
                            xh, xl = b.XH[:, k, c0:c0 + w], b.XL[:, k, c0:c0 + w]
                            pe.matmul(o, wH[:, m % 2, k], xh, start=(k == 0), stop=False)
                            pe.matmul(o, wH[:, m % 2, k], xl, start=False, stop=False)
                            last = pe.matmul(o, wL[:, m % 2, k], xh, start=False, stop=(k == KC - 1))
                        last.then_inc(s["unit"], 1)
                for guest in guests:
                    guest.tensor(pe, M)


def project_tokens(b, name, weights, parts, small, evac, on_act=False, slots=2, raws=3, make_tail=None):
    LAG = 3
    with b.stage() as ctx:
        raw = b.sb(ctx, name + "raw", [P, raws, 2, 512])
        wH = b.sb(ctx, name + "wH", [P, slots, KC, 512], f32r)
        wL = b.sb(ctx, name + "wL", [P, slots, KC, 512], f32r)
        pr = b.ps(ctx, name + "pr", [P, 4, 512])
        s = {n: b.sem(ctx, name + n) for n in ("r0", "r1", "r2", "small", "hi", "lo", "unit", "out")}
        src = weights.rearrange("(k p) f -> p k f", p=P)
        tail = make_tail(ctx, lambda eng, t: eng.wait_ge(s["out"], (parts - 1) * NT + t + 1)) if make_tail else None
        NP = KC // 2
        with b.nc.Block() as block:
            @block.sync
            def _(sp):
                for i in range(parts * NP):
                    c, k = i // NP, 2 * (i % NP)
                    if i >= raws:
                        sp.wait_ge(s["lo"], i - raws + 1)
                    sp.dma_start(raw[:, i % raws], src[:, k:k + 2, 512 * c:512 * (c + 1)]).then_inc(s[f"r{i % raws}"], 16)
                    if i == 0:
                        for dst, a in small:
                            sp.dma_start(dst, a).then_inc(s["small"], 16)
                if tail:
                    tail.load_gains(sp)
                    tail.sync(sp)

            @block.gpsimd
            def _(pool):
                if tail:
                    tail.gpsimd(pool)

            @block.scalar
            def _(act):
                def split(c):
                    for i in range(c * NP, (c + 1) * NP):
                        k = 2 * (i % NP)
                        act.wait_ge(s[f"r{i % raws}"], 16 * (i // raws + 1))
                        if c >= slots:
                            act.wait_ge(s["unit"], NT * (c - slots + 1))
                        act.activation(wH[:, c % slots, k:k + 2], raw[:, i % raws], ACT.Copy).then_inc(s["hi"], 1)
                for c in range(slots):
                    split(c)
                act.wait_ge(s["small"], 16 * len(small))
                for c in range(parts):
                    if on_act:
                        for t in range(NT):
                            act.wait_ge(s["unit"], c * NT + t + 1)
                            evac(act, c, t, pr[:, (c * NT + t) % 4]).then_inc(s["out"], 1)
                    if c + slots < parts:
                        split(c + slots)
                if tail:
                    for k in range(NT + tail.STEPS):
                        tail.scalar(act, k)

            @block.vector
            def _(dve):
                def split(c):
                    for i in range(c * NP, (c + 1) * NP):
                        k = 2 * (i % NP)
                        dve.wait_ge(s["hi"], i + 1)
                        dve.tensor_tensor(wL[:, c % slots, k:k + 2], raw[:, i % raws], wH[:, c % slots, k:k + 2].bitcast(f32), ALU.subtract).then_inc(s["lo"], 1)
                for c in range(slots):
                    split(c)
                dve.wait_ge(s["small"], 16 * len(small))
                for c in range(parts):
                    if not on_act:
                        for t in range(NT):
                            u = c * NT + t
                            dve.wait_ge(s["unit"], u + 1)
                            evac(dve, c, t, pr[:, u % 4]).then_inc(s["out"], 1)
                            if tail and c == parts - 1:
                                tail.vector(dve, t)
                    if c + slots < parts:
                        split(c + slots)
                if tail:
                    for k in range(NT, NT + tail.STEPS):
                        tail.vector(dve, k)

            @block.tensor
            def _(pe):
                for c in range(parts):
                    for t in range(NT):
                        u = c * NT + t
                        if u >= 4:
                            pe.wait_ge(s["out"], u - 3)
                        o = pr[:, u % 4]
                        for k in range(KC):
                            if t == 0 and k % 2 == 0:
                                pe.wait_ge(s["lo"], c * NP + k // 2 + 1)
                            xh, xl = (x[:, k, P * t:P * (t + 1)] for x in (b.XH, b.XL))
                            pe.matmul(o, xh, wH[:, c % slots, k], start=(k == 0), stop=False)
                            pe.matmul(o, xh, wL[:, c % slots, k], start=False, stop=False)
                            last = pe.matmul(o, xl, wH[:, c % slots, k], start=False, stop=(k == KC - 1))
                        last.then_inc(s["unit"], 1)
                        if tail and c == parts - 1 and t >= LAG:
                            tail.tensor(pe, t - LAG)
                if tail:
                    for t in range(NT - LAG, NT):
                        tail.tensor(pe, t)


class BiasGuest(Guest):
    W = 3 * P

    def __init__(self, b, ctx, bias_rows, sinks):
        self.b, self.bias_rows, self.sinks = b, bias_rows, sinks
        self.table = b.nc.dram_tensor("bias_table", [HEADS, P, self.W], f32, kind="Internal").ap()
        self.rel = b.sb(ctx, "rel", [33, HEADS])
        self.hot = b.sb(ctx, "hot", [33, self.W])
        self.g = b.sb(ctx, "bias_by_offset", [HEADS, self.W])
        self.pb = b.ps(ctx, "pb", [HEADS, 512])
        self.s_in, self.s_neg, self.s_g, self.s_ge, self.s_out, self.s_read = (
            b.sem(ctx, n) for n in ("bias_in", "bias_neg", "bias_g", "bias_ge", "bias_out", "bias_read"))

    def sync(self, sp, m):
        ins, table = self.b.ins, self.table
        if m == 0:
            sp.dma_start(self.rel[0:32, :], ins["rel_bias"]).then_inc(self.s_in, 16)
            sp.dma_start(self.hot[:, :], ins["cst"][0:33, C_HOT:C_HOT + self.W]).then_inc(self.s_in, 16)
            sp.dma_start(self.sinks[:, :], rows_of(ins["sinks"][0])).then_inc(self.s_in, 16)
        if m == 3:
            sp.wait_ge(self.s_ge, 1)
            sp.dma_start(table, self.g[:, :].rearrange("h (o w) -> h o w", o=1).broadcast_to([HEADS, P, self.W])).then_inc(self.s_out, 16)
        if m == 7:
            sp.wait_ge(self.s_out, 16)
            skew = bass.AP(tensor=table.tensor, offset=P - 1, ap=[[self.W - 1, P], [P * self.W, HEADS], [1, 2 * P]])
            sp.dma_start(self.bias_rows[:, :, :], skew).then_inc(self.s_read, 16)
        if m > 7 and m == self.end:
            sp.wait_ge(self.s_read, 16)

    def gpsimd(self, pool):
        pool.memset(self.rel[32:33, :], NEG).then_inc(self.s_neg, 1)
        pool.wait_ge(self.s_neg, 1)

    def tensor(self, pe, m):
        if m == 1:
            pe.wait_ge(self.s_in, 48)
            pe.wait_ge(self.s_neg, 1)
            pe.matmul(self.pb[:, 0:self.W], self.rel[:, :], self.hot[:, :], start=True, stop=True).then_inc(self.s_g, 1)

    def vector(self, dve, m):
        if m == 1:
            dve.wait_ge(self.s_g, 1)
            dve.tensor_copy(self.g[:, :], self.pb[:, 0:self.W]).then_inc(self.s_ge, 1)


class AdaGuest(Guest):

    def __init__(self, b, ctx, rows, end):
        self.b, self.rows, self.end = b, rows, end
        Y = b.Y[:, :, :].rearrange("p t d -> p (t d)")
        self.acc = Y[:, 0:3 * D]
        self.w = [Y[:, 3 * D * (1 + i):3 * D * (2 + i)] for i in range(2)]
        self.cc = b.sb(ctx, "cc", [P, KC])
        self.cs = b.sb(ctx, "cs", [P, KC])
        self.ones = b.sb(ctx, "ada_ones", [P, 1])
        self.pm = b.ps(ctx, "ada_ps", [1, 2, 512])
        self.s = {n: b.sem(ctx, "ada_" + n) for n in ("c", "cs", "zero", "bias", "w0", "w1", "sum", "mm", "row", "out")}

    def sync(self, sp, m):
        ins, s = self.b.ins, self.s
        if m == 0:
            sp.dma_start(self.cc[:, :], ins["c_2"]).then_inc(s["c"], 16)
        if m == 1:
            sp.wait_ge(s["zero"], 1)
            sp.dma_start(self.acc[0:1, :], ins["b_ada_2"].rearrange("(a n) -> a n", a=1)).then_inc(s["bias"], 16)
        if 1 <= m <= KC:
            k = m - 1
            if k >= 2:
                sp.wait_ge(s["sum"], k - 1)
            sp.dma_start(self.w[k % 2], ins["w_ada_2"][P * k:P * (k + 1), :]).then_inc(s[f"w{k % 2}"], 16)
        if m == self.end:
            sp.wait_ge(s["row"], 6)
            sp.dma_start(self.rows, self.w[0][0:1, :]).then_inc(s["out"], 16)
            sp.wait_ge(s["out"], 16)

    def gpsimd(self, pool):
        pool.memset(self.acc, 0.0).then_inc(self.s["zero"], 1)
        pool.memset(self.ones[:, :], 1.0).then_inc(self.s["zero"], 1)

    def scalar(self, act):
        act.wait_ge(self.s["c"], 16)
        act.activation(self.cs[:, :], self.cc[:, :], ACT.Silu).then_inc(self.s["cs"], 1)

    def vector(self, dve, m):
        s = self.s
        if 1 <= m <= KC:
            k = m - 1
            if k == 0:
                dve.wait_ge(s["cs"], 1)
                dve.wait_ge(s["bias"], 16)
            dve.wait_ge(s[f"w{k % 2}"], 16 * (k // 2 + 1))
            if k:
                dve.wait_ge(s["sum"], k)
            dve.scalar_tensor_tensor(self.acc, self.w[k % 2], self.cs[:, k:k + 1], self.acc, ALU.mult, ALU.add).then_inc(s["sum"], 1)
        if m == self.end:
            for c in range(6):
                dve.wait_ge(s["mm"], c + 1)
                dve.tensor_scalar(self.w[0][0:1, 512 * c:512 * (c + 1)], self.pm[:, c % 2], 1.0 if c // 2 == 1 else 0.0, None, ALU.add).then_inc(s["row"], 1)

    def tensor(self, pe, m):
        s = self.s
        if m == self.end:
            pe.wait_ge(s["zero"], 2)
            pe.wait_ge(s["sum"], KC)
            for c in range(6):
                if c >= 2:
                    pe.wait_ge(s["row"], c - 1)
                pe.matmul(self.pm[:, c % 2], self.ones[:, :], self.acc[:, 512 * c:512 * (c + 1)], start=True, stop=True).then_inc(s["mm"], 1)


class KeyValueGuest(Guest):

    def __init__(self, b, ctx, KT, VT, V):
        self.b, self.KT, self.VT, self.V = b, KT, VT, V
        self.tv = b.ps(ctx, "turned_values", [P, 4, P])
        self.kv = b.sem(ctx, "kv_made")
        self.s = {n: b.sem(ctx, "kv_" + n) for n in ("zero", "dup", "turned", "moved")}
        self.keys = 6

    def sync(self, sp, m):
        if m == 4:
            sp.wait_ge(self.kv, self.keys)
            sp.wait_ge(self.s["zero"], 3)
            sp.dma_start(self.KT[HD:P, 0, :], self.KT[0:HD, 0, :]).then_inc(self.s["dup"], 16)
            sp.dma_start(self.KT[0:HD, 1, :], self.KT[HD:P, 1, :]).then_inc(self.s["dup"], 16)
        if m == 8:
            sp.wait_ge(self.s["dup"], 32)

    def gpsimd(self, pool):
        zero = self.s["zero"]
        pool.memset(self.KT[0:HD, 0, 0:PAD], 0.0).then_inc(zero, 1)
        pool.wait_ge(zero, 1)
        pool.memset(self.KT[HD:P, 1, 0:PAD], 0.0).then_inc(zero, 1)
        pool.wait_ge(zero, 2)
        pool.memset(self.VT[:, 0:PAD], 0.0).then_inc(zero, 1)
        pool.wait_ge(zero, 3)

    def tensor(self, pe, m):
        if m == 4:
            pe.wait_ge(self.kv, self.keys + 3)
            pe.wait_ge(self.s["zero"], 3)
        if 4 <= m < 7:
            if m > 4:
                pe.wait_ge(self.s["moved"], m - 4)
            for i in range(3):
                t = 3 * (m - 4) + i
                last = pe.transpose(self.tv[:, i], self.VT[:, P * t:P * (t + 1)], self.b.ident[:, :])
            last.then_inc(self.s["turned"], 1)

    def vector(self, dve, m):
        if 4 <= m < 7:
            dve.wait_ge(self.s["turned"], m - 3)
            dve.tensor_copy(self.V[:, 3 * (m - 4):3 * (m - 3), :], self.tv[:, 0:3]).then_inc(self.s["moved"], 1)


def attention_stage(b, KT, V, QT, bias_rows, sinks):
    nc = b.nc
    NP = HEADS // 2
    order = list(range(1, NT)) + [0]
    with b.stage() as ctx:
        lg = b.sb(ctx, "logits", [P, 3, 2, 2 * P])
        pr = b.sb(ctx, "probs", [P, 4, 2, 2 * P])
        pT = b.sb(ctx, "probsT", [P, 2, 4, P])
        m, nm, dm, rsum, es, den, rden = (b.sb(ctx, "attn_" + n, [P, 4, 2]) for n in ("m", "nm", "dm", "rsum", "es", "den", "rden"))
        qk = b.ps(ctx, "qk", [P, 2, 2, 512])
        tp = b.ps(ctx, "attn_tp", [P, 2, 4, P])
        op = b.ps(ctx, "op", [P, 2, 512])
        s = {n: b.sem(ctx, "attn_" + n) for n in ("qk", "max", "nm", "dm", "exp", "es", "den", "rd", "pn", "tp", "pT", "pv", "xh", "xl", "mask")}
        U = NT * NP
        LAST = U + 4
        WARM = 4

        def unit(u):
            return order[u // NP], u % NP, (u % NP) // (NP // KVH)

        with nc.Block() as block:
            @block.tensor
            def _(pe):
                for k in range(LAST):
                    if k < U:
                        n, p, kvh = unit(k)
                        if k >= 2:
                            pe.wait_ge(s["max"], 2 * (k - 1))
                        for e in range(2):
                            last = pe.matmul(qk[:, k % 2, e, 0:2 * P], QT[HD * e:HD * (e + 1), p, P * n:P * (n + 1)],
                                             KT[HD * e:HD * (e + 1), kvh, P * n:P * (n + 2)], start=True, stop=True)
                        last.then_inc(s["qk"], 1)
                    if k == 1:
                        for i in range(WARM):
                            pe.matmul(op[:, i % 2], QT[:, 0, 0:P], QT[:, 1, 0:512], start=True, stop=True)
                    if 2 <= k < U + 2:
                        u = k - 2
                        pe.wait_ge(s["pn"], 2 * (u + 1))
                        if u >= 2:
                            pe.wait_ge(s["pT"], u - 1)
                        for e in range(2):
                            for j in range(2):
                                last = pe.transpose(tp[:, u % 2, 2 * e + j], pr[:, u % 4, e, P * j:P * (j + 1)], b.ident[:, :])
                        last.then_inc(s["tp"], 1)
                    if 3 <= k < U + 3:
                        u = k - 3
                        n, p, kvh = unit(u)
                        pe.wait_ge(s["pT"], u + 1)
                        if u >= 2:
                            pe.wait_ge(s["xl"], u - 1)
                        for e in range(2):
                            for j in range(2):
                                last = pe.matmul(op[HD * e:HD * (e + 1), u % 2, 0:P], V[:, n + j, HD * kvh:HD * (kvh + 1)], pT[:, u % 2, 2 * e + j],
                                                 start=(j == 0), stop=(j == 1))
                        last.then_inc(s["pv"], 1)

            @block.vector
            def _(dve):
                for k in range(LAST):
                    if k < U:
                        n, p, _ = unit(k)
                        i = k % 4
                        if k == U - NP:
                            dve.wait_ge(s["max"], 2 * k)
                            dve.memset(bias_rows[:, :, 0:PAD], NEG).then_inc(s["mask"], 1)
                            dve.wait_ge(s["mask"], 1)
                        dve.wait_ge(s["qk"], k + 1)
                        if k >= 3:
                            dve.wait_ge(s["exp"], 2 * (k - 2))
                        for e in range(2):
                            h = 2 * p + e
                            dve.tensor_tensor_reduce(out=lg[:, k % 3, e], in0=qk[:, k % 2, e, 0:2 * P], in1=bias_rows[:, h], scale=1.0, scalar=sinks[:, h:h + 1],
                                                     op0=ALU.add, op1=ALU.max, accum_out=m[:, i, e:e + 1]).then_inc(s["max"], 1)
                        dve.wait_ge(s["max"], 2 * (k + 1))
                        dve.tensor_scalar(nm[:, i], m[:, i], -1.0, None, ALU.mult).then_inc(s["nm"], 1)
                        dve.tensor_tensor(dm[:, i], sinks[:, 2 * p:2 * p + 2], m[:, i], ALU.subtract).then_inc(s["dm"], 1)
                    if 1 <= k < U + 1:
                        u = k - 1
                        i = u % 4
                        dve.wait_ge(s["es"], u + 1)
                        dve.tensor_tensor(den[:, i], es[:, i], rsum[:, i], ALU.add).then_inc(s["den"], 1)
                        dve.wait_ge(s["den"], u + 1)
                        dve.reciprocal(rden[:, i], den[:, i]).then_inc(s["rd"], 1)
                        dve.wait_ge(s["rd"], u + 1)
                        for e in range(2):
                            dve.tensor_scalar(pr[:, i, e], pr[:, i, e], rden[:, i, e:e + 1], None, ALU.mult).then_inc(s["pn"], 1)
                    if k >= 4:
                        u = k - 4
                        n, p, _ = unit(u)
                        dve.wait_ge(s["xh"], u + 1)
                        o = (slice(None), p, slice(P * n, P * (n + 1)))
                        dve.tensor_tensor(b.XL[o], op[:, u % 2, 0:P], b.XH[o].bitcast(f32), ALU.subtract).then_inc(s["xl"], 1)

            @block.scalar
            def _(act):
                for k in range(1, LAST):
                    if k < U + 1:
                        u = k - 1
                        i = u % 4
                        act.wait_ge(s["nm"], u + 1)
                        if u >= 4:
                            act.wait_ge(s["tp"], u - 3)
                        for e in range(2):
                            act.activation(pr[:, i, e], lg[:, u % 3, e], ACT.Exp, bias=nm[:, i, e:e + 1], accum_out=rsum[:, i, e:e + 1]).then_inc(s["exp"], 1)
                        act.wait_ge(s["dm"], u + 1)
                        act.wait_ge(s["exp"], 2 * (u + 1))
                        act.activation(es[:, i], dm[:, i], ACT.Exp).then_inc(s["es"], 1)
                    if 2 <= k < U + 2:
                        u = k - 2
                        act.wait_ge(s["tp"], u + 1)
                        if u >= 2:
                            act.wait_ge(s["pv"], u - 1)
                        act.activation(pT[:, u % 2], tp[:, u % 2], ACT.Copy).then_inc(s["pT"], 1)
                    if 3 <= k < U + 3:
                        u = k - 3
                        n, p, _ = unit(u)
                        act.wait_ge(s["pv"], u + 1)
                        act.activation(b.XH[:, p, P * n:P * (n + 1)], op[:, u % 2, 0:P], ACT.Copy).then_inc(s["xh"], 1)


def layer1_mixer(b, residual_in, residual_out, x1, ada_rows):
    ins = b.ins
    with b.stage() as ctx:
        KT = b.sb(ctx, "KT", [P, KVH, P * (NT + 1)])
        V = b.sb(ctx, "V", [P, NT + 1, P])

        def rows(src):
            return lambda t: src[TILES_META[t][0]:TILES_META[t][0] + TILES_META[t][1], :]
        post_stage(b, "p1", TILES_META, rows(residual_in), residual_out, ins["norm_ffn_post"][0],
                   cols=lambda t: slice(P * (t - 1), P * t) if t else slice(SEQ, TOK))
        QT = b.sb(ctx, "QT", [P, KC, SEQ])
        bias_rows = b.sb(ctx, "bias_rows", [P, HEADS, 2 * P])
        sinks = b.sb(ctx, "sinks_rows", [P, HEADS])
        with b.stage() as c2:
            VT = b.sb(c2, "VT", [P, P * (NT + 1)])
            bq = b.sb(c2, "bq", [P, KC])
            bq8 = b.sb(c2, "bq8", [P, KC])
            bk = b.sb(c2, "bk", [P, 1])
            bv = b.sb(c2, "bv", [P, 1])
            gq = b.sb(c2, "gains_q", [P, KC])
            gkv = b.sb(c2, "gains_kv", [P, KC])
            s_bq = b.sem(c2, "q_bias")
            all_tokens = SLICES_SEQ + [(SEQ, META)]
            chunks = [(ins["w_k"].rearrange("(k p) f -> p k f", p=P), all_tokens, gkv[:, :]),
                      (ins["w_v"].rearrange("(k p) f -> p k f", p=P), all_tokens, gkv[:, :])]
            chunks += [(ins["w_q"][0][m], SLICES_SEQ, gq[:, :]) for m in range(KC)]
            kvg = KeyValueGuest(b, c2, KT, VT, V)
            bias = BiasGuest(b, c2, bias_rows, sinks)
            bias.end = len(chunks)
            ada = AdaGuest(b, c2, ada_rows, len(chunks) - 1)

            def evac(act, m, n, c0, w, bank, _, u):
                cols = slice(P + c0, P + c0 + w) if c0 < SEQ else slice(PAD, P)
                if m == 0:
                    act.activation(KT[0:HD, 0, cols], bank[0:HD], ACT.Identity, bias=bk[0:HD]).then_inc(kvg.kv, 1)
                    act.activation(KT[HD:P, 1, cols], bank[HD:P], ACT.Identity, bias=bk[HD:P]).then_inc(kvg.kv, 1)
                    act.wait_ge(kvg.kv, 2 * n + 2)
                    return None
                if m == 1:
                    act.activation(VT[:, cols], bank, ACT.Identity, bias=bv[:, :]).then_inc(kvg.kv, 1)
                    act.wait_ge(kvg.kv, kvg.keys + n + 1)
                    return None
                if m == 2 and n == 0:
                    act.activation(bq8[:, :], bq[:, :], ACT.Copy, scale=HD ** -0.5).then_inc(s_bq, 1)
                    act.wait_ge(s_bq, 1)
                return act.activation(QT[:, m - 2, c0:c0 + w], bank, ACT.Identity, bias=bq8[:, m - 2:m - 1], scale=HD ** -0.5)
            small = [(bq[:, :], ins["b_q"]), (bk[:, :], ins["b_k"]), (bv[:, :], ins["b_v"]),
                     (gq[:, :], ins["gains_q"]), (gkv[:, :], ins["gains_kv"])]
            project_features(b, "w_q_", chunks, small, evac, guests=(kvg, bias, ada))
        attention_stage(b, KT, V, QT, bias_rows, sinks)
    with b.stage() as ctx:
        bo = b.sb(ctx, "bo", [P, D])
        project_tokens(b, "w_o_", ins["w_o"][0], 2, [(bo[:, :], rows_of(ins["b_o"][0]))],
                       lambda dve, c, t, bank: dve.tensor_tensor(b.Y[:, t, 512 * c:512 * (c + 1)], bank, bo[:, 512 * c:512 * (c + 1)], ALU.add),
                       raws=2, make_tail=lambda c2, ready: Tail(
                           b, c2, "p2", TILES_SEQ, lambda t: residual_out[META + P * t:META + P * (t + 1), :], x1,
                           ins["norm_mix_post"][1], ins["norm_ffn_pre"][1], ready=ready))


def gmlp_stage(b):
    nc, ins = b.nc, b.ins
    U = b.Y[:, 0:4].rearrange("p a (t f) -> p (a t) f", f=DA)
    V = b.Y[:, 4:8].rearrange("p a (t f) -> p (a t) f", f=DA)
    with ExitStack() as outer:
        G = b.sb(outer, "G", [P, NT, DA])

        def evac(act, c, t, bank):
            dst, f = ((U, ACT.Gelu_apprx_tanh), (V, ACT.Gelu_apprx_tanh), (G, ACT.Silu))[c]
            return act.activation(dst[:, t], bank, f)
        project_tokens(b, "w_in_a_", ins["w_in_2"], 3, [], evac, on_act=True, slots=1)
        with b.stage() as ctx:
            sq = b.sb(ctx, "sq", [P, NT, DA])
            gv = b.sb(ctx, "gv", [P, DA])
            bv = b.sb(ctx, "bv_ln", [P, DA])
            ws = b.sb(ctx, "ws", [P, GA, P])
            bs = b.sb(ctx, "bs", [P, GA])
            eps = b.sb(ctx, "ln_eps", [P, 1])
            st = b.sb(ctx, "ln_st", [P, 5, NT * GA])
            vm = b.ps(ctx, "vm", [P, 4, 512])
            s_in, s_mask, s_eps, s_sq, s_sd, s_vn, s_mm, s_o, s_ch = (b.sem(ctx, "gmlp_" + n) for n in ("in", "mask", "eps", "sq", "sd", "vn", "mm", "o", "chain"))
            grp = lambda x: x.rearrange("p t (g d) -> p (t g) d", d=HD)
            row = lambda x, i: x[:, i].rearrange("p (g o) -> p g o", o=1).broadcast_to([P, NT * GA, HD])
            with nc.Block() as block:
                @block.sync
                def _(sp):
                    sp.dma_start(gv[:, :], rows_of(ins["ln_v_g_2"].rearrange("g d -> (g d)"))).then_inc(s_in, 16)
                    sp.dma_start(bv[:, :], rows_of(ins["ln_v_b_2"].rearrange("g d -> (g d)"))).then_inc(s_in, 16)
                    sp.dma_start(ws[:, :, :], ins["w_spatial_2"]).then_inc(s_in, 16)
                    sp.dma_start(bs[:, :], ins["b_spatial_2"]).then_inc(s_in, 16)

                @block.gpsimd
                def _(pool):
                    pool.memset(eps[:, :], 1e-5).then_inc(s_eps, 1)
                    pool.wait_ge(s_in, 64)
                    pool.affine_select(out=ws[:, :, :], in_=ws[:, :, :], compare_op=ALU.is_ge, fill=0.0, base=0,
                                       pattern=[[0, GA], [1, P]], channel_multiplier=-1).then_inc(s_mask, 1)

                @block.scalar
                def _(act):
                    act.wait_ge(s_eps, 1)
                    act.wait_ge(s_ch, 3)
                    act.activation(sq[:, :, :], V, ACT.Square).then_inc(s_sq, 1)
                    act.wait_ge(s_ch, 4)
                    act.activation(st[:, 3], st[:, 2], ACT.Sqrt, bias=eps[:, :], scale=1.0 / HD).then_inc(s_sd, 1)

                @block.vector
                def _(dve):
                    link = linker(dve, s_ch)
                    link(dve.reduce_sum(st[:, 0], grp(V), axis=mybir.AxisListType.X))
                    link(dve.tensor_scalar(st[:, 1], st[:, 0], 1.0 / HD, None, ALU.mult))
                    link(dve.tensor_tensor(grp(V), grp(V), row(st, 1), ALU.subtract))
                    dve.wait_ge(s_sq, 1)
                    link(dve.reduce_sum(st[:, 2], grp(sq[:, :, :]), axis=mybir.AxisListType.X))
                    dve.wait_ge(s_sd, 1)
                    link(dve.reciprocal(st[:, 4], st[:, 3]))
                    link(dve.tensor_tensor(grp(V), grp(V), row(st, 4), ALU.mult))
                    dve.wait_ge(s_in, 64)
                    tiles = lambda x: x[:, :].rearrange("p (o f) -> p o f", o=1).broadcast_to([P, NT, DA])
                    link(dve.tensor_tensor(V, V, tiles(gv), ALU.mult))
                    dve.tensor_tensor(V, V, tiles(bv), ALU.add).then_inc(s_vn, 1)
                    for g in range(GA):
                        u = U[:, :, HD * g:HD * (g + 1)]
                        dve.wait_ge(s_mm, g + 1)
                        dve.scalar_tensor_tensor(u, vm[:, g % 4].rearrange("p (t d) -> p t d", d=HD), bs[:, g:g + 1], u, ALU.add, ALU.mult).then_inc(s_o, 1)
                    dve.wait_ge(s_o, GA)
                    link(dve.tensor_tensor(U, U, G[:, :, :], ALU.mult))

                @block.tensor
                def _(pe):
                    pe.wait_ge(s_mask, 1)
                    pe.wait_ge(s_vn, 1)
                    for g in range(GA):
                        if g >= 4:
                            pe.wait_ge(s_o, g - 3)
                        pe.matmul(vm[:, g % 4], ws[:, g], V[:, :, HD * g:HD * (g + 1)], start=True, stop=True).then_inc(s_mm, 1)


def recurrent_inputs(b, PB):
    ins = b.ins
    with b.stage() as ctx:
        W = SEQ + 1
        shifted = b.sb(ctx, "shifted", [P, 2, W])
        diff = b.sb(ctx, "diff", [P, 2, 512])
        mu = b.sb(ctx, "mu", [P, NB])
        s_zero, s_diff = b.sem(ctx, "shift_zero"), b.sem(ctx, "shift_diff")
        started = []

        def evac_act(act, m, n, c0, w, bank, s_dve, u):
            if not started:
                started.append(1)
                act.activation(shifted[:, :, 0:1], mu[:, 0:2].rearrange("p (a o) -> p a o", o=1), ACT.Copy, scale=0.0).then_inc(s_zero, 1)
            if m >= 2:
                act.wait_ge(s_dve, 2 * (m - 1))
            return act.activation(shifted[:, m % 2, 1 + c0:1 + c0 + w], bank, ACT.Copy)

        def evac_dve(dve, m, n, c0, w, bank, s_dve, u):
            if m == 0 and n == 0:
                dve.wait_ge(s_zero, 1)
            now, before = shifted[:, m % 2, 1 + c0:1 + c0 + w], shifted[:, m % 2, c0:c0 + w]
            if u >= 2:
                dve.wait_ge(s_dve, u - 1)
            dve.tensor_tensor(diff[:, u % 2, 0:w], before, now, ALU.subtract).then_inc(s_diff, 1)
            dve.wait_ge(s_diff, 2 * m + n + 1)
            return dve.scalar_tensor_tensor(PB[:, m, c0:c0 + w], diff[:, u % 2, 0:w], mu[:, m:m + 1], now, ALU.mult, ALU.add)
        project_features(b, "w_in_b_", [(ins["w_in_b_2"][m], SLICES_SEQ, None) for m in range(NB)], [(mu[:, :], ins["mu_b_2"])], evac_act, evac_dve, raws=2)


def recurrent_gates(b, PB, kk, ab, bv, lw):
    nc, ins = b.nc, b.ins
    r, k, v, gate = (PB[:, 4 * i:4 * i + 4] for i in range(4))
    with b.stage() as ctx:
        th = b.sb(ctx, "th", [HD + 1, SEQ])
        wup = b.sb(ctx, "wup", [HD + 1, DA])
        aup = b.sb(ctx, "aup", [P, DA])
        cols = b.sb(ctx, "gate_cols", [P, 5, 4])
        blk = b.sb(ctx, "blk", [P, P])
        eps = b.sb(ctx, "kk_eps", [P, 1])
        sq = b.sb(ctx, "kk_sq", [P, 4, SEQ])
        pp = b.ps(ctx, "gates_ps", [P, 4, 512])
        n_ = {n: b.sem(ctx, "gates_" + n) for n in ("in", "const", "th", "z", "kk", "sq", "sd", "rk", "mm", "act", "dve", "chain", "gate")}
        SL = 2

        def sl(u):
            return u // SL, slice(512 * (u % SL), 512 * (u % SL + 1))
        with nc.Block() as block:
            @block.sync
            def _(sp):
                for i, n in enumerate(("a0_2", "k_k_2", "k_a_2", "r_k_2")):
                    sp.dma_start(cols[:, i], ins[n]).then_inc(n_["in"], 16)
                sp.dma_start(wup[0:HD, :], ins["w_up_2"]).then_inc(n_["in"], 16)
                sp.dma_start(wup[HD:HD + 1, :], ins["w0_2"].rearrange("(a n) -> a n", a=1)).then_inc(n_["in"], 16)
                sp.dma_start(aup[HD:P, :], ins["a_up_2"]).then_inc(n_["in"], 16)
                sp.dma_start(blk[:, :], ins["cst"][:, C_BLK:C_BLK + P]).then_inc(n_["in"], 16)

            @block.gpsimd
            def _(pool):
                pool.memset(th[HD:HD + 1, :], 1.0).then_inc(n_["const"], 1)
                pool.wait_ge(n_["const"], 1)
                pool.memset(eps[:, :], 1e-12).then_inc(n_["const"], 1)

            @block.scalar
            def _(act):
                act.wait_ge(n_["in"], 128)
                act.wait_ge(n_["const"], 2)
                act.activation(th[0:HD, :], PB[0:HD, 16], ACT.Tanh).then_inc(n_["th"], 1)
                for t in range(NT):
                    act.wait_ge(n_["mm"], t + 1)
                    act.activation(lw[:, t], pp[:, t % 4], ACT.Sigmoid).then_inc(n_["act"], 1)
                for u in range(8):
                    c, s = sl(u)
                    act.wait_ge(n_["mm"], 8 + u + 1)
                    act.activation(ab[:, c, s], pp[:, u % 4], ACT.Sigmoid, bias=cols[:, 0, c:c + 1]).then_inc(n_["act"], 1)
                for c in range(4):
                    act.wait_ge(n_["kk"], c + 1)
                    act.activation(sq[:, c], kk[:, c], ACT.Square).then_inc(n_["sq"], 1)
                act.activation(gate, gate, ACT.Silu).then_inc(n_["gate"], 1)
                for u in range(8):
                    c, s = sl(u)
                    act.wait_ge(n_["mm"], 16 + u + 1)
                    act.activation(bv[:, c, s], pp[:, u % 4], ACT.Sqrt, bias=eps[:, :]).then_inc(n_["act"], 1)

            @block.vector
            def _(dve):
                link = linker(dve, n_["chain"])
                dve.wait_ge(n_["in"], 128)
                for c in range(4):
                    dve.tensor_scalar(kk[:, c], k[:, c], cols[:, 1, c:c + 1], None, ALU.mult).then_inc(n_["kk"], 1)
                link(dve.tensor_scalar(cols[:, 4], cols[:, 2], -1.0, 1.0, ALU.mult, ALU.add))
                for u in range(8):
                    c, s = sl(u)
                    dve.wait_ge(n_["act"], 16 + u + 1)
                    link(dve.reciprocal(bv[:, c, s], bv[:, c, s]))
                    if u == 0:
                        dve.wait_ge(n_["kk"], 4)
                    link(dve.tensor_tensor(kk[:, c, s], kk[:, c, s], bv[:, c, s], ALU.mult))
                for c in range(4):
                    link(dve.tensor_scalar(sq[:, c], ab[:, c], cols[:, 2, c:c + 1], cols[:, 4, c:c + 1], ALU.mult, ALU.add))
                    link(dve.tensor_tensor(k[:, c], k[:, c], sq[:, c], ALU.mult))
                    link(dve.scalar_tensor_tensor(ab[:, c], ab[:, c], -1.0, kk[:, c], ALU.mult, ALU.mult))
                    dve.scalar_tensor_tensor(sq[:, c], r[:, c], cols[:, 3, c:c + 1], k[:, c], ALU.mult, ALU.mult).then_inc(n_["rk"], 1)
                for u in range(8):
                    c, s = sl(u)
                    dve.wait_ge(n_["mm"], 24 + u + 1)
                    dve.tensor_tensor(bv[:, c, s], pp[:, u % 4], v[:, c, s], ALU.mult).then_inc(n_["dve"], 1)

            @block.tensor
            def _(pe):
                pe.wait_ge(n_["in"], 128)
                pe.wait_ge(n_["th"], 1)
                for u in range(32):
                    if 4 <= u < 28:
                        pe.wait_ge(n_["act"], u - 3)
                    elif u >= 28:
                        pe.wait_ge(n_["dve"], u - 27)
                    o = pp[:, u % 4]
                    if u < 8:
                        mm = pe.matmul(o, th[:, P * u:P * (u + 1)], wup[:, :], start=True, stop=True)
                    elif u < 16:
                        c, s = sl(u - 8)
                        mm = pe.matmul(o, aup[HD:P, P * c:P * (c + 1)], PB[HD:P, 16, s], start=True, stop=True)
                    elif u < 24:
                        c, s = sl(u - 16)
                        pe.wait_ge(n_["sq"], c + 1)
                        mm = pe.matmul(o, blk[:, :], sq[:, c, s], start=True, stop=True)
                    else:
                        c, s = sl(u - 24)
                        pe.wait_ge(n_["rk"], c + 1)
                        mm = pe.matmul(o, blk[:, :], sq[:, c, s], start=True, stop=True)
                    mm.then_inc(n_["mm"], 1)


class Marks:

    def __init__(self, sem, names):
        self.sem, self.names, self.n = sem, names, 0

    def mark(self, ins, name):
        assert self.names[self.n % len(self.names)] == name, (self.names[self.n % len(self.names)], name)
        self.n += 1
        ins.then_inc(self.sem, 1)

    def wait(self, eng, t, name):
        if t >= 0:
            eng.wait_ge(self.sem, t * len(self.names) + self.names.index(name) + 1)


def recurrence_stage(b, PB, kk, ab, lw):
    nc, ins = b.nc, b.ins
    LV = 6
    r, k, v = (PB[:, 4 * i:4 * i + 4] for i in range(3))
    with b.stage() as ctx:
        tri = b.sb(ctx, "tri", [P, 2 * P])
        tris = b.sb(ctx, "tris", [P, 2 * P])
        lvl = b.sb(ctx, "lvl", [P, LV, P])
        ein = b.sb(ctx, "ein", [P, 2, 4, P])
        mid = b.sb(ctx, "mid", [P, 2, 4, P])
        ta = b.sb(ctx, "ta", [P, DA])
        tb = b.sb(ctx, "tb", [P, 2, DA]); tk = b.sb(ctx, "tk_tok", [P, 2, DA]); tv = b.sb(ctx, "tv", [P, 2, DA])
        LT = b.sb(ctx, "LT", [P, 2, 4, P]); AK = b.sb(ctx, "AK", [P, 2, 4, P])
        RB = b.sb(ctx, "RB", [P, 2, 4, P]); RK = b.sb(ctx, "RK", [P, 2, 4, P])
        Xi = b.sb(ctx, "Xi", [P, 2, 4, P]); XT = b.sb(ctx, "XT", [P, 2, 4, P])
        Uo = b.sb(ctx, "Uo", [P, 2, 4, P])
        MV = b.sb(ctx, "MV", [P, DA])
        WT = b.sb(ctx, "WT", [P, 2, 4, P]); UU = b.sb(ctx, "UU", [P, 2, DA])
        SA = b.sb(ctx, "SA", [P, DA])
        S = b.sb(ctx, "S", [P, 4, P])
        Sx = b.sb(ctx, "Sx", [P, 4, HD])
        inv = b.ps(ctx, "inv_ps", [P, 4, 512])
        wk = b.ps(ctx, "work_ps", [P, 2, 512])
        ch = b.ps(ctx, "chain_ps", [P, 512])
        yp = b.ps(ctx, "y_ps", [P, 512])
        s_in, s_c = b.sem(ctx, "rec_in"), b.sem(ctx, "rec_const")
        levels = range(1, LV)
        last = LV - 1

        def of_level(l):
            return ["xt"] if l == last else ["x", "xt"]

        def marks(name, names):
            return Marks(b.sem(ctx, "rec_" + name), names)

        pf = marks("pe", ["cum", "ta", "tb", "tk", "tv", "ab0", "ab1", "ak0", "ak1", "tx0", "tx1"]
                   + [n for l in levels for n in [f"p{l}0", f"p{l}1"] + [f"{x}{l}{e}" for e in range(2) for x in of_level(l)]]
                   + ["mv", "wt", "uu"])
        af = marks("act", ["ein", "eex", "eneg", "ta", "tb", "tk", "tv", "tx0", "tx1"]
                   + [f"p{l}{e}" for l in levels for e in range(2)] + ["mv", "wt"])
        df = marks("dve", ["at", "bt", "kt", "rt", "ab0", "ab1", "ak0", "ak1"]
                   + [f"{x}{l}{e}" for l in levels for e in range(2) for x in of_level(l)] + ["uu"])
        of = marks("pool", ["m0", "i0", "m1", "i1"] + [f"u{l}{e}" for l in levels for e in range(2)])
        pc = marks("pe_chain", ["sa0", "rb0", "rb1", "st0", "rk0", "rk1", "sa1", "st1", "y"])
        ac = marks("act_chain", ["y"])
        dc = marks("dve_chain", ["sa0", "rb0", "rb1", "sx00", "sx01", "s00", "s01", "rk0", "rk1", "sa1", "sx10", "sx11", "s10", "s11"])

        def tok(t):
            return slice(P * t, P * (t + 1))

        def head(c, e):
            return slice(P * c + HD * e, P * c + HD * (e + 1))

        def rows(i):
            return slice(HD * i, HD * (i + 1))

        def four(m):
            return m.rearrange("p (o t) -> p o t", o=1).broadcast_to([P, 4, P])

        def by_four(bank):
            return bank.rearrange("p (c t) -> p c t", c=4)

        with nc.Block() as block:
            @block.sync
            def _(sp):
                sp.dma_start(tri[:, :], ins["cst"][:, C_TRIU:C_TRIU + 2 * P]).then_inc(s_in, 16)
                sp.dma_start(lvl[:, :, :], ins["cst"][:, C_LVL:C_LVL + LV * P].rearrange("p (l t) -> p l t", l=LV)).then_inc(s_in, 16)

            @block.gpsimd
            def _(pool):
                pool.memset(S[:, :, :], 0.0).then_inc(s_c, 1)
                pool.wait_ge(s_in, 32)
                pool.tensor_scalar(tris[:, :], tri[:, :], -0.6065306597126334, None, ALU.mult).then_inc(s_c, 1)
                for t in range(NT):
                    for e in range(2):
                        df.wait(pool, t, f"ab{e}")
                        pf.wait(pool, t - 1, "uu")
                        of.mark(pool.tensor_tensor(XT[:, e], LT[:, e], four(lvl[:, 0]), ALU.mult), f"m{e}")
                        of.wait(pool, t, f"m{e}")
                        of.mark(pool.tensor_tensor(XT[:, e], XT[:, e], four(b.ident[:, :]), ALU.add), f"i{e}")
                    for l in levels:
                        for e in range(2):
                            if l > 1:
                                pf.wait(pool, t, f"p{l - 1}{e}")
                            else:
                                pf.wait(pool, t - 1, f"p{last}{e}")
                            of.mark(pool.tensor_tensor(Uo[:, e], LT[:, e], four(lvl[:, l]), ALU.mult), f"u{l}{e}")

            @block.scalar
            def _(act):
                def chain(t, seg):
                    if seg == 5:
                        pc.wait(act, t, "y")
                        ac.mark(act.activation(r[:, :, tok(t)], by_four(yp[:, :]), ACT.Copy), "y")

                for t in range(NT):
                    cum = wk[:, :, :].rearrange("p a (c x) -> p (a c) x", c=2)
                    pf.wait(act, t, "cum")
                    dc.wait(act, t - 2, "s11")
                    af.mark(act.activation(ein[:, t % 2], cum[:, :, 0:P], ACT.Exp), "ein")
                    pf.wait(act, t - 1, f"xt{last}1")
                    af.mark(act.activation(mid[:, 0], cum[:, :, P:2 * P], ACT.Exp), "eex")
                    af.mark(act.activation(mid[:, 1], cum[:, :, 0:P], ACT.Exp, scale=-1.0), "eneg")
                    for n, dst, bank in (("ta", ta[:, :], 0), ("tb", tb[:, t % 2], 1), ("tk", tk[:, t % 2], 0), ("tv", tv[:, t % 2], 1)):
                        pf.wait(act, t, n)
                        if n == "ta":
                            pf.wait(act, t - 1, "wt")
                        else:
                            pc.wait(act, t - 2, "y")
                        af.mark(act.activation(dst, wk[:, bank], ACT.Copy), n)
                    for e in range(2):
                        pf.wait(act, t, f"tx{e}")
                        af.mark(act.activation(Xi[:, e], by_four(inv[:, e]), ACT.Copy), f"tx{e}")
                    for l in levels:
                        for e in range(2):
                            pf.wait(act, t, f"p{l}{e}")
                            if l == 1:
                                df.wait(act, t, "kt")
                            else:
                                pf.wait(act, t, f"xt{l - 1}{e}")
                            af.mark(act.activation(mid[:, e], by_four(inv[:, e]), ACT.Copy), f"p{l}{e}")
                        if t:
                            chain(t - 1, l)
                    pf.wait(act, t, "mv")
                    af.mark(act.activation(MV[:, :], wk[:, 0], ACT.Copy), "mv")
                    pf.wait(act, t, "wt")
                    pc.wait(act, t - 2, "sa1")
                    af.mark(act.activation(WT[:, t % 2], by_four(wk[:, 1]), ACT.Copy), "wt")
                for l in levels:
                    chain(NT - 1, l)

            @block.vector
            def _(dve):
                def chain(t, seg):
                    if seg in (1, 3):
                        q = seg // 2
                        pc.wait(dve, t, f"sa{q}")
                        df.wait(dve, t, "uu")
                        pc.wait(dve, t - 1, "y")
                        dc.mark(dve.tensor_tensor(SA[rows(q)], ch[rows(q)], UU[rows(q), t % 2], ALU.add), f"sa{q}")
                    if seg == 1:
                        for e in range(2):
                            pc.wait(dve, t, f"rb{e}")
                            dc.mark(dve.tensor_tensor(RB[:, e], by_four(wk[:, e]), four(tri[:, 0:P]), ALU.mult), f"rb{e}")
                    if seg in (2, 4):
                        q = seg // 2 - 1
                        pc.wait(dve, t, f"st{q}")
                        for e in range(2):
                            dc.mark(dve.tensor_tensor(Sx[rows(e)], S[rows(e), :, rows(e)], by_four(ch[:, :])[rows(e), :, rows(e)], ALU.add), f"sx{q}{e}")
                        for e in range(2):
                            dc.wait(dve, t, f"sx{q}{e}")
                            d = ein[rows(e), t % 2, :, HD * q + HD - 1:HD * q + HD].broadcast_to([HD, 4, HD])
                            dc.mark(dve.tensor_tensor(S[rows(e), :, rows(e)], Sx[rows(e)], d, ALU.mult), f"s{q}{e}")
                    if seg == 2:
                        for e in range(2):
                            pc.wait(dve, t, f"rk{e}")
                            dc.mark(dve.tensor_tensor(RK[:, e], by_four(wk[:, e]), four(tri[:, 0:P]), ALU.mult), f"rk{e}")

                dve.wait_ge(s_c, 2)
                for t in range(NT):
                    af.wait(dve, t, "eneg")
                    df.mark(dve.tensor_tensor(kk[:, :, tok(t)], kk[:, :, tok(t)], mid[:, 0], ALU.mult), "at")
                    df.mark(dve.tensor_tensor(ab[:, :, tok(t)], ab[:, :, tok(t)], mid[:, 1], ALU.mult), "bt")
                    df.mark(dve.tensor_tensor(k[:, :, tok(t)], k[:, :, tok(t)], mid[:, 1], ALU.mult), "kt")
                    df.mark(dve.tensor_tensor(r[:, :, tok(t)], r[:, :, tok(t)], ein[:, t % 2], ALU.mult), "rt")
                    for x, dst, bank in (("ab", LT, 0), ("ak", AK, 2)):
                        for e in range(2):
                            pf.wait(dve, t, f"{x}{e}")
                            if x == "ab":
                                of.wait(dve, t - 1, f"u{last}{e}")
                            df.mark(dve.tensor_tensor(dst[:, e], by_four(inv[:, bank + e]), four(tri[:, P:2 * P]), ALU.mult), f"{x}{e}")
                    for l in levels:
                        for e in range(2):
                            for x in of_level(l):
                                pf.wait(dve, t, f"{x}{l}{e}")
                                bank = (3, 2)[e] if l == last else (2 if x == "x" else 3)
                                m = Xi if x == "x" else XT
                                df.mark(dve.tensor_tensor(m[:, e], m[:, e], by_four(inv[:, bank]), ALU.add), f"{x}{l}{e}")
                        if t:
                            chain(t - 1, l)
                    pf.wait(dve, t, "uu")
                    df.mark(dve.tensor_copy(UU[:, t % 2], wk[:, 0]), "uu")
                for l in levels:
                    chain(NT - 1, l)

            @block.tensor
            def _(pe):
                def gram(bank, left, right, t, e):
                    for c in range(4):
                        mm = pe.matmul(bank[:, P * c:P * (c + 1)], left[rows(e), c, tok(t)], right[rows(e), c, tok(t)], start=True, stop=True)
                    return mm

                def chain(t, seg):
                    if seg in (1, 3):
                        q = seg // 2
                        af.wait(pe, t, "wt")
                        if q:
                            dc.wait(pe, t, "s01")
                        else:
                            dc.wait(pe, t - 1, "s11")
                            pe.wait_ge(s_c, 2)
                        for c in range(4):
                            mm = pe.matmul(ch[rows(q), P * c:P * (c + 1)], WT[:, t % 2, c, rows(q)], S[:, c], start=True, stop=True)
                        pc.mark(mm, f"sa{q}")
                    if seg in (2, 4):
                        q = seg // 2 - 1
                        if q == 0:
                            ac.wait(pe, t - 1, "y")
                        for c in range(4):
                            pe.matmul(yp[:, P * c + HD * q:P * c + HD * (q + 1)], S[:, c], r[:, c, P * t + HD * q:P * t + HD * (q + 1)],
                                      start=(q == 0 and c == 0), stop=False, skip_group_check=True)
                        dc.wait(pe, t, f"sa{q}")
                        for c in range(4):
                            o = ch[:, P * c:P * (c + 1)]
                            pe.matmul(o, tk[rows(q), t % 2, P * c:P * (c + 1)], tv[rows(q), t % 2, P * c:P * (c + 1)], start=True, stop=False)
                            mm = pe.matmul(o, tb[rows(q), t % 2, P * c:P * (c + 1)], SA[rows(q), P * c:P * (c + 1)], start=False, stop=True)
                        pc.mark(mm, f"st{q}")
                    if seg == 1:
                        for e in range(2):
                            if t + 1 < NT:
                                af.wait(pe, t + 1, ("tk", "tv")[e])
                            else:
                                af.wait(pe, t, "wt")
                                df.wait(pe, t, "uu")
                            pc.mark(gram(wk[:, e], ab, r, t, e), f"rb{e}")
                    if seg == 2:
                        for e in range(2):
                            dc.wait(pe, t, f"rb{e}")
                            pc.mark(gram(wk[:, e], k, r, t, e), f"rk{e}")
                    if seg == 5:
                        dc.wait(pe, t, "sa1")
                        dc.wait(pe, t, "rk1")
                        for c in range(4):
                            for e in range(2):
                                o = yp[rows(e), P * c:P * (c + 1)]
                                pe.matmul(o, SA[:, head(c, e)], RB[:, e, c], start=False, stop=False, skip_group_check=True)
                                mm = pe.matmul(o, tv[:, t % 2, head(c, e)], RK[:, e, c], start=False, stop=True, skip_group_check=True)
                        pc.mark(mm, "y")

                def four_of(name, e, bank, left, right):
                    for c in range(4):
                        mm = pe.matmul(inv[:, bank, P * c:P * (c + 1)], left[:, e, c], right[:, e, c], start=True, stop=True)
                    pf.mark(mm, name)

                pe.wait_ge(s_c, 2)
                for t in range(NT):
                    af.wait(pe, t - 1, "wt")
                    df.wait(pe, t - 1, "uu")
                    for c in range(4):
                        mm = pe.matmul(wk[:, c // 2, 2 * P * (c % 2):2 * P * (c % 2 + 1)], lw[:, t, P * c:P * (c + 1)], tris[:, :], start=True, stop=True)
                    pf.mark(mm, "cum")
                    af.wait(pe, t, "eneg")
                    for n, src, bank, ready, free in (("ta", kk, 0, "at", None), ("tb", ab, 1, "bt", None), ("tk", k, 0, "kt", "ta"), ("tv", v, 1, None, "tb")):
                        if ready:
                            df.wait(pe, t, ready)
                        if free:
                            af.wait(pe, t, free)
                        for c in range(4):
                            mm = pe.transpose(wk[:, bank, P * c:P * (c + 1)], src[:, c, tok(t)], b.ident[:, :])
                        pf.mark(mm, n)
                    for x, left, bank in (("ab", ab, 0), ("ak", k, 2)):
                        for e in range(2):
                            if x == "ab":
                                af.wait(pe, t - 1, f"p{last}{e}")
                            else:
                                df.wait(pe, t - 1, f"xt{last}{1 - e}")
                            pf.mark(gram(inv[:, bank + e], left, kk, t, e), f"{x}{e}")
                    for e in range(2):
                        of.wait(pe, t, f"i{e}")
                        for c in range(4):
                            mm = pe.transpose(inv[:, e, P * c:P * (c + 1)], XT[:, e, c], b.ident[:, :])
                        pf.mark(mm, f"tx{e}")
                    for l in levels:
                        for e in range(2):
                            of.wait(pe, t, f"u{l}{e}")
                            if l == 1:
                                af.wait(pe, t, f"tx{e}")
                            else:
                                df.wait(pe, t, f"x{l - 1}{e}")
                                af.wait(pe, t, f"p{l - 1}{e}")
                            four_of(f"p{l}{e}", e, e, Uo, Xi)
                        for e in range(2):
                            af.wait(pe, t, f"p{l}{e}")
                            for x in of_level(l):
                                bank = (3, 2)[e] if l == last else (2 if x == "x" else 3)
                                if l == last:
                                    df.wait(pe, t, f"xt{l - 1}1" if e == 0 else f"x{l - 1}1")
                                elif e == 1:
                                    df.wait(pe, t, f"{x}{l}0")
                                elif l > 1:
                                    df.wait(pe, t, f"{x}{l - 1}1")
                                else:
                                    df.wait(pe, t, "ak0" if x == "x" else "ak1")
                                if l > 1:
                                    df.wait(pe, t, f"xt{l - 1}{e}")
                                if x == "x":
                                    four_of(f"x{l}{e}", e, bank, XT, mid)
                                else:
                                    four_of(f"xt{l}{e}", e, bank, mid, XT)
                        if t:
                            chain(t - 1, l)
                    df.wait(pe, t, "ak1")
                    dc.wait(pe, t - 1, "rk0")
                    for h in range(8):
                        mm = pe.matmul(wk[:, 0, HD * h:HD * (h + 1)], AK[:, h % 2, h // 2], tv[:, t % 2, HD * h:HD * (h + 1)], start=True, stop=True)
                    pf.mark(mm, "mv")
                    dc.wait(pe, t - 1, "rk1")
                    df.wait(pe, t, f"xt{last}1")
                    for c in range(4):
                        for e in range(2):
                            mm = pe.matmul(wk[rows(e), 1, P * c:P * (c + 1)], ta[:, head(c, e)], XT[:, e, c], start=True, stop=True)
                    pf.mark(mm, "wt")
                    af.wait(pe, t, "mv")
                    for h in range(8):
                        mm = pe.matmul(wk[:, 0, HD * h:HD * (h + 1)], XT[:, h % 2, h // 2], MV[:, HD * h:HD * (h + 1)], start=True, stop=True)
                    pf.mark(mm, "uu")
                for l in levels:
                    chain(NT - 1, l)


def recurrent_output(b, PB, bv):
    nc, ins = b.nc, b.ins
    y, gate = PB[:, 0:4], PB[:, 12:16]
    with b.stage() as ctx:
        blk = b.sb(ctx, "blk2", [P, P])
        eps = b.sb(ctx, "gn_eps", [P, 1])
        cols = b.sb(ctx, "gn_cols", [P, 2, 4])
        sq = b.sb(ctx, "gn_sq", [P, 2, 512])
        sd = b.sb(ctx, "gn_sd", [P, 2, 512])
        pp = b.ps(ctx, "gn_ps", [P, 2, 2, 512])
        s = {n: b.sem(ctx, "gn_" + n) for n in ("in", "eps", "mean", "yc", "sq", "var", "sd", "rs", "yn", "aff", "sum", "out")}
        U = 8

        def sl(u):
            return u // 2, slice(512 * (u % 2), 512 * (u % 2 + 1))
        with nc.Block() as block:
            @block.sync
            def _(sp):
                sp.dma_start(blk[:, :], ins["cst"][:, C_BLK:C_BLK + P]).then_inc(s["in"], 16)
                sp.dma_start(cols[:, 0], ins["gn_g_2"]).then_inc(s["in"], 16)
                sp.dma_start(cols[:, 1], ins["gn_b_2"]).then_inc(s["in"], 16)

            @block.gpsimd
            def _(pool):
                pool.memset(eps[:, :], 64e-5).then_inc(s["eps"], 1)

            @block.tensor
            def _(pe):
                pe.wait_ge(s["in"], 48)
                for i in range(U + 1):
                    if i < U:
                        c, t = sl(i)
                        if i >= 2:
                            pe.wait_ge(s["yc"], i - 1)
                        pe.matmul(pp[:, i % 2, 0], blk[:, :], y[:, c, t], start=True, stop=True).then_inc(s["mean"], 1)
                    if i >= 1:
                        u = i - 1
                        pe.wait_ge(s["sq"], u + 1)
                        if u >= 2:
                            pe.wait_ge(s["sd"], u - 1)
                        pe.matmul(pp[:, u % 2, 1], blk[:, :], sq[:, u % 2], start=True, stop=True).then_inc(s["var"], 1)

            @block.scalar
            def _(act):
                act.wait_ge(s["eps"], 1)
                act.wait_ge(s["in"], 48)
                for i in range(U + 2):
                    if i < U:
                        c, t = sl(i)
                        act.wait_ge(s["yc"], i + 1)
                        if i >= 2:
                            act.wait_ge(s["var"], i - 1)
                        act.activation(sq[:, i % 2], y[:, c, t], ACT.Square).then_inc(s["sq"], 1)
                    if 1 <= i <= U:
                        u = i - 1
                        act.wait_ge(s["var"], u + 1)
                        if u >= 2:
                            act.wait_ge(s["yn"], u - 1)
                        act.activation(sd[:, u % 2], pp[:, u % 2, 1], ACT.Sqrt, bias=eps[:, :], scale=1.0 / HD).then_inc(s["sd"], 1)
                    if i >= 2:
                        u = i - 2
                        c, t = sl(u)
                        act.wait_ge(s["yn"], u + 1)
                        act.activation(y[:, c, t], y[:, c, t], ACT.Identity, bias=cols[:, 1, c:c + 1], scale=cols[:, 0, c:c + 1]).then_inc(s["aff"], 1)

            @block.vector
            def _(dve):
                for i in range(U + 3):
                    if i < U:
                        c, t = sl(i)
                        dve.wait_ge(s["mean"], i + 1)
                        dve.scalar_tensor_tensor(y[:, c, t], pp[:, i % 2, 0], -1.0 / HD, y[:, c, t], ALU.mult, ALU.add).then_inc(s["yc"], 1)
                    if 1 <= i <= U:
                        u = i - 1
                        c, t = sl(u)
                        dve.wait_ge(s["sd"], u + 1)
                        dve.reciprocal(sd[:, u % 2], sd[:, u % 2]).then_inc(s["rs"], 1)
                        dve.wait_ge(s["rs"], u + 1)
                        dve.tensor_tensor(y[:, c, t], y[:, c, t], sd[:, u % 2], ALU.mult).then_inc(s["yn"], 1)
                    if i >= 3:
                        u = i - 3
                        c, t = sl(u)
                        dve.wait_ge(s["aff"], u + 1)
                        dve.tensor_tensor(y[:, c, t], y[:, c, t], bv[:, c, t], ALU.add).then_inc(s["sum"], 1)
                        dve.wait_ge(s["sum"], u + 1)
                        dve.tensor_tensor(gate[:, c, t], gate[:, c, t], y[:, c, t], ALU.mult).then_inc(s["out"], 1)


def join_stage(b, PB, out_a):
    nc = b.nc
    gate = PB[:, 12:16]
    with b.stage() as ctx:
        a = b.sb(ctx, "out_a_in", [P, 2, DA])
        tp = b.ps(ctx, "join_tp", [P, 2, 4, P])
        s_a = [b.sem(ctx, f"join_a{i}") for i in range(2)]
        s_tp, s_h, s_l, s_gh, s_gl = (b.sem(ctx, "join_" + n) for n in ("tp", "h", "l", "gh", "gl"))
        with nc.Block() as block:
            @block.sync
            def _(sp):
                for t in range(NT):
                    if t >= 2:
                        sp.wait_ge(s_tp, t - 1)
                    sp.dma_start(a[:, t % 2], out_a[:, t]).then_inc(s_a[t % 2], 16)

            @block.tensor
            def _(pe):
                for t in range(NT):
                    pe.wait_ge(s_a[t % 2], 16 * (t // 2 + 1))
                    if t >= 2:
                        pe.wait_ge(s_l, t - 1)
                    for c in range(4):
                        mm = pe.transpose(tp[:, t % 2, c], a[:, t % 2, P * c:P * (c + 1)], b.ident[:, :])
                    mm.then_inc(s_tp, 1)

            @block.scalar
            def _(act):
                for t in range(NT):
                    if t % 2 == 0:
                        c = t // 2
                        act.activation(b.XH[:, 4 + c], gate[:, c], ACT.Copy).then_inc(s_gh, 1)
                    act.wait_ge(s_tp, t + 1)
                    act.activation(b.XH[:, 0:4, P * t:P * (t + 1)], tp[:, t % 2], ACT.Copy).then_inc(s_h, 1)

            @block.vector
            def _(dve):
                for t in range(NT):
                    if t % 2 == 0:
                        c = t // 2
                        dve.wait_ge(s_gh, c + 1)
                        dve.tensor_tensor(b.XL[:, 4 + c], gate[:, c], b.XH[:, 4 + c].bitcast(f32), ALU.subtract).then_inc(s_gl, 1)
                    dve.wait_ge(s_h, t + 1)
                    o = (slice(None), slice(0, 4), slice(P * t, P * (t + 1)))
                    dve.tensor_tensor(b.XL[o], tp[:, t % 2], b.XH[o].bitcast(f32), ALU.subtract).then_inc(s_l, 1)


class FinalTail:
    STEPS = 3
    ALPHA = 2 ** 0.25

    def __init__(self, b, ctx, x, out, ready):
        self.b, self.x, self.out, self.ready = b, x, out, ready
        self.rx = b.sb(ctx, "fin_x", [P, 2, D])
        self.z = b.sb(ctx, "fin_z", [P, 3, D])
        self.g = b.sb(ctx, "fin_g", [P, D])
        self.be = b.sb(ctx, "fin_b", [P, D])
        self.eps = b.sb(ctx, "fin_eps", [P, 1])
        self.st = b.sb(ctx, "fin_st", [P, NT, 2, 6])
        self.mv = b.sb(ctx, "fin_mv", [P, NT, 2])
        self.sd = b.sb(ctx, "fin_sd", [P, 3, NT])
        self.s = {n: b.sem(ctx, "fin_" + n) for n in ("x0", "x1", "gb", "eps", "z", "st", "mv", "sd", "rs", "shift", "c", "n", "o", "out")}

    def load_gains(self, sp):
        sp.dma_start(self.g[:, :], rows_of(self.b.ins["ln_g_2"])).then_inc(self.s["gb"], 16)
        sp.dma_start(self.be[:, :], rows_of(self.b.ins["ln_b_2"])).then_inc(self.s["gb"], 16)

    def sync(self, sp):
        s = self.s
        for t in range(NT + 3):
            if t < NT:
                if t >= 2:
                    sp.wait_ge(s["z"], t - 1)
                sp.dma_start(self.rx[:, t % 2], self.x[P * t:P * (t + 1), :]).then_inc(s[f"x{t % 2}"], 16)
            if t >= 3:
                u = t - 3
                sp.wait_ge(s["o"], u + 1)
                sp.dma_start(self.out[0, P * u:P * (u + 1), :], self.b.Y[:, u]).then_inc(s["out"], 16)
        sp.wait_ge(s["out"], 16 * NT)

    def gpsimd(self, pool):
        s, Y = self.s, self.b.Y
        pool.memset(self.eps[:, :], 1e-5).then_inc(s["eps"], 1)
        pool.wait_ge(s["gb"], 32)
        for t in range(NT):
            pool.wait_ge(s["n"], t + 1)
            pool.tensor_tensor(Y[:, t], Y[:, t], self.be[:, :], ALU.add).then_inc(s["o"], 1)

    def scalar(self, act, k):
        s = self.s
        if k == 0:
            act.wait_ge(s["eps"], 1)
        if k < NT:
            act.wait_ge(s["mv"], k + 1)
            act.activation(self.sd[:, 0, k:k + 1], self.mv[:, k, 1:2], ACT.Sqrt, bias=self.eps[:, :]).then_inc(s["sd"], 1)
        if 1 <= k < NT + 1:
            t = k - 1
            act.wait_ge(s["shift"], t + 1)
            act.activation(self.z[:, t % 3], self.z[:, t % 3], ACT.Identity, bias=self.sd[:, 2, t:t + 1], scale=self.sd[:, 1, t:t + 1]).then_inc(s["c"], 1)

    def vector(self, dve, k):
        s, z, sd = self.s, self.z, self.sd
        if k < NT:
            self.ready(dve, k)
            dve.wait_ge(s[f"x{k % 2}"], 16 * (k // 2 + 1))
            if k >= 3:
                dve.wait_ge(s["n"], k - 2)
            dve.scalar_tensor_tensor(z[:, k % 3], self.rx[:, k % 2], self.ALPHA, self.b.Y[:, k], ALU.mult, ALU.add).then_inc(s["z"], 1)
            dve.wait_ge(s["z"], k + 1)
            for h in range(2):
                dve.bn_stats(self.st[:, k, h], z[:, k % 3, 512 * h:512 * (h + 1)]).then_inc(s["st"], 1)
            dve.wait_ge(s["st"], 2 * k + 2)
            dve.bn_aggr(self.mv[:, k], self.st[:, k].rearrange("p a b -> p (a b)")).then_inc(s["mv"], 1)
        if 2 <= k < NT + 2:
            t = k - 2
            if t == 0:
                dve.wait_ge(s["gb"], 32)
            dve.wait_ge(s["c"], t + 1)
            dve.tensor_tensor(self.b.Y[:, t], z[:, t % 3], self.g[:, :], ALU.mult).then_inc(s["n"], 1)
        if k < NT:
            dve.wait_ge(s["sd"], k + 1)
            dve.reciprocal(sd[:, 1, k:k + 1], sd[:, 0, k:k + 1]).then_inc(s["rs"], 1)
            dve.wait_ge(s["rs"], k + 1)
            dve.scalar_tensor_tensor(sd[:, 2, k:k + 1], self.mv[:, k, 0:1], -1.0, sd[:, 1, k:k + 1], ALU.mult, ALU.mult).then_inc(s["shift"], 1)

    def tensor(self, pe, t):
        pass


def second_block(b, x3, x4, ada_rows):
    nc, ins = b.nc, b.ins
    shift, scale1, gate = (ada_rows[0, D * i:D * (i + 1)] for i in range(3))
    out_a = nc.dram_tensor("out_a", [P, NT, DA], f32, kind="Internal").ap()
    with ExitStack() as right:
        b.alloc_x(right, "b2", SEQ, "right")
        post_stage(b, "p3", TILES_SEQ, lambda t: x3[P * t:P * (t + 1), :], x4, ins["norm_ffn_post"][1], modulate=(scale1, shift))
        gmlp_stage(b)
        with b.stage() as ctx:
            s_a = b.sem(ctx, "out_a_kept")
            with nc.Block() as block:
                @block.sync
                def _(sp):
                    sp.dma_start(out_a, b.Y[:, 0:4].rearrange("p a (t f) -> p (a t) f", f=DA)).then_inc(s_a, 16)
                    sp.wait_ge(s_a, 16)
        left = ExitStack()
        PB = b.sb(left, "PB", [P, NB, SEQ])
        recurrent_inputs(b, PB)
    with ExitStack() as ctx:
        kk = b.sb(ctx, "kk", [P, 4, SEQ])
        ab = b.sb(ctx, "ab", [P, 4, SEQ])
        bv = b.Y[:, 0:4]
        lw = b.Y[:, 4:8].rearrange("p a (t f) -> p (a t) f", f=DA)
        recurrent_gates(b, PB, kk, ab, bv, lw)
        recurrence_stage(b, PB, kk, ab, lw)
        recurrent_output(b, PB, bv)
    with ExitStack() as right:
        b.alloc_x(right, "b3", SEQ, "right")
        join_stage(b, PB, out_a)
        left.close()
        gate_rows = b.Y[:, NT]
        project_tokens(b, "w_out_", ins["w_out_2"], 2, [(gate_rows, rows_of(gate))],
                       lambda dve, c, t, bank: dve.tensor_tensor(b.Y[:, t, 512 * c:512 * (c + 1)], bank, gate_rows[:, 512 * c:512 * (c + 1)], ALU.mult),
                       make_tail=lambda ctx, ready: FinalTail(b, ctx, x4, b.out, ready))


def program(nc, ins, out):
    with ExitStack() as ctx:
        b = Builder(nc, ctx, ins, out)
        meta, x = ins["meta_tokens"], ins["x"]
        with ExitStack() as first:
            b.alloc_x(first, "b1", TOK, "right")
            pool_stage(b)
            post_stage(b, "p0", TILES_META, lambda t: meta if t == 0 else x[0, P * (t - 1):P * t, :], b.res[0], ins["norm_mix_post"][0], ins["norm_ffn_pre"][0])
            ffn_stage(b, "f0", 0, TILES_META, SLICES_META)
            ada_rows = nc.dram_tensor("ada_rows", [1, 3 * D], f32, kind="Internal").ap()
            layer1_mixer(b, b.res[0], b.res[1], b.res[2], ada_rows)
            ffn_stage(b, "f1", 1, TILES_SEQ, SLICES_SEQ)
        second_block(b, b.res[2], b.res[3], ada_rows)


def kernel(**inputs):
    import concourse.bacc as bacc
    from concourse.bass_utils import run_bass_kernel_spmd

    nc = bacc.Bacc("TRN2", target_bir_lowering=False, num_devices=1)
    arrays = {f"in_{n}": a for n, a in lay_out(inputs).items()}
    ins = {n[3:]: nc.dram_tensor(n, a.shape, mybir.dt.from_np(a.dtype), kind="ExternalInput").ap() for n, a in arrays.items()}
    out = nc.dram_tensor("out", (1, SEQ, D), f32, kind="ExternalOutput").ap()
    program(nc, ins, out)
    r = run_bass_kernel_spmd(nc, [arrays], core_ids=[0])
    return r.results[0]["out"]
```

```python
import concourse.bass as bass
from concourse import mybir
from contextlib import ExitStack, contextmanager

f32 = mybir.dt.float32
f32r = mybir.dt.float32r
ALU = mybir.AluOpType
ACT = mybir.ActivationFunctionType

P = 128
D = 1024
KC = D // P
SEQ = 1024
META = 16
NT = SEQ // P
TOK = META + SEQ
FF = 2816
NQ = FF // P
EPS = 1e-6
POOLS = (2, 4, 8, 16)
HEADS = 16
KVH = 2
HD = 64
PAD = P - META
NEG = -1e30

TILES_META = [(0, META)] + [(META + P * i, P) for i in range(NT)]
TILES_SEQ = [(P * i, P) for i in range(NT)]
SLICES_META = [(0, 348), (348, 346), (694, 346)]
SLICES_SEQ = [(0, 512), (512, 512)]

C_ID = 0
C_BAND = C_ID + P
C_PREV = C_BAND + 4 * P
C_MBAND = C_PREV + 4 * META
C_MPREV = C_MBAND + 4 * META
C_HOT = C_MPREV + 4 * META
C_DIST = 3 * P - 1
C_TRIU = C_HOT + C_DIST + 1
C_TRIX = C_TRIU + P
C_BLK = C_TRIX + P
C_CAUS = C_BLK + P
C_LVL = C_CAUS + P
C_IND = C_LVL + 6 * P
C_BACK = C_IND + 4 * 8
C_END = C_BACK + 4 * P
CHUNK = 64
DA = 512
GA = DA // HD
COLS_A = 3 * DA
NB = 17


def constants():
    import math
    import numpy as np
    c = np.zeros((P, C_END), np.float32)
    i = np.arange(P)
    s, t = i[:, None], i[None, :]
    c[:, C_ID:C_ID + P] = np.eye(P)
    for g, w in enumerate(POOLS):
        c[:, C_BAND + g * P:C_BAND + (g + 1) * P] = ((t - s >= 0) & (t - s < w)) / w - (s == t)
        prev = ((t + P - s) < w) / w
        c[:, C_PREV + g * META:C_PREV + (g + 1) * META] = prev[:, :META]
        c[:META, C_MPREV + g * META:C_MPREV + (g + 1) * META] = prev[P - META:, :META]
        m = ((t - s >= 0) & (t - s < w)) / np.minimum(t + 1, w).astype(np.float32) - (s == t)
        c[:META, C_MBAND + g * META:C_MBAND + (g + 1) * META] = m[:META, :META]
    for u in range(C_DIST):
        d = 2 * P - 1 - u
        if 0 <= d < P:
            if d < 16:
                b = d
            else:
                b = min(31, 16 + int(np.float32(np.float32(math.log(np.float32(d) / np.float32(16.0))) / np.float32(math.log(8.0))) * np.float32(16)))
            c[b, C_HOT + u] = 1
        else:
            c[32, C_HOT + u] = 1
    same = (s // CHUNK) == (t // CHUNK)
    c[:, C_TRIU:C_TRIU + P] = (s <= t) & same
    c[:, C_TRIX:C_TRIX + P] = (s < t) & same
    c[:, C_BLK:C_BLK + P] = same
    c[:, C_CAUS:C_CAUS + P] = s <= t
    for l in range(6):
        m = 1 << l
        c[:, C_LVL + l * P:C_LVL + (l + 1) * P] = (s // (2 * m) == t // (2 * m)) & (s % (2 * m) < m) & (t % (2 * m) >= m)
    for f in range(4):
        heads = 2 * f + i[:, None] // HD == np.arange(8)[None, :]
        c[:, C_IND + 8 * f:C_IND + 8 * (f + 1)] = heads
        c[0:8, C_BACK + P * f:C_BACK + P * (f + 1)] = heads.T
    return c


def rows_of(vector, n=P):
    return vector.rearrange("(a n) -> a n", a=1).broadcast_to([n, vector.shape[0]])


def lay_out(inputs):
    import numpy as np
    a = {n: np.ascontiguousarray(v) for n, v in inputs.items()}
    for n in ("b_q", "b_k", "b_v"):
        a[n] = np.ascontiguousarray(a[n].reshape(-1, P).T)
    a["gains_q"] = np.ascontiguousarray(a["norm_mix_pre"][1].reshape(-1, P).T)
    a["gains_kv"] = np.ascontiguousarray(a["kv_norm"].reshape(-1, P).T)
    for n in ("w_gate_up", "w_q"):
        w = a[n]
        w = w.reshape(w.shape[0], KC, P, w.shape[2] // P, P)
        a[n] = np.ascontiguousarray(w.transpose(0, 3, 2, 1, 4))
    for n in ("c_2", "mu_b_2", "a0_2", "k_k_2", "k_a_2", "r_k_2", "gn_g_2", "gn_b_2"):
        a[n] = np.ascontiguousarray(a[n].reshape(-1, P).T)
    a["w_spatial_2"] = np.ascontiguousarray(a["w_spatial_2"].transpose(2, 0, 1))
    a["b_spatial_2"] = np.ascontiguousarray(a["b_spatial_2"].T)
    w = a["w_in_2"]
    a["w_in_2"] = np.ascontiguousarray(w[:, :COLS_A])
    a["w_in_b_2"] = np.ascontiguousarray(w[:, COLS_A:].reshape(KC, P, NB, P).transpose(2, 1, 0, 3))
    a["cst"] = constants()
    return a


class Builder:

    def __init__(self, nc, ctx, ins, out):
        self.nc, self.ctx, self.ins, self.out = nc, ctx, ins, out
        self.eps = self.sb(ctx, "eps", [P, 1])
        self.ident = self.sb(ctx, "identity", [P, P])
        self.scopes = []
        self.Y = self.sb(ctx, "Y", [P, NT + 1, D])
        self.res = [nc.dram_tensor(f"residual{i}", [TOK, D], f32, kind="Internal").ap() for i in range(4)]

    def sb(self, ctx, name, shape, dt=f32, side="left"):
        return ctx.enter_context(self.nc.sbuf_tensor(name, shape, dt, side=side))

    def ps(self, ctx, name, shape, dt=f32):
        return ctx.enter_context(self.nc.psum_tensor(name, shape, dt))

    def sem(self, ctx, name):
        handle = ctx.enter_context(self.nc.semaphore(name))
        self.scopes[-1].append(handle)
        return handle

    @contextmanager
    def stage(self):
        with ExitStack() as ctx:
            self.scopes.append([])
            yield ctx
            used = self.scopes.pop()
            if used:
                with self.nc.Block() as block:
                    @block.gpsimd
                    def _(pool):
                        for handle in used:
                            pool.sem_clear(handle)

    def alloc_x(self, ctx, name, tokens, side="left"):
        self.XH = self.sb(ctx, name + "XH", [P, KC, tokens], f32r, side)
        self.XL = self.sb(ctx, name + "XL", [P, KC, tokens], f32r, side)


def linker(eng, sem):
    n = [0]

    def link(ins):
        n[0] += 1
        ins.then_inc(sem, 1)
        eng.wait_ge(sem, n[0])
    return link


def pool_stage(b):
    nc, ins = b.nc, b.ins
    G = len(POOLS)
    with b.stage() as ctx:
        cst = b.sb(ctx, "pool_constants", [P, C_HOT])
        xin = b.sb(ctx, "xin", [P, 3, D])
        junk = b.sb(ctx, "sq_junk", [P, D])
        xn = b.sb(ctx, "xn", [P, 3, D])
        gpre = b.sb(ctx, "gpre", [P, D])
        scale = b.sb(ctx, "pool_scale_rows", [P, D])
        wraw = b.sb(ctx, "wraw", [P, 2 * G, 256])
        wH = b.sb(ctx, "wH", [P, 2 * G, 256], f32r)
        wL = b.sb(ctx, "wL", [P, 2 * G, 256], f32r)
        pH = b.sb(ctx, "pH", [P, 2, KC, P], f32r)
        pL = b.sb(ctx, "pL", [P, 2, KC, P], f32r)
        ss = b.sb(ctx, "ss", [P, 9]); sd = b.sb(ctx, "sd", [P, 9]); rs = b.sb(ctx, "rs", [P, 9])
        pt = b.ps(ctx, "pt", [P, 2, KC, P])
        mx = b.ps(ctx, "mx", [P, 2, D])
        loaded = [b.sem(ctx, f"pool_x{i}") for i in range(3)]
        s_cst, s_w, s_sc = b.sem(ctx, "pool_cst"), b.sem(ctx, "pool_w_in"), b.sem(ctx, "pool_sc")
        s_wh, s_wl, s_eps = b.sem(ctx, "pool_wh"), b.sem(ctx, "pool_wl"), b.sem(ctx, "pool_eps")
        s_ss, s_sd, s_r, s_xn = (b.sem(ctx, f"pool_{n}") for n in ("ss", "sd", "r", "xn"))
        s_pt, s_ph, s_pl, s_mx, s_y = (b.sem(ctx, f"pool_{n}") for n in ("pt", "ph", "pl", "mx", "y"))
        N = len(TILES_META)

        with nc.Block() as block:
            @block.sync
            def _(sp):
                for t, (_, r) in enumerate(TILES_META):
                    if t >= 3:
                        sp.wait_ge(s_xn, t - 2)
                    src = ins["meta_tokens"] if t == 0 else ins["x"][0, P * (t - 1):P * t, :]
                    sp.dma_start(xin[0:r, t % 3], src).then_inc(loaded[t % 3], 16)
                    if t == 0:
                        sp.dma_start(cst[:, :], ins["cst"][:, 0:C_HOT]).then_inc(s_cst, 16)
                        sp.dma_start(b.ident[:, :], ins["cst"][:, C_ID:C_ID + P]).then_inc(s_cst, 16)
                        sp.dma_start(gpre[:, :], rows_of(ins["norm_mix_pre"][0])).then_inc(s_cst, 16)
                        sp.dma_start(wraw[:, :, :], ins["pool_w"][0].rearrange("g (k p) d -> p (g k) d", p=P)).then_inc(s_w, 16)
                        sp.dma_start(scale[:, :], rows_of(ins["pool_scale"][0])).then_inc(s_sc, 16)

            @block.gpsimd
            def _(pool):
                pool.memset(b.eps[:, :], EPS).then_inc(s_eps, 1)

            @block.scalar
            def _(act):
                act.wait_ge(s_eps, 1)

                def square(t):
                    r = TILES_META[t][1]
                    act.wait_ge(loaded[t % 3], 16 * (t // 3 + 1))
                    act.activation(junk[0:r], xin[0:r, t % 3], ACT.Square, accum_out=ss[0:r, t:t + 1]).then_inc(s_ss, 1)
                    act.wait_ge(s_ss, t + 1)
                    act.activation(sd[0:r, t:t + 1], ss[0:r, t:t + 1], ACT.Sqrt, bias=b.eps[0:r], scale=1.0 / D).then_inc(s_sd, 1)

                for t in range(N + 1):
                    if t == 0:
                        square(0)
                    if t + 1 < N:
                        square(t + 1)
                    if t == 0:
                        act.wait_ge(s_w, 16)
                        act.activation(wH[:, :, :], wraw[:, :, :], ACT.Copy).then_inc(s_wh, 1)
                    if t >= 1:
                        k, r = t - 1, TILES_META[t - 1][1]
                        act.wait_ge(s_pt, k + 1)
                        if k >= 2:
                            act.wait_ge(s_mx, k - 1)
                        act.activation(pH[:, k % 2, :, 0:r], pt[:, k % 2, :, 0:r], ACT.Copy).then_inc(s_ph, 1)

            @block.vector
            def _(dve):
                dve.wait_ge(s_cst, 48)

                def norm(t):
                    r = TILES_META[t][1]
                    dve.wait_ge(s_sd, t + 1)
                    dve.reciprocal(rs[0:r, t:t + 1], sd[0:r, t:t + 1]).then_inc(s_r, 1)
                    dve.wait_ge(s_r, t + 1)
                    if t >= 3:
                        dve.wait_ge(s_pt, t - 1)
                    dve.scalar_tensor_tensor(xn[0:r, t % 3], xin[0:r, t % 3], rs[0:r, t:t + 1], gpre[0:r], ALU.mult, ALU.mult).then_inc(s_xn, 1)

                for t in range(N + 3):
                    if t == 0:
                        norm(0)
                        norm(1)
                    if t == 0:
                        dve.wait_ge(s_wh, 1)
                        dve.tensor_tensor(wL[:, :, :], wraw[:, :, :], wH[:, :, :].bitcast(f32), ALU.subtract).then_inc(s_wl, 1)
                        dve.wait_ge(s_sc, 16)
                    if 1 <= t <= N:
                        k, r = t - 1, TILES_META[t - 1][1]
                        dve.wait_ge(s_ph, k + 1)
                        dve.tensor_tensor(pL[:, k % 2, :, 0:r], pt[:, k % 2, :, 0:r], pH[:, k % 2, :, 0:r].bitcast(f32), ALU.subtract).then_inc(s_pl, 1)
                    if 1 <= t and t + 1 < N:
                        norm(t + 1)
                    if 2 <= t < N + 2:
                        k, r = t - 2, TILES_META[t - 2][1]
                        dve.wait_ge(s_mx, k + 1)
                        dve.tensor_tensor(b.Y[0:r, k], mx[0:r, k % 2], scale[0:r], ALU.mult).then_inc(s_y, 1)

            @block.tensor
            def _(pe):
                pe.wait_ge(s_cst, 48)
                for t in range(N + 1):
                    if t < N:
                        r = TILES_META[t][1]
                        pe.wait_ge(s_xn, t + 1)
                        if t >= 2:
                            pe.wait_ge(s_pl, t - 1)
                        for f in range(KC):
                            g = f // 2
                            band = cst[0:r, C_BAND + g * P:C_BAND + g * P + r] if t else cst[0:r, C_MBAND + g * META:C_MBAND + (g + 1) * META]
                            last = pe.matmul(pt[:, t % 2, f, 0:r], xn[0:r, t % 3, f * P:(f + 1) * P], band, start=True, stop=True, skip_group_check=True)
                            if t:
                                rp = TILES_META[t - 1][1]
                                c0 = C_PREV if t > 1 else C_MPREV
                                last = pe.matmul(pt[:, t % 2, f, 0:META], xn[0:rp, (t - 1) % 3, f * P:(f + 1) * P],
                                                 cst[0:rp, c0 + g * META:c0 + (g + 1) * META], start=False, stop=True, skip_group_check=True)
                        last.then_inc(s_pt, 1)
                    if t >= 1:
                        k, r = t - 1, TILES_META[t - 1][1]
                        pe.wait_ge(s_pl, k + 1)
                        pe.wait_ge(s_wl, 1)
                        if k >= 2:
                            pe.wait_ge(s_y, k - 1)
                        for g in range(G):
                            for i in range(2):
                                c = 2 * g + i
                                o = mx[0:r, k % 2, 256 * g:256 * (g + 1)]
                                pe.matmul(o, pH[:, k % 2, c, 0:r], wH[:, c], start=(i == 0), stop=False)
                                pe.matmul(o, pL[:, k % 2, c, 0:r], wH[:, c], start=False, stop=False)
                                last = pe.matmul(o, pH[:, k % 2, c, 0:r], wL[:, c], start=False, stop=(i == 1))
                        last.then_inc(s_mx, 1)


class Tail:

    STEPS = 5

    def __init__(self, b, ctx, name, tiles, residual, store, post_gain, pre_gain=None, modulate=None, cols=None,
                 ready=None, junk=None, loads=2, slots=2):
        self.b, self.tiles, self.residual, self.store = b, tiles, residual, store
        self.post_gain, self.pre_gain, self.modulate = post_gain, pre_gain, modulate
        self.loads, self.slots, self.N = loads, slots, len(tiles)
        self.cols = cols or (lambda t: slice(tiles[t][0], tiles[t][0] + tiles[t][1]))
        self.ready = ready or (lambda eng, t: None)
        self.rx = b.sb(ctx, name + "rx", [P, loads, D])
        self.junk = junk if junk is not None else b.sb(ctx, name + "junk", [P, D])
        self.xn = b.sb(ctx, name + "xn", [P, 2, D])
        self.gpost = b.sb(ctx, name + "gpost", [P, D])
        self.gpre = b.sb(ctx, name + "gpre", [P, D]) if pre_gain is not None else None
        self.scale = b.sb(ctx, name + "scale", [P, D]) if modulate else None
        self.shift = b.sb(ctx, name + "shift", [P, D]) if modulate else None
        self.st = b.sb(ctx, name + "st", [P, 6, 9])
        self.tp = b.ps(ctx, name + "tp", [P, slots, KC, P])
        names = [f"rx{i}" for i in range(loads)] + ["gains", "ss1", "sd1", "r1", "xg", "x", "ss2", "sd2", "r2", "xn", "tp", "xh", "xl", "stored"]
        self.s = {n: b.sem(ctx, name + n) for n in names}

    def load_gains(self, sp):
        s = self.s["gains"]
        sp.dma_start(self.gpost[:, :], rows_of(self.post_gain)).then_inc(s, 16)
        self.gains = 16
        if self.gpre is not None:
            sp.dma_start(self.gpre[:, :], rows_of(self.pre_gain)).then_inc(s, 16)
            self.gains += 16
        if self.modulate:
            sp.dma_start(self.scale[:, :], rows_of(self.modulate[0])).then_inc(s, 16)
            sp.dma_start(self.shift[:, :], rows_of(self.modulate[1])).then_inc(s, 16)
            self.gains += 32

    def load(self, sp, t):
        r = self.tiles[t][1]
        if t >= self.loads:
            sp.wait_ge(self.s["x"], t - self.loads + 1)
        sp.dma_start(self.rx[0:r, t % self.loads], self.residual(t)).then_inc(self.s[f"rx{t % self.loads}"], 16)

    def keep(self, sp, t):
        c, r = self.tiles[t]
        sp.wait_ge(self.s["x"], t + 1)
        sp.dma_start(self.store[c:c + r, :], self.b.Y[0:r, t]).then_inc(self.s["stored"], 16)

    def sync(self, sp):
        ahead = self.loads - 1
        for t in range(ahead):
            self.load(sp, t)
        for t in range(self.N):
            if t + ahead < self.N:
                self.load(sp, t + ahead)
            self.keep(sp, t)
        sp.wait_ge(self.s["stored"], 16 * self.N)

    def gpsimd(self, pool):
        s, Y = self.s, self.b.Y
        for t in range(self.N):
            r = self.tiles[t][1]
            pool.wait_ge(s[f"rx{t % self.loads}"], 16 * (t // self.loads + 1))
            pool.wait_ge(s["xg"], t + 1)
            pool.tensor_tensor(Y[0:r, t], Y[0:r, t], self.rx[0:r, t % self.loads], ALU.add).then_inc(s["x"], 1)

    def _square(self, act, t, row, total, root):
        r, st = self.tiles[t][1], self.st
        act.activation(self.junk[0:r], self.b.Y[0:r, t], ACT.Square, accum_out=st[0:r, row, t:t + 1]).then_inc(self.s[total], 1)
        act.wait_ge(self.s[total], t + 1)
        act.activation(st[0:r, row + 1, t:t + 1], st[0:r, row, t:t + 1], ACT.Sqrt, bias=self.b.eps[0:r], scale=1.0 / D).then_inc(self.s[root], 1)

    def scalar(self, act, k):
        s = self.s
        if k < self.N:
            self.ready(act, k)
            self._square(act, k, 0, "ss1", "sd1")
        if 0 <= k - 2 < self.N and not self.modulate:
            act.wait_ge(s["x"], k - 1)
            self._square(act, k - 2, 3, "ss2", "sd2")
        if 0 <= k - 3 < self.N:
            t = k - 3
            act.wait_ge(s["tp"], t + 1)
            act.activation(self.b.XH[:, :, self.cols(t)], self.tp[:, t % self.slots, :, 0:self.tiles[t][1]], ACT.Copy).then_inc(s["xh"], 1)

    def vector(self, dve, k):
        s, st, Y, xn = self.s, self.st, self.b.Y, self.xn
        if k == 0:
            dve.wait_ge(s["gains"], self.gains)
        if k < self.N:
            t, r = k, self.tiles[k][1]
            self.ready(dve, t)
            dve.wait_ge(s["sd1"], t + 1)
            dve.reciprocal(st[0:r, 2, t:t + 1], st[0:r, 1, t:t + 1]).then_inc(s["r1"], 1)
            dve.wait_ge(s["r1"], t + 1)
            dve.scalar_tensor_tensor(Y[0:r, t], Y[0:r, t], st[0:r, 2, t:t + 1], self.gpost[0:r], ALU.mult, ALU.mult).then_inc(s["xg"], 1)
        lag = self.slots + 2
        if 0 <= k - lag < self.N:
            t = k - lag
            r, o = self.tiles[t][1], self.cols(t)
            dve.wait_ge(s["xh"], t + 1)
            dve.tensor_tensor(self.b.XL[:, :, o], self.tp[:, t % self.slots, :, 0:r], self.b.XH[:, :, o].bitcast(f32), ALU.subtract).then_inc(s["xl"], 1)
        if 0 <= k - 2 < self.N:
            t = k - 2
            r = self.tiles[t][1]
            if self.modulate:
                dve.wait_ge(s["x"], t + 1)
                if t >= 2:
                    dve.wait_ge(s["tp"], t - 1)
                dve.tensor_tensor(xn[0:r, t % 2], Y[0:r, t], self.scale[0:r], ALU.mult).then_inc(s["r2"], 1)
                dve.wait_ge(s["r2"], t + 1)
                dve.tensor_tensor(xn[0:r, t % 2], xn[0:r, t % 2], self.shift[0:r], ALU.add).then_inc(s["xn"], 1)
            else:
                dve.wait_ge(s["sd2"], t + 1)
                dve.reciprocal(st[0:r, 5, t:t + 1], st[0:r, 4, t:t + 1]).then_inc(s["r2"], 1)
                dve.wait_ge(s["r2"], t + 1)
                if t >= 2:
                    dve.wait_ge(s["tp"], t - 1)
                if self.gpre is not None:
                    dve.scalar_tensor_tensor(xn[0:r, t % 2], Y[0:r, t], st[0:r, 5, t:t + 1], self.gpre[0:r], ALU.mult, ALU.mult).then_inc(s["xn"], 1)
                else:
                    dve.tensor_scalar(xn[0:r, t % 2], Y[0:r, t], st[0:r, 5, t:t + 1], None, ALU.mult).then_inc(s["xn"], 1)

    def tensor(self, pe, t):
        r = self.tiles[t][1]
        pe.wait_ge(self.s["xn"], t + 1)
        if t >= self.slots:
            pe.wait_ge(self.s["xl"], t - self.slots + 1)
        for f in range(KC):
            last = pe.transpose(self.tp[:, t % self.slots, f, 0:r], self.xn[0:r, t % 2, f * P:(f + 1) * P], self.b.ident[0:r, 0:r])
        last.then_inc(self.s["tp"], 1)


def post_stage(b, name, tiles, residual, store, post_gain, pre_gain=None, **more):
    with b.stage() as ctx:
        tail = Tail(b, ctx, name, tiles, residual, store, post_gain, pre_gain, loads=3, **more)
        with b.nc.Block() as block:
            @block.sync
            def _(sp):
                tail.load_gains(sp)
                tail.sync(sp)

            @block.gpsimd
            def _(pool):
                tail.gpsimd(pool)

            @block.scalar
            def _(act):
                for k in range(tail.N + tail.STEPS):
                    tail.scalar(act, k)

            @block.vector
            def _(dve):
                for k in range(tail.N + tail.STEPS):
                    tail.vector(dve, k)

            @block.tensor
            def _(pe):
                for t in range(tail.N):
                    tail.tensor(pe, t)


def ffn_stage(b, name, layer, tiles, slices):
    nc, ins = b.nc, b.ins
    NS, NTL = len(slices), len(tiles)
    ND = 2 * NTL
    NG = NQ // 2
    WMAX = max(w for _, w in slices)
    wgu = ins["w_gate_up"][layer].rearrange("c p k f -> p c k f")
    wdn = ins["w_down"][layer]
    with b.stage() as ctx:
        raw = b.sb(ctx, name + "raw", [P, 3, KC, P])
        wH = b.sb(ctx, name + "wH", [P, 2, 2, KC, P], f32r)
        wL = b.sb(ctx, name + "wL", [P, 2, 2, KC, P], f32r)
        dH = b.sb(ctx, name + "dH", [P, 2, D], f32r)
        dL = b.sb(ctx, name + "dL", [P, 2, D], f32r)
        hH = b.sb(ctx, name + "hH", [P, 2, 2, TOK], f32r)
        hL = b.sb(ctx, name + "hL", [P, 2, 2, TOK], f32r)
        sg = b.sb(ctx, name + "sg", [P, 2, WMAX])
        hf = b.sb(ctx, name + "hf", [P, 2, WMAX])
        gu = b.ps(ctx, name + "gu", [P, 2, 2, 512])
        dn = b.ps(ctx, name + "dn", [P, 4, 512])
        s = {n: b.sem(ctx, name + n) for n in ("rg", "ru", "rd", "ghi", "uhi", "dhi", "glo", "ulo", "dlo", "unit", "silu", "mul", "hh", "hl", "down", "acc", "zero")}

        def gate_src(q):
            return wgu[:, bass.ds(q, 1)].rearrange("p c k f -> p (c k) f")

        def up_src(q):
            return wgu[:, bass.ds(NQ + q, 1)].rearrange("p c k f -> p (c k) f")

        def down_src(q):
            return wdn[bass.ds(q * P, P), :]

        with nc.Block() as block:
            @block.sync
            def _(sp):
                def gate_up(q, first=False):
                    if not first:
                        sp.wait_ge(s["glo"], q)
                    sp.dma_start(raw[:, 0], gate_src(q)).then_inc(s["rg"], 16)
                    if not first:
                        sp.wait_ge(s["ulo"], q)
                    sp.dma_start(raw[:, 1], up_src(q)).then_inc(s["ru"], 16)

                def down(q):
                    sp.wait_ge(s["dlo"], q)
                    sp.dma_start(raw[:, 2].rearrange("p k f -> p (k f)"), down_src(q)).then_inc(s["rd"], 16)

                gate_up(0, first=True)
                gate_up(1)
                with sp.Fori(0, NQ - 2) as q:
                    gate_up(q + 2)
                    down(q)
                down(NQ - 2)
                down(NQ - 1)

            @block.gpsimd
            def _(pool):
                pool.memset(b.Y[:, 0:NTL, :], 0.0).then_inc(s["zero"], 1)

            @block.scalar
            def _(act):
                def split_gate_up(q, slot, wait_slot=True):
                    if wait_slot:
                        act.wait_ge(s["unit"], (q - 1) * NS)
                    act.wait_ge(s["rg"], 16 * q + 16)
                    act.activation(wH[:, slot, 0], raw[:, 0], ACT.Copy).then_inc(s["ghi"], 1)
                    act.wait_ge(s["ru"], 16 * q + 16)
                    act.activation(wH[:, slot, 1], raw[:, 1], ACT.Copy).then_inc(s["uhi"], 1)

                def split_down(q, c):
                    act.wait_ge(s["down"], (q - c) * NTL)
                    act.wait_ge(s["rd"], 16 * q + 16)
                    act.activation(dH[:, c], raw[:, 2].rearrange("p k f -> p (k f)"), ACT.Copy).then_inc(s["dhi"], 1)

                def unit(q, n, slot, c, first=False):
                    c0, w = slices[n]
                    u = q * NS + n
                    i = (c * NS + n) % 2
                    act.wait_ge(s["unit"], u + 1)
                    if not first:
                        act.wait_ge(s["mul"], u - 1)
                    act.activation(sg[:, i, 0:w], gu[:, i, 0, 0:w], ACT.Silu).then_inc(s["silu"], 1)
                    act.wait_ge(s["mul"], u + 1)
                    act.activation(hH[:, slot, c, c0:c0 + w], hf[:, i, 0:w], ACT.Copy).then_inc(s["hh"], 1)

                def step(g, slot, first=False, final=False):
                    for c in range(2):
                        q = 2 * g + c
                        if not (final and c == 1):
                            split_gate_up(q + 1, (c + 1) % 2, wait_slot=not (first and c == 0))
                        if not first:
                            split_down(q - 2, c)
                        for n in range(NS):
                            unit(q, n, slot, c, first=first and c == 0 and n < 2)

                split_gate_up(0, 0, wait_slot=False)
                step(0, 0, first=True)
                with act.Fori(0, (NG - 3) // 2) as j:
                    step(2 * j + 1, 1)
                    step(2 * j + 2, 0)
                step(NG - 2, 1)
                step(NG - 1, 0, final=True)
                split_down(NQ - 2, 0)
                split_down(NQ - 1, 1)

            @block.vector
            def _(dve):
                def split_gate_up(q, slot):
                    dve.wait_ge(s["ghi"], q + 1)
                    dve.tensor_tensor(wL[:, slot, 0], raw[:, 0], wH[:, slot, 0].bitcast(f32), ALU.subtract).then_inc(s["glo"], 1)
                    dve.wait_ge(s["uhi"], q + 1)
                    dve.tensor_tensor(wL[:, slot, 1], raw[:, 1], wH[:, slot, 1].bitcast(f32), ALU.subtract).then_inc(s["ulo"], 1)

                def split_down(q, c):
                    dve.wait_ge(s["dhi"], q + 1)
                    dve.tensor_tensor(dL[:, c], raw[:, 2].rearrange("p k f -> p (k f)"), dH[:, c].bitcast(f32), ALU.subtract).then_inc(s["dlo"], 1)

                def unit(q, n, slot, c):
                    c0, w = slices[n]
                    u = q * NS + n
                    i = (c * NS + n) % 2
                    dve.wait_ge(s["silu"], u + 1)
                    dve.tensor_tensor(hf[:, i, 0:w], sg[:, i, 0:w], gu[:, i, 1, 0:w], ALU.mult).then_inc(s["mul"], 1)
                    dve.wait_ge(s["hh"], u + 1)
                    dve.tensor_tensor(hL[:, slot, c, c0:c0 + w], hf[:, i, 0:w], hH[:, slot, c, c0:c0 + w].bitcast(f32), ALU.subtract).then_inc(s["hl"], 1)

                def adds(g, par):
                    for i in range(ND):
                        t, half = i // 2, i % 2
                        r = tiles[t][1]
                        y = b.Y[0:r, t, 512 * half:512 * (half + 1)]
                        dve.wait_ge(s["down"], g * ND + i + 1)
                        dve.wait_ge(s["acc"], g * ND + i + 1)
                        dve.tensor_tensor(y, dn[0:r, (par * ND + i) % 4], y, ALU.add).then_inc(s["acc"], 1)

                def step(g, slot, first=False, final=False):
                    for c in range(2):
                        q = 2 * g + c
                        if not (final and c == 1):
                            split_gate_up(q + 1, (c + 1) % 2)
                        if not first:
                            split_down(q - 2, c)
                        for n in range(NS):
                            unit(q, n, slot, c)
                    if not first:
                        adds(g - 1, 1 - slot)

                split_gate_up(0, 0)
                dve.wait_ge(s["zero"], 1)
                dve.sem_inc(s["acc"], ND)
                step(0, 0, first=True)
                with dve.Fori(0, (NG - 3) // 2) as j:
                    step(2 * j + 1, 1)
                    step(2 * j + 2, 0)
                step(NG - 2, 1)
                step(NG - 1, 0, final=True)
                split_down(NQ - 2, 0)
                split_down(NQ - 1, 1)
                adds(NG - 1, 0)

            @block.tensor
            def _(pe):
                def gate_up(g, slot, first=False):
                    for c in range(2):
                        q = 2 * g + c
                        pe.wait_ge(s["ulo"], q + 1)
                        for n, (c0, w) in enumerate(slices):
                            i = (c * NS + n) % 2
                            u = q * NS + n
                            if not (first and c == 0 and n < 2):
                                pe.wait_ge(s["mul"], u - 1)
                            for j in range(2):
                                o = gu[:, i, j, 0:w]
                                for k in range(KC):
                                    xh, xl = b.XH[:, k, c0:c0 + w], b.XL[:, k, c0:c0 + w]
                                    pe.matmul(o, wH[:, c, j, k], xh, start=(k == 0), stop=False)
                                    pe.matmul(o, wH[:, c, j, k], xl, start=False, stop=False)
                                    last = pe.matmul(o, wL[:, c, j, k], xh, start=False, stop=(k == KC - 1))
                            last.then_inc(s["unit"], 1)

                def down(g, slot):
                    pe.wait_ge(s["dlo"], 2 * g + 2)
                    pe.wait_ge(s["hl"], (2 * g + 2) * NS)
                    for i in range(ND):
                        t, half = i // 2, i % 2
                        t0, r = tiles[t]
                        o = dn[0:r, (slot * ND + i) % 4]
                        pe.wait_ge(s["acc"], (g + 1) * ND + i - 3)
                        for c in range(2):
                            hh, hl = hH[:, slot, c, t0:t0 + r], hL[:, slot, c, t0:t0 + r]
                            wh, wl = (w[:, c, 512 * half:512 * (half + 1)] for w in (dH, dL))
                            pe.matmul(o, hh, wh, start=(c == 0), stop=False)
                            pe.matmul(o, hh, wl, start=False, stop=False)
                            last = pe.matmul(o, hl, wh, start=False, stop=(c == 1))
                        last.then_inc(s["down"], 1)

                gate_up(0, 0, first=True)
                with pe.Fori(0, (NG - 3) // 2) as j:
                    gate_up(2 * j + 1, 1)
                    down(2 * j, 0)
                    gate_up(2 * j + 2, 0)
                    down(2 * j + 1, 1)
                gate_up(NG - 2, 1)
                down(NG - 3, 0)
                gate_up(NG - 1, 0)
                down(NG - 2, 1)
                down(NG - 1, 0)


class Guest:

    def sync(self, sp, m):
        pass

    def gpsimd(self, pool):
        pass

    def scalar(self, act):
        pass

    def vector(self, dve, m):
        pass

    def tensor(self, pe, m):
        pass


def project_features(b, name, chunks, small, evac_act, evac_dve=None, raws=3, guests=()):
    M = len(chunks)
    units = [(m, n, c0, w) for m in range(M) for n, (c0, w) in enumerate(chunks[m][1])]
    of = [[u for u in range(len(units)) if units[u][0] == m] for m in range(M)]
    gained = [0]
    for _, _, gain in chunks:
        gained.append(gained[-1] + (gain is not None))
    with b.stage() as ctx:
        raw = b.sb(ctx, name + "raw", [P, raws, KC, P])
        wH = b.sb(ctx, name + "wH", [P, 2, KC, P], f32r)
        wL = b.sb(ctx, name + "wL", [P, 2, KC, P], f32r)
        pr = b.ps(ctx, name + "pr", [P, 4, 512])
        s = {n: b.sem(ctx, name + n) for n in ("r0", "r1", "r2", "small", "gained", "hi", "lo", "unit", "act", "dve")}
        with b.nc.Block() as block:
            @block.sync
            def _(sp):
                for dst, src in small:
                    sp.dma_start(dst, src).then_inc(s["small"], 16)
                for m in range(M):
                    if m >= raws:
                        sp.wait_ge(s["lo"], m - raws + 1)
                    sp.dma_start(raw[:, m % raws], chunks[m][0]).then_inc(s[f"r{m % raws}"], 16)
                    for guest in guests:
                        guest.sync(sp, m)
                for guest in guests:
                    guest.sync(sp, M)

            @block.gpsimd
            def _(pool):
                for guest in guests:
                    guest.gpsimd(pool)

            @block.scalar
            def _(act):
                act.wait_ge(s["small"], 16 * len(small))
                for guest in guests:
                    guest.scalar(act)

                def split(m):
                    act.wait_ge(s[f"r{m % raws}"], 16 * (m // raws + 1))
                    if chunks[m][2] is not None:
                        act.wait_ge(s["gained"], gained[m + 1])
                    if m >= 2:
                        act.wait_ge(s["unit"], of[m - 2][-1] + 1)
                    act.activation(wH[:, m % 2], raw[:, m % raws], ACT.Copy).then_inc(s["hi"], 1)
                split(0)
                for m in range(M):
                    if m + 1 < M:
                        split(m + 1)
                    for u in of[m]:
                        _, n, c0, w = units[u]
                        act.wait_ge(s["unit"], u + 1)
                        made = evac_act(act, m, n, c0, w, pr[:, u % 4, 0:w], s["dve"], u)
                        if made:
                            made.then_inc(s["act"], 1)
                        else:
                            act.sem_inc(s["act"], 1)

            @block.vector
            def _(dve):
                dve.wait_ge(s["small"], 16 * len(small))

                def gain(m):
                    if chunks[m][2] is not None:
                        g = chunks[m][2].rearrange("p (k o) -> p k o", o=1).broadcast_to([P, KC, P])
                        dve.wait_ge(s[f"r{m % raws}"], 16 * (m // raws + 1))
                        dve.tensor_tensor(raw[:, m % raws], raw[:, m % raws], g, ALU.mult).then_inc(s["gained"], 1)

                def split(m):
                    dve.wait_ge(s["hi"], m + 1)
                    dve.tensor_tensor(wL[:, m % 2], raw[:, m % raws], wH[:, m % 2].bitcast(f32), ALU.subtract).then_inc(s["lo"], 1)
                gain(0)
                gain(1)
                split(0)
                for m in range(M):
                    if m + 1 < M:
                        split(m + 1)
                    if m + 2 < M:
                        gain(m + 2)
                    for guest in guests:
                        guest.vector(dve, m)
                    if evac_dve:
                        for u in of[m]:
                            _, n, c0, w = units[u]
                            dve.wait_ge(s["act"], u + 1)
                            evac_dve(dve, m, n, c0, w, pr[:, u % 4, 0:w], s["dve"], u).then_inc(s["dve"], 1)
                for guest in guests:
                    guest.vector(dve, M)

            @block.tensor
            def _(pe):
                done = s["dve"] if evac_dve else s["act"]
                for m in range(M):
                    for guest in guests:
                        guest.tensor(pe, m)
                    pe.wait_ge(s["lo"], m + 1)
                    for u in of[m]:
                        _, n, c0, w = units[u]
                        if u >= 4:
                            pe.wait_ge(done, u - 3)
                        o = pr[:, u % 4, 0:w]
                        for k in range(KC):
                            xh, xl = b.XH[:, k, c0:c0 + w], b.XL[:, k, c0:c0 + w]
                            pe.matmul(o, wH[:, m % 2, k], xh, start=(k == 0), stop=False)
                            pe.matmul(o, wH[:, m % 2, k], xl, start=False, stop=False)
                            last = pe.matmul(o, wL[:, m % 2, k], xh, start=False, stop=(k == KC - 1))
                        last.then_inc(s["unit"], 1)
                for guest in guests:
                    guest.tensor(pe, M)


def project_tokens(b, name, weights, parts, small, evac, on_act=False, slots=2, raws=3, make_tail=None, order=None, side=None):
    order = order or list(range(parts))
    LAG = 3
    with b.stage() as ctx:
        raw = b.sb(ctx, name + "raw", [P, raws, 2, 512])
        wH = b.sb(ctx, name + "wH", [P, slots, KC, 512], f32r)
        wL = b.sb(ctx, name + "wL", [P, slots, KC, 512], f32r)
        pr = b.ps(ctx, name + "pr", [P, 4, 512])
        s = {n: b.sem(ctx, name + n) for n in ("r0", "r1", "r2", "small", "hi", "lo", "unit", "out")}
        src = weights.rearrange("(k p) f -> p k f", p=P)
        tail = make_tail(ctx, lambda eng, t: eng.wait_ge(s["out"], (parts - 1) * NT + t + 1)) if make_tail else None
        NP = KC // 2
        with b.nc.Block() as block:
            @block.sync
            def _(sp):
                for i in range(parts * NP):
                    c, k = i // NP, 2 * (i % NP)
                    if i >= raws:
                        sp.wait_ge(s["lo"], i - raws + 1)
                    sp.dma_start(raw[:, i % raws], src[:, k:k + 2, 512 * order[c]:512 * (order[c] + 1)]).then_inc(s[f"r{i % raws}"], 16)
                    if i == 0:
                        for dst, a in small:
                            sp.dma_start(dst, a).then_inc(s["small"], 16)
                if side:
                    side.sync(sp)
                if tail:
                    tail.load_gains(sp)
                    tail.sync(sp)

            @block.gpsimd
            def _(pool):
                if side:
                    side.gpsimd(pool)
                if tail:
                    tail.gpsimd(pool)

            @block.scalar
            def _(act):
                def split(c):
                    for i in range(c * NP, (c + 1) * NP):
                        k = 2 * (i % NP)
                        act.wait_ge(s[f"r{i % raws}"], 16 * (i // raws + 1))
                        if c >= slots:
                            act.wait_ge(s["unit"], NT * (c - slots + 1))
                        act.activation(wH[:, c % slots, k:k + 2], raw[:, i % raws], ACT.Copy).then_inc(s["hi"], 1)
                for c in range(slots):
                    split(c)
                act.wait_ge(s["small"], 16 * len(small))
                for c in range(parts):
                    if on_act:
                        for t in range(NT):
                            act.wait_ge(s["unit"], c * NT + t + 1)
                            evac(act, c, t, pr[:, (c * NT + t) % 4]).then_inc(s["out"], 1)
                    if side:
                        side.scalar(act, c)
                    if c + slots < parts:
                        split(c + slots)
                if tail:
                    for k in range(NT + tail.STEPS):
                        tail.scalar(act, k)

            @block.vector
            def _(dve):
                def split(c):
                    for i in range(c * NP, (c + 1) * NP):
                        k = 2 * (i % NP)
                        dve.wait_ge(s["hi"], i + 1)
                        dve.tensor_tensor(wL[:, c % slots, k:k + 2], raw[:, i % raws], wH[:, c % slots, k:k + 2].bitcast(f32), ALU.subtract).then_inc(s["lo"], 1)
                for c in range(slots):
                    split(c)
                dve.wait_ge(s["small"], 16 * len(small))
                for c in range(parts):
                    if not on_act:
                        for t in range(NT):
                            u = c * NT + t
                            dve.wait_ge(s["unit"], u + 1)
                            evac(dve, c, t, pr[:, u % 4]).then_inc(s["out"], 1)
                            if tail and c == parts - 1:
                                tail.vector(dve, t)
                    if c + slots < parts:
                        split(c + slots)
                    if side:
                        side.vector(dve, c, s["out"])
                if tail:
                    for k in range(NT, NT + tail.STEPS):
                        tail.vector(dve, k)

            @block.tensor
            def _(pe):
                for c in range(parts):
                    for t in range(NT):
                        u = c * NT + t
                        if u >= 4:
                            pe.wait_ge(s["out"], u - 3)
                        o = pr[:, u % 4]
                        for k in range(KC):
                            if t == 0 and k % 2 == 0:
                                pe.wait_ge(s["lo"], c * NP + k // 2 + 1)
                            xh, xl = (x[:, k, P * t:P * (t + 1)] for x in (b.XH, b.XL))
                            pe.matmul(o, xh, wH[:, c % slots, k], start=(k == 0), stop=False)
                            pe.matmul(o, xh, wL[:, c % slots, k], start=False, stop=False)
                            last = pe.matmul(o, xl, wH[:, c % slots, k], start=False, stop=(k == KC - 1))
                        last.then_inc(s["unit"], 1)
                        if tail and c == parts - 1 and t >= LAG:
                            tail.tensor(pe, t - LAG)
                if side:
                    side.tensor(pe)
                if tail:
                    for t in range(NT - LAG, NT):
                        tail.tensor(pe, t)


class BiasGuest(Guest):
    W = 3 * P

    def __init__(self, b, ctx, bias_rows, sinks):
        self.b, self.bias_rows, self.sinks = b, bias_rows, sinks
        self.table = b.nc.dram_tensor("bias_table", [HEADS, P, self.W], f32, kind="Internal").ap()
        self.rel = b.sb(ctx, "rel", [33, HEADS])
        self.hot = b.sb(ctx, "hot", [33, self.W])
        self.g = b.sb(ctx, "bias_by_offset", [HEADS, self.W])
        self.pb = b.ps(ctx, "pb", [HEADS, 512])
        self.s_in, self.s_neg, self.s_g, self.s_ge, self.s_out, self.s_read = (
            b.sem(ctx, n) for n in ("bias_in", "bias_neg", "bias_g", "bias_ge", "bias_out", "bias_read"))

    def sync(self, sp, m):
        ins, table = self.b.ins, self.table
        if m == 0:
            sp.dma_start(self.rel[0:32, :], ins["rel_bias"]).then_inc(self.s_in, 16)
            sp.dma_start(self.hot[:, :], ins["cst"][0:33, C_HOT:C_HOT + self.W]).then_inc(self.s_in, 16)
            sp.dma_start(self.sinks[:, :], rows_of(ins["sinks"][0])).then_inc(self.s_in, 16)
        if m == 3:
            sp.wait_ge(self.s_ge, 1)
            sp.dma_start(table, self.g[:, :].rearrange("h (o w) -> h o w", o=1).broadcast_to([HEADS, P, self.W])).then_inc(self.s_out, 16)
        if m == 7:
            sp.wait_ge(self.s_out, 16)
            skew = bass.AP(tensor=table.tensor, offset=P - 1, ap=[[self.W - 1, P], [P * self.W, HEADS], [1, 2 * P]])
            sp.dma_start(self.bias_rows[:, :, :], skew).then_inc(self.s_read, 16)
        if m > 7 and m == self.end:
            sp.wait_ge(self.s_read, 16)

    def gpsimd(self, pool):
        pool.memset(self.rel[32:33, :], NEG).then_inc(self.s_neg, 1)
        pool.wait_ge(self.s_neg, 1)

    def tensor(self, pe, m):
        if m == 1:
            pe.wait_ge(self.s_in, 48)
            pe.wait_ge(self.s_neg, 1)
            pe.matmul(self.pb[:, 0:self.W], self.rel[:, :], self.hot[:, :], start=True, stop=True).then_inc(self.s_g, 1)

    def vector(self, dve, m):
        if m == 1:
            dve.wait_ge(self.s_g, 1)
            dve.tensor_copy(self.g[:, :], self.pb[:, 0:self.W]).then_inc(self.s_ge, 1)


class AdaGuest(Guest):

    def __init__(self, b, ctx, rows, end):
        self.b, self.rows, self.end = b, rows, end
        Y = b.Y[:, :, :].rearrange("p t d -> p (t d)")
        self.acc = Y[:, 0:3 * D]
        self.w = [Y[:, 3 * D * (1 + i):3 * D * (2 + i)] for i in range(2)]
        self.cc = b.sb(ctx, "cc", [P, KC])
        self.cs = b.sb(ctx, "cs", [P, KC])
        self.ones = b.sb(ctx, "ada_ones", [P, 1])
        self.pm = b.ps(ctx, "ada_ps", [1, 2, 512])
        self.s = {n: b.sem(ctx, "ada_" + n) for n in ("c", "cs", "zero", "bias", "w0", "w1", "sum", "mm", "row", "out")}

    def sync(self, sp, m):
        ins, s = self.b.ins, self.s
        if m == 0:
            sp.dma_start(self.cc[:, :], ins["c_2"]).then_inc(s["c"], 16)
        if m == 1:
            sp.wait_ge(s["zero"], 1)
            sp.dma_start(self.acc[0:1, :], ins["b_ada_2"].rearrange("(a n) -> a n", a=1)).then_inc(s["bias"], 16)
        if 1 <= m <= KC:
            k = m - 1
            if k >= 2:
                sp.wait_ge(s["sum"], k - 1)
            sp.dma_start(self.w[k % 2], ins["w_ada_2"][P * k:P * (k + 1), :]).then_inc(s[f"w{k % 2}"], 16)
        if m == self.end:
            sp.wait_ge(s["row"], 6)
            sp.dma_start(self.rows, self.w[0][0:1, :]).then_inc(s["out"], 16)
            sp.wait_ge(s["out"], 16)

    def gpsimd(self, pool):
        pool.memset(self.acc, 0.0).then_inc(self.s["zero"], 1)
        pool.memset(self.ones[:, :], 1.0).then_inc(self.s["zero"], 1)

    def scalar(self, act):
        act.wait_ge(self.s["c"], 16)
        act.activation(self.cs[:, :], self.cc[:, :], ACT.Silu).then_inc(self.s["cs"], 1)

    def vector(self, dve, m):
        s = self.s
        if 1 <= m <= KC:
            k = m - 1
            if k == 0:
                dve.wait_ge(s["cs"], 1)
                dve.wait_ge(s["bias"], 16)
            dve.wait_ge(s[f"w{k % 2}"], 16 * (k // 2 + 1))
            if k:
                dve.wait_ge(s["sum"], k)
            dve.scalar_tensor_tensor(self.acc, self.w[k % 2], self.cs[:, k:k + 1], self.acc, ALU.mult, ALU.add).then_inc(s["sum"], 1)
        if m == self.end:
            for c in range(6):
                dve.wait_ge(s["mm"], c + 1)
                dve.tensor_scalar(self.w[0][0:1, 512 * c:512 * (c + 1)], self.pm[:, c % 2], 1.0 if c // 2 == 1 else 0.0, None, ALU.add).then_inc(s["row"], 1)

    def tensor(self, pe, m):
        s = self.s
        if m == self.end:
            pe.wait_ge(s["zero"], 2)
            pe.wait_ge(s["sum"], KC)
            for c in range(6):
                if c >= 2:
                    pe.wait_ge(s["row"], c - 1)
                pe.matmul(self.pm[:, c % 2], self.ones[:, :], self.acc[:, 512 * c:512 * (c + 1)], start=True, stop=True).then_inc(s["mm"], 1)


class KeyValueGuest(Guest):

    def __init__(self, b, ctx, KT, VT, V):
        self.b, self.KT, self.VT, self.V = b, KT, VT, V
        self.tv = b.ps(ctx, "turned_values", [P, 4, P])
        self.kv = b.sem(ctx, "kv_made")
        self.s = {n: b.sem(ctx, "kv_" + n) for n in ("zero", "dup", "turned", "moved")}
        self.keys = 6

    def sync(self, sp, m):
        if m == 4:
            sp.wait_ge(self.kv, self.keys)
            sp.wait_ge(self.s["zero"], 3)
            sp.dma_start(self.KT[HD:P, 0, :], self.KT[0:HD, 0, :]).then_inc(self.s["dup"], 16)
            sp.dma_start(self.KT[0:HD, 1, :], self.KT[HD:P, 1, :]).then_inc(self.s["dup"], 16)
        if m == 8:
            sp.wait_ge(self.s["dup"], 32)

    def gpsimd(self, pool):
        zero = self.s["zero"]
        pool.memset(self.KT[0:HD, 0, 0:PAD], 0.0).then_inc(zero, 1)
        pool.wait_ge(zero, 1)
        pool.memset(self.KT[HD:P, 1, 0:PAD], 0.0).then_inc(zero, 1)
        pool.wait_ge(zero, 2)
        pool.memset(self.VT[:, 0:PAD], 0.0).then_inc(zero, 1)
        pool.wait_ge(zero, 3)

    def tensor(self, pe, m):
        if m == 4:
            pe.wait_ge(self.kv, self.keys + 3)
            pe.wait_ge(self.s["zero"], 3)
        if 4 <= m < 7:
            if m > 4:
                pe.wait_ge(self.s["moved"], m - 4)
            for i in range(3):
                t = 3 * (m - 4) + i
                last = pe.transpose(self.tv[:, i], self.VT[:, P * t:P * (t + 1)], self.b.ident[:, :])
            last.then_inc(self.s["turned"], 1)

    def vector(self, dve, m):
        if 4 <= m < 7:
            dve.wait_ge(self.s["turned"], m - 3)
            dve.tensor_copy(self.V[:, 3 * (m - 4):3 * (m - 3), :], self.tv[:, 0:3]).then_inc(self.s["moved"], 1)


def attention_stage(b, KT, V, QT, bias_rows, sinks):
    nc = b.nc
    NP = HEADS // 2
    order = list(range(1, NT)) + [0]
    with b.stage() as ctx:
        lg = b.sb(ctx, "logits", [P, 3, 2, 2 * P])
        pr = b.sb(ctx, "probs", [P, 4, 2, 2 * P])
        pT = b.sb(ctx, "probsT", [P, 2, 4, P])
        m, nm, dm, rsum, es, den, rden = (b.sb(ctx, "attn_" + n, [P, 4, 2]) for n in ("m", "nm", "dm", "rsum", "es", "den", "rden"))
        qk = b.ps(ctx, "qk", [P, 2, 2, 512])
        tp = b.ps(ctx, "attn_tp", [P, 2, 4, P])
        op = b.ps(ctx, "op", [P, 2, 512])
        s = {n: b.sem(ctx, "attn_" + n) for n in ("qk", "max", "nm", "dm", "exp", "es", "den", "rd", "pn", "tp", "pT", "pv", "xh", "xl", "mask")}
        U = NT * NP
        LAST = U + 4
        WARM = 4

        def unit(u):
            return order[u // NP], u % NP, (u % NP) // (NP // KVH)

        with nc.Block() as block:
            @block.tensor
            def _(pe):
                for k in range(LAST):
                    if k < U:
                        n, p, kvh = unit(k)
                        if k >= 2:
                            pe.wait_ge(s["max"], 2 * (k - 1))
                        for e in range(2):
                            last = pe.matmul(qk[:, k % 2, e, 0:2 * P], QT[HD * e:HD * (e + 1), p, P * n:P * (n + 1)],
                                             KT[HD * e:HD * (e + 1), kvh, P * n:P * (n + 2)], start=True, stop=True)
                        last.then_inc(s["qk"], 1)
                    if k == 1:
                        for i in range(WARM):
                            pe.matmul(op[:, i % 2], QT[:, 0, 0:P], QT[:, 1, 0:512], start=True, stop=True)
                    if 2 <= k < U + 2:
                        u = k - 2
                        pe.wait_ge(s["pn"], 2 * (u + 1))
                        if u >= 2:
                            pe.wait_ge(s["pT"], u - 1)
                        for e in range(2):
                            for j in range(2):
                                last = pe.transpose(tp[:, u % 2, 2 * e + j], pr[:, u % 4, e, P * j:P * (j + 1)], b.ident[:, :])
                        last.then_inc(s["tp"], 1)
                    if 3 <= k < U + 3:
                        u = k - 3
                        n, p, kvh = unit(u)
                        pe.wait_ge(s["pT"], u + 1)
                        if u >= 2:
                            pe.wait_ge(s["xl"], u - 1)
                        for e in range(2):
                            for j in range(2):
                                last = pe.matmul(op[HD * e:HD * (e + 1), u % 2, 0:P], V[:, n + j, HD * kvh:HD * (kvh + 1)], pT[:, u % 2, 2 * e + j],
                                                 start=(j == 0), stop=(j == 1))
                        last.then_inc(s["pv"], 1)

            @block.vector
            def _(dve):
                for k in range(LAST):
                    if k < U:
                        n, p, _ = unit(k)
                        i = k % 4
                        if k == U - NP:
                            dve.wait_ge(s["max"], 2 * k)
                            dve.memset(bias_rows[:, :, 0:PAD], NEG).then_inc(s["mask"], 1)
                            dve.wait_ge(s["mask"], 1)
                        dve.wait_ge(s["qk"], k + 1)
                        if k >= 3:
                            dve.wait_ge(s["exp"], 2 * (k - 2))
                        for e in range(2):
                            h = 2 * p + e
                            dve.tensor_tensor_reduce(out=lg[:, k % 3, e], in0=qk[:, k % 2, e, 0:2 * P], in1=bias_rows[:, h], scale=1.0, scalar=sinks[:, h:h + 1],
                                                     op0=ALU.add, op1=ALU.max, accum_out=m[:, i, e:e + 1]).then_inc(s["max"], 1)
                        dve.wait_ge(s["max"], 2 * (k + 1))
                        dve.tensor_scalar(nm[:, i], m[:, i], -1.0, None, ALU.mult).then_inc(s["nm"], 1)
                        dve.tensor_tensor(dm[:, i], sinks[:, 2 * p:2 * p + 2], m[:, i], ALU.subtract).then_inc(s["dm"], 1)
                    if 1 <= k < U + 1:
                        u = k - 1
                        i = u % 4
                        dve.wait_ge(s["es"], u + 1)
                        dve.tensor_tensor(den[:, i], es[:, i], rsum[:, i], ALU.add).then_inc(s["den"], 1)
                        dve.wait_ge(s["den"], u + 1)
                        dve.reciprocal(rden[:, i], den[:, i]).then_inc(s["rd"], 1)
                        dve.wait_ge(s["rd"], u + 1)
                        for e in range(2):
                            dve.tensor_scalar(pr[:, i, e], pr[:, i, e], rden[:, i, e:e + 1], None, ALU.mult).then_inc(s["pn"], 1)
                    if k >= 4:
                        u = k - 4
                        n, p, _ = unit(u)
                        dve.wait_ge(s["xh"], u + 1)
                        o = (slice(None), p, slice(P * n, P * (n + 1)))
                        dve.tensor_tensor(b.XL[o], op[:, u % 2, 0:P], b.XH[o].bitcast(f32), ALU.subtract).then_inc(s["xl"], 1)

            @block.scalar
            def _(act):
                for k in range(1, LAST):
                    if k < U + 1:
                        u = k - 1
                        i = u % 4
                        act.wait_ge(s["nm"], u + 1)
                        if u >= 4:
                            act.wait_ge(s["tp"], u - 3)
                        for e in range(2):
                            act.activation(pr[:, i, e], lg[:, u % 3, e], ACT.Exp, bias=nm[:, i, e:e + 1], accum_out=rsum[:, i, e:e + 1]).then_inc(s["exp"], 1)
                        act.wait_ge(s["dm"], u + 1)
                        act.wait_ge(s["exp"], 2 * (u + 1))
                        act.activation(es[:, i], dm[:, i], ACT.Exp).then_inc(s["es"], 1)
                    if 2 <= k < U + 2:
                        u = k - 2
                        act.wait_ge(s["tp"], u + 1)
                        if u >= 2:
                            act.wait_ge(s["pv"], u - 1)
                        act.activation(pT[:, u % 2], tp[:, u % 2], ACT.Copy).then_inc(s["pT"], 1)
                    if 3 <= k < U + 3:
                        u = k - 3
                        n, p, _ = unit(u)
                        act.wait_ge(s["pv"], u + 1)
                        act.activation(b.XH[:, p, P * n:P * (n + 1)], op[:, u % 2, 0:P], ACT.Copy).then_inc(s["xh"], 1)


def layer1_mixer(b, residual_in, residual_out, x1, ada_rows):
    ins = b.ins
    with b.stage() as ctx:
        KT = b.sb(ctx, "KT", [P, KVH, P * (NT + 1)])
        V = b.sb(ctx, "V", [P, NT + 1, P])

        def rows(src):
            return lambda t: src[TILES_META[t][0]:TILES_META[t][0] + TILES_META[t][1], :]
        post_stage(b, "p1", TILES_META, rows(residual_in), residual_out, ins["norm_ffn_post"][0],
                   cols=lambda t: slice(P * (t - 1), P * t) if t else slice(SEQ, TOK))
        QT = b.sb(ctx, "QT", [P, KC, SEQ])
        bias_rows = b.sb(ctx, "bias_rows", [P, HEADS, 2 * P])
        sinks = b.sb(ctx, "sinks_rows", [P, HEADS])
        with b.stage() as c2:
            VT = b.sb(c2, "VT", [P, P * (NT + 1)])
            bq = b.sb(c2, "bq", [P, KC])
            bq8 = b.sb(c2, "bq8", [P, KC])
            bk = b.sb(c2, "bk", [P, 1])
            bv = b.sb(c2, "bv", [P, 1])
            gq = b.sb(c2, "gains_q", [P, KC])
            gkv = b.sb(c2, "gains_kv", [P, KC])
            s_bq = b.sem(c2, "q_bias")
            all_tokens = SLICES_SEQ + [(SEQ, META)]
            chunks = [(ins["w_k"].rearrange("(k p) f -> p k f", p=P), all_tokens, gkv[:, :]),
                      (ins["w_v"].rearrange("(k p) f -> p k f", p=P), all_tokens, gkv[:, :])]
            chunks += [(ins["w_q"][0][m], SLICES_SEQ, gq[:, :]) for m in range(KC)]
            kvg = KeyValueGuest(b, c2, KT, VT, V)
            bias = BiasGuest(b, c2, bias_rows, sinks)
            bias.end = len(chunks)
            ada = AdaGuest(b, c2, ada_rows, len(chunks) - 1)

            def evac(act, m, n, c0, w, bank, _, u):
                cols = slice(P + c0, P + c0 + w) if c0 < SEQ else slice(PAD, P)
                if m == 0:
                    act.activation(KT[0:HD, 0, cols], bank[0:HD], ACT.Identity, bias=bk[0:HD]).then_inc(kvg.kv, 1)
                    act.activation(KT[HD:P, 1, cols], bank[HD:P], ACT.Identity, bias=bk[HD:P]).then_inc(kvg.kv, 1)
                    act.wait_ge(kvg.kv, 2 * n + 2)
                    return None
                if m == 1:
                    act.activation(VT[:, cols], bank, ACT.Identity, bias=bv[:, :]).then_inc(kvg.kv, 1)
                    act.wait_ge(kvg.kv, kvg.keys + n + 1)
                    return None
                if m == 2 and n == 0:
                    act.activation(bq8[:, :], bq[:, :], ACT.Copy, scale=HD ** -0.5).then_inc(s_bq, 1)
                    act.wait_ge(s_bq, 1)
                return act.activation(QT[:, m - 2, c0:c0 + w], bank, ACT.Identity, bias=bq8[:, m - 2:m - 1], scale=HD ** -0.5)
            small = [(bq[:, :], ins["b_q"]), (bk[:, :], ins["b_k"]), (bv[:, :], ins["b_v"]),
                     (gq[:, :], ins["gains_q"]), (gkv[:, :], ins["gains_kv"])]
            project_features(b, "w_q_", chunks, small, evac, guests=(kvg, bias, ada))
        attention_stage(b, KT, V, QT, bias_rows, sinks)
    with b.stage() as ctx:
        bo = b.sb(ctx, "bo", [P, D])
        project_tokens(b, "w_o_", ins["w_o"][0], 2, [(bo[:, :], rows_of(ins["b_o"][0]))],
                       lambda dve, c, t, bank: dve.tensor_tensor(b.Y[:, t, 512 * c:512 * (c + 1)], bank, bo[:, 512 * c:512 * (c + 1)], ALU.add),
                       raws=2, make_tail=lambda c2, ready: Tail(
                           b, c2, "p2", TILES_SEQ, lambda t: residual_out[META + P * t:META + P * (t + 1), :], x1,
                           ins["norm_mix_post"][1], ins["norm_ffn_pre"][1], ready=ready))


class SpatialGate:

    def __init__(self, b, ctx, U, V, G):
        self.b, self.U, self.V, self.G = b, U, V, G
        self.sq = b.sb(ctx, "sq", [P, NT, DA])
        self.gv = b.sb(ctx, "gv", [P, DA])
        self.bv = b.sb(ctx, "bv_ln", [P, DA])
        self.ws = b.sb(ctx, "ws", [P, GA, P])
        self.bs = b.sb(ctx, "bs", [P, GA])
        self.eps = b.sb(ctx, "ln_eps", [P, 1])
        self.st = b.sb(ctx, "ln_st", [P, 5, NT * GA])
        self.vm = b.ps(ctx, "vm", [P, 4, 512])
        self.s = {n: b.sem(ctx, "gmlp_" + n) for n in ("in", "mask", "eps", "sq", "sd", "vn", "mm", "o", "ug", "chain")}

    def sync(self, sp):
        ins, s_in = self.b.ins, self.s["in"]
        sp.dma_start(self.gv[:, :], rows_of(ins["ln_v_g_2"].rearrange("g d -> (g d)"))).then_inc(s_in, 16)
        sp.dma_start(self.bv[:, :], rows_of(ins["ln_v_b_2"].rearrange("g d -> (g d)"))).then_inc(s_in, 16)
        sp.dma_start(self.ws[:, :, :], ins["w_spatial_2"]).then_inc(s_in, 16)
        sp.dma_start(self.bs[:, :], ins["b_spatial_2"]).then_inc(s_in, 16)

    def gpsimd(self, pool):
        s = self.s
        pool.memset(self.eps[:, :], 1e-5).then_inc(s["eps"], 1)
        pool.wait_ge(s["chain"], 3)
        pool.tensor_tensor(self.sq[:, :, :], self.V, self.V, ALU.mult).then_inc(s["sq"], 1)
        pool.wait_ge(s["in"], 64)
        pool.affine_select(out=self.ws[:, :, :], in_=self.ws[:, :, :], compare_op=ALU.is_ge, fill=0.0, base=0,
                           pattern=[[0, GA], [1, P]], channel_multiplier=-1).then_inc(s["mask"], 1)

    def scalar(self, act, c):
        if c == 1:
            act.wait_ge(self.s["eps"], 1)
            act.wait_ge(self.s["chain"], 4)
            act.activation(self.st[:, 3], self.st[:, 2], ACT.Sqrt, bias=self.eps[:, :], scale=1.0 / HD).then_inc(self.s["sd"], 1)

    def vector(self, dve, c, out):
        s, st, U, V = self.s, self.st, self.U, self.V
        grp = lambda x: x.rearrange("p t (g d) -> p (t g) d", d=HD)
        row = lambda x, i: x[:, i].rearrange("p (g o) -> p g o", o=1).broadcast_to([P, NT * GA, HD])
        tiles = lambda x: x[:, :].rearrange("p (o f) -> p o f", o=1).broadcast_to([P, NT, DA])
        if c == 0:
            self.link = link = linker(dve, s["chain"])
            dve.wait_ge(out, NT)
            link(dve.reduce_sum(st[:, 0], grp(V), axis=mybir.AxisListType.X))
            link(dve.tensor_scalar(st[:, 1], st[:, 0], 1.0 / HD, None, ALU.mult))
            link(dve.tensor_tensor(grp(V), grp(V), row(st, 1), ALU.subtract))
            dve.wait_ge(s["sq"], 1)
            link(dve.reduce_sum(st[:, 2], grp(self.sq[:, :, :]), axis=mybir.AxisListType.X))
        if c == 1:
            dve.wait_ge(s["sd"], 1)
            self.link(dve.reciprocal(st[:, 4], st[:, 3]))
            self.link(dve.tensor_tensor(grp(V), grp(V), row(st, 4), ALU.mult))
            dve.wait_ge(s["in"], 64)
            self.link(dve.tensor_tensor(V, V, tiles(self.gv), ALU.mult))
            dve.tensor_tensor(V, V, tiles(self.bv), ALU.add).then_inc(s["vn"], 1)
            for t in range(NT):
                dve.wait_ge(out, 2 * NT + t + 1)
                dve.tensor_tensor(U[:, t], U[:, t], self.G[:, t], ALU.mult).then_inc(s["ug"], 1)
        if c == 2:
            dve.wait_ge(s["ug"], NT)
            for g in range(GA):
                u = U[:, :, HD * g:HD * (g + 1)]
                dve.wait_ge(s["mm"], g + 1)
                dve.scalar_tensor_tensor(u, self.vm[:, g % 4].rearrange("p (t d) -> p t d", d=HD), self.bs[:, g:g + 1], u, ALU.add, ALU.mult).then_inc(s["o"], 1)

    def tensor(self, pe):
        s = self.s
        pe.wait_ge(s["mask"], 1)
        pe.wait_ge(s["vn"], 1)
        for g in range(GA):
            if g >= 4:
                pe.wait_ge(s["o"], g - 3)
            pe.matmul(self.vm[:, g % 4], self.ws[:, g], self.V[:, :, HD * g:HD * (g + 1)], start=True, stop=True).then_inc(s["mm"], 1)


def gmlp_stage(b):
    U = b.Y[:, 0:4].rearrange("p a (t f) -> p (a t) f", f=DA)
    V = b.Y[:, 4:8].rearrange("p a (t f) -> p (a t) f", f=DA)
    with b.stage() as ctx:
        G = b.sb(ctx, "G", [P, NT, DA])

        def evac(act, c, t, bank):
            dst, f = ((V, ACT.Gelu_apprx_tanh), (U, ACT.Gelu_apprx_tanh), (G, ACT.Silu))[c]
            return act.activation(dst[:, t], bank, f)
        project_tokens(b, "w_in_a_", b.ins["w_in_2"], 3, [], evac, on_act=True, slots=1, order=[1, 0, 2], side=SpatialGate(b, ctx, U, V, G))


class KeepGuest(Guest):

    def __init__(self, b, ctx, out_a):
        self.b, self.out_a, self.kept = b, out_a, b.sem(ctx, "out_a_kept")

    def sync(self, sp, m):
        if m == 2:
            sp.dma_start(self.out_a, self.b.Y[:, 0:4].rearrange("p a (t f) -> p (a t) f", f=DA)).then_inc(self.kept, 16)
        if m == NB:
            sp.wait_ge(self.kept, 16)


def recurrent_inputs(b, PB, out_a):
    ins = b.ins
    with b.stage() as ctx:
        W = SEQ + 1
        shifted = b.sb(ctx, "shifted", [P, 2, W])
        diff = b.sb(ctx, "diff", [P, 2, 512])
        mu = b.sb(ctx, "mu", [P, NB])
        s_zero, s_diff = b.sem(ctx, "shift_zero"), b.sem(ctx, "shift_diff")
        started = []

        def evac_act(act, m, n, c0, w, bank, s_dve, u):
            if not started:
                started.append(1)
                act.activation(shifted[:, :, 0:1], mu[:, 0:2].rearrange("p (a o) -> p a o", o=1), ACT.Copy, scale=0.0).then_inc(s_zero, 1)
            if m >= 2:
                act.wait_ge(s_dve, 2 * (m - 1))
            return act.activation(shifted[:, m % 2, 1 + c0:1 + c0 + w], bank, ACT.Copy)

        def evac_dve(dve, m, n, c0, w, bank, s_dve, u):
            if m == 0 and n == 0:
                dve.wait_ge(s_zero, 1)
            now, before = shifted[:, m % 2, 1 + c0:1 + c0 + w], shifted[:, m % 2, c0:c0 + w]
            if u >= 2:
                dve.wait_ge(s_dve, u - 1)
            dve.tensor_tensor(diff[:, u % 2, 0:w], before, now, ALU.subtract).then_inc(s_diff, 1)
            dve.wait_ge(s_diff, 2 * m + n + 1)
            return dve.scalar_tensor_tensor(PB[:, m, c0:c0 + w], diff[:, u % 2, 0:w], mu[:, m:m + 1], now, ALU.mult, ALU.add)
        project_features(b, "w_in_b_", [(ins["w_in_b_2"][m], SLICES_SEQ, None) for m in range(NB)], [(mu[:, :], ins["mu_b_2"])], evac_act, evac_dve, raws=2,
                         guests=(KeepGuest(b, ctx, out_a),))


def recurrent_gates(b, PB, kk, ab, bv, lw):
    nc, ins = b.nc, b.ins
    r, k, v, gate = (PB[:, 4 * i:4 * i + 4] for i in range(4))
    with b.stage() as ctx:
        th = b.sb(ctx, "th", [HD + 1, SEQ])
        wup = b.sb(ctx, "wup", [HD + 1, DA])
        aup = b.sb(ctx, "aup", [P, DA])
        cols = b.sb(ctx, "gate_cols", [P, 5, 4])
        blk = b.sb(ctx, "blk", [P, P])
        eps = b.sb(ctx, "kk_eps", [P, 1])
        sq = b.sb(ctx, "kk_sq", [P, 4, SEQ])
        pp = b.ps(ctx, "gates_ps", [P, 4, 512])
        n_ = {n: b.sem(ctx, "gates_" + n) for n in ("in", "const", "th", "z", "kk", "sq", "sd", "rk", "mm", "act", "dve", "chain", "gate", "rn")}
        ind = b.sb(ctx, "kk_ind", [P, 4, 8])
        back = b.sb(ctx, "kk_back", [8, 4, P])
        nrm = b.sb(ctx, "kk_norm", [8, 2, SEQ])
        SL = 2
        units = [("norm", i) for i in range(2)] + [(n, i) for n in ("decay", "back", "rate", "bonus") for i in range(8)]
        on_dve = [n in ("back", "bonus") for n, _ in units]
        first = {n: units.index((n, 0)) for n in ("norm", "decay", "back", "rate", "bonus")}

        def emptied(eng, u):
            eng.wait_ge(n_["dve" if on_dve[u] else "act"], sum(1 for v in on_dve[:u + 1] if v == on_dve[u]))

        def sl(u):
            return u // SL, slice(512 * (u % SL), 512 * (u % SL + 1))
        with nc.Block() as block:
            @block.sync
            def _(sp):
                for i, n in enumerate(("a0_2", "k_k_2", "k_a_2", "r_k_2")):
                    sp.dma_start(cols[:, i], ins[n]).then_inc(n_["in"], 16)
                sp.dma_start(wup[0:HD, :], ins["w_up_2"]).then_inc(n_["in"], 16)
                sp.dma_start(wup[HD:HD + 1, :], ins["w0_2"].rearrange("(a n) -> a n", a=1)).then_inc(n_["in"], 16)
                sp.dma_start(aup[HD:P, :], ins["a_up_2"]).then_inc(n_["in"], 16)
                sp.dma_start(blk[:, :], ins["cst"][:, C_BLK:C_BLK + P]).then_inc(n_["in"], 16)
                sp.dma_start(ind[:, :, :], ins["cst"][:, C_IND:C_BACK].rearrange("p (f h) -> p f h", h=8)).then_inc(n_["in"], 16)
                sp.dma_start(back[:, :, :], ins["cst"][0:8, C_BACK:C_END].rearrange("h (f p) -> h f p", p=P)).then_inc(n_["in"], 16)

            @block.gpsimd
            def _(pool):
                pool.memset(th[HD:HD + 1, :], 1.0).then_inc(n_["const"], 1)
                pool.wait_ge(n_["const"], 1)
                pool.memset(eps[:, :], 1e-12).then_inc(n_["const"], 1)

            @block.scalar
            def _(act):
                act.wait_ge(n_["in"], 160)
                act.wait_ge(n_["const"], 2)
                for c in range(4):
                    act.wait_ge(n_["kk"], c + 1)
                    act.activation(sq[:, c], kk[:, c], ACT.Square).then_inc(n_["sq"], 1)
                for i in range(2):
                    act.wait_ge(n_["mm"], first["norm"] + i + 1)
                    act.activation(nrm[:, 0, 512 * i:512 * (i + 1)], pp[0:8, i % 4], ACT.Sqrt, bias=eps[0:8, :]).then_inc(n_["act"], 1)
                act.activation(th[0:HD, :], PB[0:HD, 16], ACT.Tanh).then_inc(n_["th"], 1)
                for t in range(NT):
                    u = first["decay"] + t
                    act.wait_ge(n_["mm"], u + 1)
                    act.activation(lw[:, t], pp[:, u % 4], ACT.Sigmoid).then_inc(n_["act"], 1)
                for i in range(8):
                    c, s = sl(i)
                    u = first["rate"] + i
                    act.wait_ge(n_["mm"], u + 1)
                    act.activation(ab[:, c, s], pp[:, u % 4], ACT.Sigmoid, bias=cols[:, 0, c:c + 1]).then_inc(n_["act"], 1)
                act.activation(gate, gate, ACT.Silu).then_inc(n_["gate"], 1)

            @block.vector
            def _(dve):
                link = linker(dve, n_["chain"])
                dve.wait_ge(n_["in"], 160)
                for c in range(4):
                    dve.tensor_scalar(kk[:, c], k[:, c], cols[:, 1, c:c + 1], None, ALU.mult).then_inc(n_["kk"], 1)
                link(dve.tensor_scalar(cols[:, 4], cols[:, 2], -1.0, 1.0, ALU.mult, ALU.add))
                for i in range(2):
                    dve.wait_ge(n_["act"], i + 1)
                    dve.reciprocal(nrm[:, 1, 512 * i:512 * (i + 1)], nrm[:, 0, 512 * i:512 * (i + 1)]).then_inc(n_["rn"], 1)
                for i in range(8):
                    c, s = sl(i)
                    u = first["back"] + i
                    dve.wait_ge(n_["mm"], u + 1)
                    dve.tensor_tensor(kk[:, c, s], kk[:, c, s], pp[:, u % 4], ALU.mult).then_inc(n_["dve"], 1)
                dve.wait_ge(n_["dve"], 8)
                for c in range(5):
                    if c < 4:
                        dve.wait_ge(n_["act"], 10 + 2 * (c + 1))
                        link(dve.tensor_scalar(sq[:, c], ab[:, c], cols[:, 2, c:c + 1], cols[:, 4, c:c + 1], ALU.mult, ALU.add))
                        link(dve.tensor_tensor(k[:, c], k[:, c], sq[:, c], ALU.mult))
                        dve.scalar_tensor_tensor(sq[:, c], r[:, c], cols[:, 3, c:c + 1], k[:, c], ALU.mult, ALU.mult).then_inc(n_["rk"], 1)
                        link(dve.scalar_tensor_tensor(ab[:, c], ab[:, c], -1.0, kk[:, c], ALU.mult, ALU.mult))
                    if c >= 1:
                        for i in range(2 * (c - 1), 2 * c):
                            f, s = sl(i)
                            u = first["bonus"] + i
                            dve.wait_ge(n_["mm"], u + 1)
                            dve.tensor_tensor(bv[:, f, s], pp[:, u % 4], v[:, f, s], ALU.mult).then_inc(n_["dve"], 1)

            @block.tensor
            def _(pe):
                pe.wait_ge(n_["in"], 160)
                for u, (what, i) in enumerate(units):
                    if u >= 4:
                        emptied(pe, u - 4)
                    c, s = sl(i)
                    o = pp[:, u % 4]
                    if what == "norm":
                        for f in range(4):
                            pe.wait_ge(n_["sq"], f + 1)
                            mm = pe.matmul(pp[0:8, u % 4], ind[:, f], sq[:, f, 512 * i:512 * (i + 1)], start=(f == 0), stop=(f == 3))
                    elif what == "decay":
                        pe.wait_ge(n_["th"], 1)
                        mm = pe.matmul(o, th[:, P * i:P * (i + 1)], wup[:, :], start=True, stop=True)
                    elif what == "back":
                        pe.wait_ge(n_["rn"], i % SL + 1)
                        mm = pe.matmul(o, back[:, c], nrm[:, 1, s], start=True, stop=True)
                    elif what == "rate":
                        mm = pe.matmul(o, aup[HD:P, P * c:P * (c + 1)], PB[HD:P, 16, s], start=True, stop=True)
                    else:
                        pe.wait_ge(n_["rk"], c + 1)
                        mm = pe.matmul(o, blk[:, :], sq[:, c, s], start=True, stop=True)
                    mm.then_inc(n_["mm"], 1)


class Marks:

    def __init__(self, sem, names):
        self.sem, self.names, self.n = sem, names, 0

    def mark(self, ins, name):
        assert self.names[self.n % len(self.names)] == name, (self.names[self.n % len(self.names)], name)
        self.n += 1
        ins.then_inc(self.sem, 1)

    def wait(self, eng, t, name):
        if t >= 0:
            eng.wait_ge(self.sem, t * len(self.names) + self.names.index(name) + 1)


def recurrence_stage(b, PB, kk, ab, lw):
    nc, ins = b.nc, b.ins
    LV = 6
    r, k, v = (PB[:, 4 * i:4 * i + 4] for i in range(3))
    with b.stage() as ctx:
        tri = b.sb(ctx, "tri", [P, 2 * P])
        tris = b.sb(ctx, "tris", [P, 2 * P])
        lvl = b.sb(ctx, "lvl", [P, LV, P])
        ein = b.sb(ctx, "ein", [P, 2, 4, P])
        mid = b.sb(ctx, "mid", [P, 2, 4, P])
        ex = PB[:, 16].rearrange("p (a c t) -> p a c t", a=2, c=4)
        ta = b.sb(ctx, "ta", [P, DA])
        tb = b.sb(ctx, "tb", [P, 2, DA]); tk = b.sb(ctx, "tk_tok", [P, 2, DA]); tv = b.sb(ctx, "tv", [P, 2, DA])
        LT = b.sb(ctx, "LT", [P, 2, 4, P]); AK = b.sb(ctx, "AK", [P, 2, 4, P])
        RB = b.sb(ctx, "RB", [P, 2, 4, P]); RK = b.sb(ctx, "RK", [P, 2, 4, P])
        Xi = b.sb(ctx, "Xi", [P, 2, 4, P]); XT = b.sb(ctx, "XT", [P, 2, 4, P])
        Uo = b.sb(ctx, "Uo", [P, 2, 4, P])
        MV = b.sb(ctx, "MV", [P, DA])
        WT = b.sb(ctx, "WT", [P, 2, 4, P]); UU = b.sb(ctx, "UU", [P, 2, DA])
        SA = b.sb(ctx, "SA", [P, DA])
        S = b.sb(ctx, "S", [P, 4, P])
        Sx = b.sb(ctx, "Sx", [P, 4, HD])
        inv = b.ps(ctx, "inv_ps", [P, 4, 512])
        wk = b.ps(ctx, "work_ps", [P, 2, 512])
        ch = b.ps(ctx, "chain_ps", [P, 512])
        yp = b.ps(ctx, "y_ps", [P, 512])
        s_in, s_c = b.sem(ctx, "rec_in"), b.sem(ctx, "rec_const")
        levels = range(1, LV)
        last = LV - 1

        def of_level(l):
            return ["xt"] if l == last else ["x", "xt"]

        def marks(name, names):
            return Marks(b.sem(ctx, "rec_" + name), names)

        pg, ag, dg = marks("pe_decay", ["cum"]), marks("act_decay", ["eex", "eneg", "ein"]), marks("dve_decay", ["at", "bt", "kt", "rt"])
        pf = marks("pe", ["ab0", "ab1", "ta", "tb", "tk", "tv", "ak0", "ak1", "tx0", "tx1"]
                   + [n for l in levels for n in [f"p{l}0", f"p{l}1"] + [f"{x}{l}{e}" for e in range(2) for x in of_level(l)]]
                   + ["mv", "wt", "uu"])
        af = marks("act", ["ta", "tb", "tk", "tv", "tx0", "tx1"]
                   + [f"p{l}{e}" for l in levels for e in range(2)] + ["mv", "wt"])
        df = marks("dve", ["ab0", "ab1", "ak0", "ak1"]
                   + [f"{x}{l}{e}" for l in levels for e in range(2) for x in of_level(l)] + ["uu"])
        of = marks("pool", ["m0", "i0", "m1", "i1"] + [f"u{l}{e}" for l in levels for e in range(2)])
        pc = marks("pe_chain", ["sa0", "rb0", "rb1", "st0", "rk0", "rk1", "sa1", "st1", "y"])
        ac = marks("act_chain", ["y"])
        dc = marks("dve_chain", ["sa0", "rb0", "rb1", "sx00", "sx01", "s00", "s01", "rk0", "rk1", "sa1", "sx10", "sx11", "s10", "s11"])

        def tok(t):
            return slice(P * t, P * (t + 1))

        def head(c, e):
            return slice(P * c + HD * e, P * c + HD * (e + 1))

        def rows(i):
            return slice(HD * i, HD * (i + 1))

        def four(m):
            return m.rearrange("p (o t) -> p o t", o=1).broadcast_to([P, 4, P])

        def by_four(bank):
            return bank.rearrange("p (c t) -> p c t", c=4)

        with nc.Block() as block:
            @block.sync
            def _(sp):
                sp.dma_start(tri[:, :], ins["cst"][:, C_TRIU:C_TRIU + 2 * P]).then_inc(s_in, 16)
                sp.dma_start(lvl[:, :, :], ins["cst"][:, C_LVL:C_LVL + LV * P].rearrange("p (l t) -> p l t", l=LV)).then_inc(s_in, 16)

            @block.gpsimd
            def _(pool):
                pool.memset(S[:, :, :], 0.0).then_inc(s_c, 1)
                pool.wait_ge(s_in, 32)
                pool.tensor_scalar(tris[:, :], tri[:, :], -0.6065306597126334, None, ALU.mult).then_inc(s_c, 1)
                for t in range(NT):
                    for e in range(2):
                        df.wait(pool, t, f"ab{e}")
                        pf.wait(pool, t - 1, "uu")
                        of.mark(pool.tensor_tensor(XT[:, e], LT[:, e], four(lvl[:, 0]), ALU.mult), f"m{e}")
                        of.wait(pool, t, f"m{e}")
                        of.mark(pool.tensor_tensor(XT[:, e], XT[:, e], four(b.ident[:, :]), ALU.add), f"i{e}")
                    for l in levels:
                        for e in range(2):
                            if l > 1:
                                pf.wait(pool, t, f"p{l - 1}{e}")
                            else:
                                pf.wait(pool, t - 1, f"p{last}{e}")
                            of.mark(pool.tensor_tensor(Uo[:, e], LT[:, e], four(lvl[:, l]), ALU.mult), f"u{l}{e}")

            @block.scalar
            def _(act):
                def chain(t, seg):
                    if seg == 5:
                        pc.wait(act, t, "y")
                        ac.mark(act.activation(r[:, :, tok(t)], by_four(yp[:, :]), ACT.Copy), "y")

                def decays(t):
                    cum = wk[:, :, :].rearrange("p a (c x) -> p (a c) x", c=2)
                    pg.wait(act, t, "cum")
                    dg.wait(act, t - 1, "rt")
                    ag.mark(act.activation(ex[:, 0], cum[:, :, P:2 * P], ACT.Exp), "eex")
                    ag.mark(act.activation(ex[:, 1], cum[:, :, 0:P], ACT.Exp, scale=-1.0), "eneg")
                    dc.wait(act, t - 2, "s11")
                    ag.mark(act.activation(ein[:, t % 2], cum[:, :, 0:P], ACT.Exp), "ein")

                decays(0)
                for t in range(NT):
                    for n, dst, bank in (("ta", ta[:, :], 1), ("tb", tb[:, t % 2], 0), ("tk", tk[:, t % 2], 1), ("tv", tv[:, t % 2], 0)):
                        pf.wait(act, t, n)
                        if n == "ta":
                            pf.wait(act, t - 1, "wt")
                        else:
                            pc.wait(act, t - 2, "y")
                        af.mark(act.activation(dst, wk[:, bank], ACT.Copy), n)
                    for e in range(2):
                        pf.wait(act, t, f"tx{e}")
                        af.mark(act.activation(Xi[:, e], by_four(inv[:, e]), ACT.Copy), f"tx{e}")
                    for l in levels:
                        for e in range(2):
                            pf.wait(act, t, f"p{l}{e}")
                            if l == 1:
                                pf.wait(act, t - 1, f"xt{last}1")
                            else:
                                pf.wait(act, t, f"xt{l - 1}{e}")
                            af.mark(act.activation(mid[:, e], by_four(inv[:, e]), ACT.Copy), f"p{l}{e}")
                        if l == last and t + 1 < NT:
                            decays(t + 1)
                        if t:
                            chain(t - 1, l)
                    pf.wait(act, t, "mv")
                    af.mark(act.activation(MV[:, :], wk[:, 0], ACT.Copy), "mv")
                    pf.wait(act, t, "wt")
                    pc.wait(act, t - 2, "sa1")
                    af.mark(act.activation(WT[:, t % 2], by_four(wk[:, 1]), ACT.Copy), "wt")
                for l in levels:
                    chain(NT - 1, l)

            @block.vector
            def _(dve):
                def chain(t, seg):
                    if seg in (1, 3):
                        q = seg // 2
                        pc.wait(dve, t, f"sa{q}")
                        df.wait(dve, t, "uu")
                        pc.wait(dve, t - 1, "y")
                        dc.mark(dve.tensor_tensor(SA[rows(q)], ch[rows(q)], UU[rows(q), t % 2], ALU.add), f"sa{q}")
                    if seg == 1:
                        for e in range(2):
                            pc.wait(dve, t, f"rb{e}")
                            dc.mark(dve.tensor_tensor(RB[:, e], by_four(wk[:, e]), four(tri[:, 0:P]), ALU.mult), f"rb{e}")
                    if seg in (2, 4):
                        q = seg // 2 - 1
                        pc.wait(dve, t, f"st{q}")
                        for e in range(2):
                            dc.mark(dve.tensor_tensor(Sx[rows(e)], S[rows(e), :, rows(e)], by_four(ch[:, :])[rows(e), :, rows(e)], ALU.add), f"sx{q}{e}")
                        for e in range(2):
                            dc.wait(dve, t, f"sx{q}{e}")
                            d = ein[rows(e), t % 2, :, HD * q + HD - 1:HD * q + HD].broadcast_to([HD, 4, HD])
                            dc.mark(dve.tensor_tensor(S[rows(e), :, rows(e)], Sx[rows(e)], d, ALU.mult), f"s{q}{e}")
                    if seg == 2:
                        for e in range(2):
                            pc.wait(dve, t, f"rk{e}")
                            dc.mark(dve.tensor_tensor(RK[:, e], by_four(wk[:, e]), four(tri[:, 0:P]), ALU.mult), f"rk{e}")

                dve.wait_ge(s_c, 2)

                def decayed(t):
                    ag.wait(dve, t, "eneg")
                    dg.mark(dve.tensor_tensor(kk[:, :, tok(t)], kk[:, :, tok(t)], ex[:, 0], ALU.mult), "at")
                    dg.mark(dve.tensor_tensor(ab[:, :, tok(t)], ab[:, :, tok(t)], ex[:, 1], ALU.mult), "bt")
                    dg.mark(dve.tensor_tensor(k[:, :, tok(t)], k[:, :, tok(t)], ex[:, 1], ALU.mult), "kt")
                    ag.wait(dve, t, "ein")
                    dg.mark(dve.tensor_tensor(r[:, :, tok(t)], r[:, :, tok(t)], ein[:, t % 2], ALU.mult), "rt")

                decayed(0)
                for t in range(NT):
                    for x, dst, bank in (("ab", LT, 0), ("ak", AK, 2)):
                        for e in range(2):
                            pf.wait(dve, t, f"{x}{e}")
                            if x == "ab":
                                of.wait(dve, t - 1, f"u{last}{e}")
                            df.mark(dve.tensor_tensor(dst[:, e], by_four(inv[:, bank + e]), four(tri[:, P:2 * P]), ALU.mult), f"{x}{e}")
                    for l in levels:
                        for e in range(2):
                            for x in of_level(l):
                                pf.wait(dve, t, f"{x}{l}{e}")
                                bank = (3, 2)[e] if l == last else (2 if x == "x" else 3)
                                m = Xi if x == "x" else XT
                                df.mark(dve.tensor_tensor(m[:, e], m[:, e], by_four(inv[:, bank]), ALU.add), f"{x}{l}{e}")
                        if t:
                            chain(t - 1, l)
                    if t + 1 < NT:
                        decayed(t + 1)
                    pf.wait(dve, t, "uu")
                    df.mark(dve.tensor_copy(UU[:, t % 2], wk[:, 0]), "uu")
                for l in levels:
                    chain(NT - 1, l)

            @block.tensor
            def _(pe):
                def gram(bank, left, right, t, e):
                    for c in range(4):
                        mm = pe.matmul(bank[:, P * c:P * (c + 1)], left[rows(e), c, tok(t)], right[rows(e), c, tok(t)], start=True, stop=True)
                    return mm

                def chain(t, seg):
                    if seg in (1, 3):
                        q = seg // 2
                        af.wait(pe, t, "wt")
                        if q:
                            dc.wait(pe, t, "s01")
                        else:
                            dc.wait(pe, t - 1, "s11")
                            pe.wait_ge(s_c, 2)
                        for c in range(4):
                            mm = pe.matmul(ch[rows(q), P * c:P * (c + 1)], WT[:, t % 2, c, rows(q)], S[:, c], start=True, stop=True)
                        pc.mark(mm, f"sa{q}")
                    if seg in (2, 4):
                        q = seg // 2 - 1
                        if q == 0:
                            ac.wait(pe, t - 1, "y")
                        for c in range(4):
                            pe.matmul(yp[:, P * c + HD * q:P * c + HD * (q + 1)], S[:, c], r[:, c, P * t + HD * q:P * t + HD * (q + 1)],
                                      start=(q == 0 and c == 0), stop=False, skip_group_check=True)
                        dc.wait(pe, t, f"sa{q}")
                        for c in range(4):
                            o = ch[:, P * c:P * (c + 1)]
                            pe.matmul(o, tk[rows(q), t % 2, P * c:P * (c + 1)], tv[rows(q), t % 2, P * c:P * (c + 1)], start=True, stop=False)
                            mm = pe.matmul(o, tb[rows(q), t % 2, P * c:P * (c + 1)], SA[rows(q), P * c:P * (c + 1)], start=False, stop=True)
                        pc.mark(mm, f"st{q}")
                    if seg == 1:
                        for e in range(2):
                            dg.wait(pe, t, "rt")
                            if t + 1 < NT:
                                af.wait(pe, t + 1, ("tv", "tk")[e])
                            else:
                                af.wait(pe, t, "wt")
                                df.wait(pe, t, "uu")
                            pc.mark(gram(wk[:, e], ab, r, t, e), f"rb{e}")
                    if seg == 2:
                        for e in range(2):
                            dc.wait(pe, t, f"rb{e}")
                            pc.mark(gram(wk[:, e], k, r, t, e), f"rk{e}")
                    if seg == 5:
                        dc.wait(pe, t, "sa1")
                        dc.wait(pe, t, "rk1")
                        for c in range(4):
                            for e in range(2):
                                o = yp[rows(e), P * c:P * (c + 1)]
                                pe.matmul(o, SA[:, head(c, e)], RB[:, e, c], start=False, stop=False, skip_group_check=True)
                                mm = pe.matmul(o, tv[:, t % 2, head(c, e)], RK[:, e, c], start=False, stop=True, skip_group_check=True)
                        pc.mark(mm, "y")

                def four_of(name, e, bank, left, right):
                    for c in range(4):
                        mm = pe.matmul(inv[:, bank, P * c:P * (c + 1)], left[:, e, c], right[:, e, c], start=True, stop=True)
                    pf.mark(mm, name)

                pe.wait_ge(s_c, 2)

                def decays(t):
                    if t:
                        af.wait(pe, t - 1, "tv")
                        dc.wait(pe, t - 2, "rk1")
                    for c in range(4):
                        mm = pe.matmul(wk[:, c // 2, 2 * P * (c % 2):2 * P * (c % 2 + 1)], lw[:, t, P * c:P * (c + 1)], tris[:, :], start=True, stop=True)
                    pg.mark(mm, "cum")

                decays(0)
                for t in range(NT):
                    dg.wait(pe, t, "bt")
                    for e in range(2):
                        af.wait(pe, t - 1, f"p{last}{e}")
                        pf.mark(gram(inv[:, e], ab, kk, t, e), f"ab{e}")
                    ag.wait(pe, t, "ein")
                    for n, src, bank, ready, free in (("ta", kk, 1, "at", None), ("tb", ab, 0, "bt", None), ("tk", k, 1, "kt", "ta"), ("tv", v, 0, None, "tb")):
                        if ready:
                            dg.wait(pe, t, ready)
                        if free:
                            af.wait(pe, t, free)
                        elif n == "ta":
                            af.wait(pe, t - 1, "wt")
                        else:
                            df.wait(pe, t - 1, "uu")
                        for c in range(4):
                            mm = pe.transpose(wk[:, bank, P * c:P * (c + 1)], src[:, c, tok(t)], b.ident[:, :])
                        pf.mark(mm, n)
                    for e in range(2):
                        df.wait(pe, t - 1, f"xt{last}{1 - e}")
                        pf.mark(gram(inv[:, 2 + e], k, kk, t, e), f"ak{e}")
                    for e in range(2):
                        of.wait(pe, t, f"i{e}")
                        for c in range(4):
                            mm = pe.transpose(inv[:, e, P * c:P * (c + 1)], XT[:, e, c], b.ident[:, :])
                        pf.mark(mm, f"tx{e}")
                    for l in levels:
                        if l == last and t + 1 < NT:
                            decays(t + 1)
                        for e in range(2):
                            of.wait(pe, t, f"u{l}{e}")
                            if l == 1:
                                af.wait(pe, t, f"tx{e}")
                            else:
                                df.wait(pe, t, f"x{l - 1}{e}")
                                af.wait(pe, t, f"p{l - 1}{e}")
                            four_of(f"p{l}{e}", e, e, Uo, Xi)
                        for e in range(2):
                            af.wait(pe, t, f"p{l}{e}")
                            for x in of_level(l):
                                bank = (3, 2)[e] if l == last else (2 if x == "x" else 3)
                                if l == last:
                                    df.wait(pe, t, f"xt{l - 1}1" if e == 0 else f"x{l - 1}1")
                                elif e == 1:
                                    df.wait(pe, t, f"{x}{l}0")
                                elif l > 1:
                                    df.wait(pe, t, f"{x}{l - 1}1")
                                else:
                                    df.wait(pe, t, "ak0" if x == "x" else "ak1")
                                if l > 1:
                                    df.wait(pe, t, f"xt{l - 1}{e}")
                                if x == "x":
                                    four_of(f"x{l}{e}", e, bank, XT, mid)
                                else:
                                    four_of(f"xt{l}{e}", e, bank, mid, XT)
                        if t:
                            chain(t - 1, l)
                    df.wait(pe, t, "ak1")
                    dc.wait(pe, t - 1, "rk0")
                    if t + 1 < NT:
                        ag.wait(pe, t + 1, "ein")
                    else:
                        af.wait(pe, t, "tv")
                    for h in range(8):
                        mm = pe.matmul(wk[:, 0, HD * h:HD * (h + 1)], AK[:, h % 2, h // 2], tv[:, t % 2, HD * h:HD * (h + 1)], start=True, stop=True)
                    pf.mark(mm, "mv")
                    dc.wait(pe, t - 1, "rk1")
                    df.wait(pe, t, f"xt{last}1")
                    for c in range(4):
                        for e in range(2):
                            mm = pe.matmul(wk[rows(e), 1, P * c:P * (c + 1)], ta[:, head(c, e)], XT[:, e, c], start=True, stop=True)
                    pf.mark(mm, "wt")
                    af.wait(pe, t, "mv")
                    for h in range(8):
                        mm = pe.matmul(wk[:, 0, HD * h:HD * (h + 1)], XT[:, h % 2, h // 2], MV[:, HD * h:HD * (h + 1)], start=True, stop=True)
                    pf.mark(mm, "uu")
                for l in levels:
                    chain(NT - 1, l)


def recurrent_output(b, PB, bv):
    nc, ins = b.nc, b.ins
    y, gate = PB[:, 0:4], PB[:, 12:16]
    with b.stage() as ctx:
        blk = b.sb(ctx, "blk2", [P, P])
        ind = b.sb(ctx, "gn_ind", [P, 4, 8])
        back = b.sb(ctx, "gn_back", [8, 4, P])
        eps = b.sb(ctx, "gn_eps", [P, 1])
        cols = b.sb(ctx, "gn_cols", [P, 2, 4])
        sq = b.sb(ctx, "gn_sq", [P, 8, 512])
        sd = b.sb(ctx, "gn_sd", [8, 2, 2, 512])
        pp = b.ps(ctx, "gn_ps", [P, 4, 512])
        s = {n: b.sem(ctx, "gn_" + n) for n in ("in", "eps", "mm", "dve", "act", "sq", "rs", "aff", "sum", "out")}
        units = [("mean", i) for i in range(8)] + [("var", i) for i in range(2)] + [("back", i) for i in range(8)]

        def emptied(eng, u):
            if units[u][0] == "var":
                eng.wait_ge(s["act"], units[u][1] + 1)
            else:
                eng.wait_ge(s["dve"], units[u][1] + (9 if units[u][0] == "back" else 1))

        def sl(i):
            return i % 4, slice(512 * (i // 4), 512 * (i // 4 + 1))
        with nc.Block() as block:
            @block.sync
            def _(sp):
                sp.dma_start(blk[:, :], ins["cst"][:, C_BLK:C_BLK + P]).then_inc(s["in"], 16)
                sp.dma_start(ind[:, :, :], ins["cst"][:, C_IND:C_BACK].rearrange("p (f h) -> p f h", h=8)).then_inc(s["in"], 16)
                sp.dma_start(back[:, :, :], ins["cst"][0:8, C_BACK:C_END].rearrange("h (f p) -> h f p", p=P)).then_inc(s["in"], 16)
                sp.dma_start(cols[:, 0], ins["gn_g_2"]).then_inc(s["in"], 16)
                sp.dma_start(cols[:, 1], ins["gn_b_2"]).then_inc(s["in"], 16)

            @block.gpsimd
            def _(pool):
                pool.memset(eps[:, :], 64e-5).then_inc(s["eps"], 1)
                for i in range(8):
                    c, t = sl(i)
                    pool.wait_ge(s["aff"], i + 1)
                    pool.tensor_tensor(y[:, c, t], y[:, c, t], bv[:, c, t], ALU.add).then_inc(s["sum"], 1)

            @block.tensor
            def _(pe):
                pe.wait_ge(s["in"], 80)
                for u, (what, i) in enumerate(units):
                    if u >= 4:
                        emptied(pe, u - 4)
                    if what == "mean":
                        c, t = sl(i)
                        mm = pe.matmul(pp[:, u % 4], blk[:, :], y[:, c, t], start=True, stop=True)
                    elif what == "var":
                        for c in range(4):
                            pe.wait_ge(s["sq"], 4 * i + c + 1)
                            mm = pe.matmul(pp[0:8, u % 4], ind[:, c], sq[:, 4 * i + c], start=(c == 0), stop=(c == 3))
                    else:
                        pe.wait_ge(s["rs"], i // 4 + 1)
                        mm = pe.matmul(pp[:, u % 4], back[:, i % 4], sd[:, i // 4, 1], start=True, stop=True)
                    mm.then_inc(s["mm"], 1)

            @block.scalar
            def _(act):
                act.wait_ge(s["eps"], 1)
                act.wait_ge(s["in"], 80)
                for i in range(8):
                    c, t = sl(i)
                    act.wait_ge(s["dve"], i + 1)
                    act.activation(sq[:, i], y[:, c, t], ACT.Square).then_inc(s["sq"], 1)
                for i in range(2):
                    act.wait_ge(s["mm"], 8 + i + 1)
                    act.activation(sd[:, i, 0], pp[0:8, i % 4], ACT.Sqrt, bias=eps[0:8, :], scale=1.0 / HD).then_inc(s["act"], 1)
                for i in range(8):
                    c, t = sl(i)
                    act.wait_ge(s["dve"], 8 + i + 1)
                    act.activation(y[:, c, t], y[:, c, t], ACT.Identity, bias=cols[:, 1, c:c + 1], scale=cols[:, 0, c:c + 1]).then_inc(s["aff"], 1)

            @block.vector
            def _(dve):
                for i in range(8):
                    c, t = sl(i)
                    dve.wait_ge(s["mm"], i + 1)
                    dve.scalar_tensor_tensor(y[:, c, t], pp[:, i % 4], -1.0 / HD, y[:, c, t], ALU.mult, ALU.add).then_inc(s["dve"], 1)
                for i in range(8 + 4):
                    if i < 8:
                        c, t = sl(i)
                        u = 10 + i
                        if i % 4 == 0:
                            h = i // 4
                            dve.wait_ge(s["act"], h + 1)
                            dve.reciprocal(sd[:, h, 1], sd[:, h, 0]).then_inc(s["rs"], 1)
                        dve.wait_ge(s["mm"], u + 1)
                        dve.wait_ge(s["dve"], i + 1)
                        dve.wait_ge(s["sq"], i + 1)
                        dve.tensor_tensor(y[:, c, t], y[:, c, t], pp[:, u % 4], ALU.mult).then_inc(s["dve"], 1)
                    if i >= 4:
                        c, t = sl(i - 4)
                        dve.wait_ge(s["sum"], i - 3)
                        dve.tensor_tensor(gate[:, c, t], gate[:, c, t], y[:, c, t], ALU.mult).then_inc(s["out"], 1)


def join_stage(b, PB, out_a):
    nc = b.nc
    gate = PB[:, 12:16]
    with b.stage() as ctx:
        a = b.sb(ctx, "out_a_in", [P, 2, DA])
        tp = b.ps(ctx, "join_tp", [P, 2, 4, P])
        s_a = [b.sem(ctx, f"join_a{i}") for i in range(2)]
        s_tp, s_h, s_l, s_gh, s_gl = (b.sem(ctx, "join_" + n) for n in ("tp", "h", "l", "gh", "gl"))
        with nc.Block() as block:
            @block.sync
            def _(sp):
                for t in range(NT):
                    if t >= 2:
                        sp.wait_ge(s_tp, t - 1)
                    sp.dma_start(a[:, t % 2], out_a[:, t]).then_inc(s_a[t % 2], 16)

            @block.tensor
            def _(pe):
                for t in range(NT):
                    pe.wait_ge(s_a[t % 2], 16 * (t // 2 + 1))
                    if t >= 2:
                        pe.wait_ge(s_l, t - 1)
                    for c in range(4):
                        mm = pe.transpose(tp[:, t % 2, c], a[:, t % 2, P * c:P * (c + 1)], b.ident[:, :])
                    mm.then_inc(s_tp, 1)

            @block.scalar
            def _(act):
                for t in range(NT):
                    if t % 2 == 0:
                        c = t // 2
                        act.activation(b.XH[:, 4 + c], gate[:, c], ACT.Copy).then_inc(s_gh, 1)
                    act.wait_ge(s_tp, t + 1)
                    act.activation(b.XH[:, 0:4, P * t:P * (t + 1)], tp[:, t % 2], ACT.Copy).then_inc(s_h, 1)

            @block.vector
            def _(dve):
                for t in range(NT):
                    if t % 2 == 0:
                        c = t // 2
                        dve.wait_ge(s_gh, c + 1)
                        dve.tensor_tensor(b.XL[:, 4 + c], gate[:, c], b.XH[:, 4 + c].bitcast(f32), ALU.subtract).then_inc(s_gl, 1)
                    dve.wait_ge(s_h, t + 1)
                    o = (slice(None), slice(0, 4), slice(P * t, P * (t + 1)))
                    dve.tensor_tensor(b.XL[o], tp[:, t % 2], b.XH[o].bitcast(f32), ALU.subtract).then_inc(s_l, 1)


class FinalTail:
    STEPS = 3
    ALPHA = 2 ** 0.25

    def __init__(self, b, ctx, x, out, ready):
        self.b, self.x, self.out, self.ready = b, x, out, ready
        self.rx = b.sb(ctx, "fin_x", [P, 2, D])
        self.z = b.sb(ctx, "fin_z", [P, 3, D])
        self.g = b.sb(ctx, "fin_g", [P, D])
        self.be = b.sb(ctx, "fin_b", [P, D])
        self.eps = b.sb(ctx, "fin_eps", [P, 1])
        self.st = b.sb(ctx, "fin_st", [P, NT, 2, 6])
        self.mv = b.sb(ctx, "fin_mv", [P, NT, 2])
        self.sd = b.sb(ctx, "fin_sd", [P, 3, NT])
        self.s = {n: b.sem(ctx, "fin_" + n) for n in ("x0", "x1", "gb", "eps", "z", "st", "mv", "sd", "rs", "shift", "c", "n", "o", "out")}

    def load_gains(self, sp):
        sp.dma_start(self.g[:, :], rows_of(self.b.ins["ln_g_2"])).then_inc(self.s["gb"], 16)
        sp.dma_start(self.be[:, :], rows_of(self.b.ins["ln_b_2"])).then_inc(self.s["gb"], 16)

    def sync(self, sp):
        s = self.s
        for t in range(NT + 3):
            if t < NT:
                if t >= 2:
                    sp.wait_ge(s["z"], t - 1)
                sp.dma_start(self.rx[:, t % 2], self.x[P * t:P * (t + 1), :]).then_inc(s[f"x{t % 2}"], 16)
            if t >= 3:
                u = t - 3
                sp.wait_ge(s["o"], u + 1)
                sp.dma_start(self.out[0, P * u:P * (u + 1), :], self.b.Y[:, u]).then_inc(s["out"], 16)
        sp.wait_ge(s["out"], 16 * NT)

    def gpsimd(self, pool):
        s, Y = self.s, self.b.Y
        pool.memset(self.eps[:, :], 1e-5).then_inc(s["eps"], 1)
        pool.wait_ge(s["gb"], 32)
        for t in range(NT):
            pool.wait_ge(s["n"], t + 1)
            pool.tensor_tensor(Y[:, t], Y[:, t], self.be[:, :], ALU.add).then_inc(s["o"], 1)

    def scalar(self, act, k):
        s = self.s
        if k == 0:
            act.wait_ge(s["eps"], 1)
        if k < NT:
            act.wait_ge(s["mv"], k + 1)
            act.activation(self.sd[:, 0, k:k + 1], self.mv[:, k, 1:2], ACT.Sqrt, bias=self.eps[:, :]).then_inc(s["sd"], 1)
        if 1 <= k < NT + 1:
            t = k - 1
            act.wait_ge(s["shift"], t + 1)
            act.activation(self.z[:, t % 3], self.z[:, t % 3], ACT.Identity, bias=self.sd[:, 2, t:t + 1], scale=self.sd[:, 1, t:t + 1]).then_inc(s["c"], 1)

    def vector(self, dve, k):
        s, z, sd = self.s, self.z, self.sd
        if k < NT:
            self.ready(dve, k)
            dve.wait_ge(s[f"x{k % 2}"], 16 * (k // 2 + 1))
            if k >= 3:
                dve.wait_ge(s["n"], k - 2)
            dve.scalar_tensor_tensor(z[:, k % 3], self.rx[:, k % 2], self.ALPHA, self.b.Y[:, k], ALU.mult, ALU.add).then_inc(s["z"], 1)
            dve.wait_ge(s["z"], k + 1)
            for h in range(2):
                dve.bn_stats(self.st[:, k, h], z[:, k % 3, 512 * h:512 * (h + 1)]).then_inc(s["st"], 1)
            dve.wait_ge(s["st"], 2 * k + 2)
            dve.bn_aggr(self.mv[:, k], self.st[:, k].rearrange("p a b -> p (a b)")).then_inc(s["mv"], 1)
        if 2 <= k < NT + 2:
            t = k - 2
            if t == 0:
                dve.wait_ge(s["gb"], 32)
            dve.wait_ge(s["c"], t + 1)
            dve.tensor_tensor(self.b.Y[:, t], z[:, t % 3], self.g[:, :], ALU.mult).then_inc(s["n"], 1)
        if k < NT:
            dve.wait_ge(s["sd"], k + 1)
            dve.reciprocal(sd[:, 1, k:k + 1], sd[:, 0, k:k + 1]).then_inc(s["rs"], 1)
            dve.wait_ge(s["rs"], k + 1)
            dve.scalar_tensor_tensor(sd[:, 2, k:k + 1], self.mv[:, k, 0:1], -1.0, sd[:, 1, k:k + 1], ALU.mult, ALU.mult).then_inc(s["shift"], 1)

    def tensor(self, pe, t):
        pass


def second_block(b, x3, x4, ada_rows):
    nc, ins = b.nc, b.ins
    shift, scale1, gate = (ada_rows[0, D * i:D * (i + 1)] for i in range(3))
    out_a = nc.dram_tensor("out_a", [P, NT, DA], f32, kind="Internal").ap()
    with ExitStack() as right:
        b.alloc_x(right, "b2", SEQ, "right")
        post_stage(b, "p3", TILES_SEQ, lambda t: x3[P * t:P * (t + 1), :], x4, ins["norm_ffn_post"][1], modulate=(scale1, shift))
        gmlp_stage(b)
        left = ExitStack()
        PB = b.sb(left, "PB", [P, NB, SEQ])
        recurrent_inputs(b, PB, out_a)
    with ExitStack() as ctx:
        kk = b.sb(ctx, "kk", [P, 4, SEQ])
        ab = b.sb(ctx, "ab", [P, 4, SEQ])
        bv = b.Y[:, 0:4]
        lw = b.Y[:, 4:8].rearrange("p a (t f) -> p (a t) f", f=DA)
        recurrent_gates(b, PB, kk, ab, bv, lw)
        recurrence_stage(b, PB, kk, ab, lw)
        recurrent_output(b, PB, bv)
    with ExitStack() as right:
        b.alloc_x(right, "b3", SEQ, "right")
        join_stage(b, PB, out_a)
        left.close()
        gate_rows = b.Y[:, NT]
        project_tokens(b, "w_out_", ins["w_out_2"], 2, [(gate_rows, rows_of(gate))],
                       lambda dve, c, t, bank: dve.tensor_tensor(b.Y[:, t, 512 * c:512 * (c + 1)], bank, gate_rows[:, 512 * c:512 * (c + 1)], ALU.mult),
                       make_tail=lambda ctx, ready: FinalTail(b, ctx, x4, b.out, ready))


def program(nc, ins, out):
    with ExitStack() as ctx:
        b = Builder(nc, ctx, ins, out)
        meta, x = ins["meta_tokens"], ins["x"]
        with ExitStack() as first:
            b.alloc_x(first, "b1", TOK, "right")
            pool_stage(b)
            post_stage(b, "p0", TILES_META, lambda t: meta if t == 0 else x[0, P * (t - 1):P * t, :], b.res[0], ins["norm_mix_post"][0], ins["norm_ffn_pre"][0])
            ffn_stage(b, "f0", 0, TILES_META, SLICES_META)
            ada_rows = nc.dram_tensor("ada_rows", [1, 3 * D], f32, kind="Internal").ap()
            layer1_mixer(b, b.res[0], b.res[1], b.res[2], ada_rows)
            ffn_stage(b, "f1", 1, TILES_SEQ, SLICES_SEQ)
        second_block(b, b.res[2], b.res[3], ada_rows)


def kernel(**inputs):
    import concourse.bacc as bacc
    from concourse.bass_utils import run_bass_kernel_spmd

    nc = bacc.Bacc("TRN2", target_bir_lowering=False, num_devices=1)
    arrays = {f"in_{n}": a for n, a in lay_out(inputs).items()}
    ins = {n[3:]: nc.dram_tensor(n, a.shape, mybir.dt.from_np(a.dtype), kind="ExternalInput").ap() for n, a in arrays.items()}
    out = nc.dram_tensor("out", (1, SEQ, D), f32, kind="ExternalOutput").ap()
    program(nc, ins, out)
    r = run_bass_kernel_spmd(nc, [arrays], core_ids=[0])
    return r.results[0]["out"]
```
